# Optimizing a Trainium2 kernel written in Bass

```python
import math
import jax, jax.numpy as jnp
from jax import lax
import numpy as np

D_MODEL = 1024
BATCH = 1
SEQ = 256
DEPTH = 2

HEAD_DIM = 64
A_WIDTH = D_MODEL // 2
A_HEADS = A_WIDTH // HEAD_DIM
DILATED_BRANCHES = ((128, 1), (512, 4), (2048, 16))
BLOCK = 128
B_WIDTH = D_MODEL // 2
B_GROUPS = 4
B_GROUP_CH = B_WIDTH // B_GROUPS
CHUNK = 128
C_WIDTH = D_MODEL // 2
CONV_WIDTH = 31
D_WIDTH = D_MODEL // 2
D_HEADS = D_WIDTH // HEAD_DIM
N_BUCKETS = 32
MAX_DISTANCE = 2048
N_GROUPS = 4
EXPERTS_PER_GROUP = 4
N_EXPERTS = N_GROUPS * EXPERTS_PER_GROUP
EXPERT_TOP_K = 2
D_EXPERT = D_MODEL // 2
EPS = 1e-6
NEG = -1e30
N_EVEN = (DEPTH + 1) // 2
N_ODD = DEPTH // 2


def rms_norm(x, g):
    xf = x.astype(jnp.float32)
    y = xf * lax.rsqrt(jnp.mean(xf * xf, -1, keepdims=True) + EPS)
    return (y * g.astype(jnp.float32)).astype(x.dtype)

def layer_norm(x, g, b):
    xf = x.astype(jnp.float32)
    mu = jnp.mean(xf, -1, keepdims=True)
    xc = xf - mu
    var = jnp.mean(xc * xc, -1, keepdims=True)
    y = xc * lax.rsqrt(var + EPS) * g.astype(jnp.float32) + b.astype(jnp.float32)
    return y.astype(x.dtype)

def t5_bucket(dist):
    max_exact = N_BUCKETS // 2
    d = np.maximum(dist, 1).astype(np.float32)
    large = max_exact + (np.log(d / max_exact) / np.log(MAX_DISTANCE / max_exact)
                         * (N_BUCKETS - max_exact)).astype(np.int32)
    large = np.minimum(large, N_BUCKETS - 1)
    return np.where(dist < max_exact, dist, large).astype(np.int32)

def dilated_branch(q, k, v, rel_table, window, dilation):
    b, h, s, hd = q.shape
    n_keys = window // dilation
    sub_len = -(-s // dilation)
    lp = -(-sub_len // BLOCK) * BLOCK
    sp = lp * dilation
    nb = lp // BLOCK
    pad = ((0, 0), (0, 0), (0, sp - s), (0, 0))

    def to_blocks(t):
        t = jnp.pad(t, pad).reshape(b, h, lp, dilation, hd)
        t = jnp.swapaxes(t, 2, 3)
        return t.reshape(b, h, dilation, nb, BLOCK, hd)

    def with_prev(t):
        prev = jnp.pad(t, ((0, 0), (0, 0), (0, 0), (1, 0), (0, 0), (0, 0)))[:, :, :, :-1]
        return jnp.concatenate([prev, t], axis=4)

    qb = to_blocks(q)
    kb = with_prev(to_blocks(k))
    vb = with_prev(to_blocks(v))
    scores = jnp.einsum('bhrnqd,bhrnkd->bhrnqk', qb, kb)

    qi = np.arange(BLOCK)[:, None]
    kj = np.arange(2 * BLOCK)[None, :]
    sub_dist = qi + BLOCK - kj
    in_window = (sub_dist >= 0) & (sub_dist <= n_keys)
    bucket = t5_bucket(np.clip(sub_dist, 0, None) * dilation)
    bias = jnp.transpose(rel_table.astype(jnp.float32)[bucket], (2, 0, 1))
    first_block = (np.arange(nb) == 0)[:, None, None]
    valid = in_window[None] & ~(first_block & (kj < BLOCK)[None])
    logits = jnp.where(valid, scores + bias[None, :, None, None], NEG)

    mx = jnp.max(logits, -1)
    p = jnp.exp(logits - mx[..., None])
    den = jnp.sum(p, -1)
    num = jnp.einsum('bhrnqk,bhrnkd->bhrnqd', p, vb)

    def from_blocks(t):
        rest = t.shape[5:]
        t = t.reshape(b, h, dilation, lp, *rest)
        t = jnp.swapaxes(t, 2, 3).reshape(b, h, sp, *rest)
        return t[:, :, :s]

    return from_blocks(num), from_blocks(den), from_blocks(mx)

def dilated_attention(q, k, v, rel_table):
    b, s, h, hd = q.shape
    qf = jnp.swapaxes(q.astype(jnp.float32), 1, 2) * (hd ** -0.5)
    kf = jnp.swapaxes(k.astype(jnp.float32), 1, 2)
    vf = jnp.swapaxes(v.astype(jnp.float32), 1, 2)
    outs = [dilated_branch(qf, kf, vf, rel_table, w, d) for (w, d) in DILATED_BRANCHES]
    m_all = jnp.max(jnp.stack([m for (_, _, m) in outs]), 0)
    num = sum(n * jnp.exp(m - m_all)[..., None] for (n, _, m) in outs)
    den = sum(l * jnp.exp(m - m_all) for (_, l, m) in outs)
    o = num / den[..., None]
    return jnp.swapaxes(o, 1, 2).reshape(b, s, h * hd)

def spatial_gating(u, v, ln_g, ln_b, w_s, b_s):
    b, s, _ = v.shape
    u = jax.nn.gelu(u)
    v = layer_norm(jax.nn.gelu(v), ln_g, ln_b)
    vc = v.reshape(b, s // CHUNK, CHUNK, B_GROUPS, B_GROUP_CH)
    tril = np.tril(np.ones((CHUNK, CHUNK), dtype=bool))
    w = jnp.where(tril[None], w_s, 0.0)
    mixed = jnp.einsum('gts,bnsgc->bntgc', w, vc) + jnp.swapaxes(b_s, 0, 1)[None, None, :, :, None]
    return u * mixed.reshape(b, s, B_WIDTH).astype(u.dtype)

def conv_module(a, gate, w_dw, b_dw, ln_g, ln_b):
    hcur = a * jax.nn.sigmoid(gate)
    hcur = lax.conv_general_dilated(
        hcur, w_dw[:, None, :].astype(hcur.dtype), window_strides=(1,),
        padding=[(CONV_WIDTH - 1, 0)], dimension_numbers=('NWC', 'WIO', 'NWC'),
        feature_group_count=C_WIDTH) + b_dw
    hcur = layer_norm(hcur, ln_g, ln_b)
    return jax.nn.silu(hcur)

def stick_breaking_attention(q, k, v):
    b, s, h, hd = q.shape
    qf = jnp.transpose(q.astype(jnp.float32), (0, 2, 1, 3)) * (hd ** -0.5)
    kf = jnp.transpose(k.astype(jnp.float32), (0, 2, 1, 3))
    vf = jnp.transpose(v.astype(jnp.float32), (0, 2, 1, 3))
    nb = s // BLOCK
    q_blocks = jnp.moveaxis(qf.reshape(b, h, nb, BLOCK, hd), 2, 0)
    key_pos = jnp.arange(s)

    def block(args):
        qb, i = args
        z = jnp.einsum('bhqd,bhkd->bhqk', qb, kf)
        t = i * BLOCK + jnp.arange(BLOCK)
        causal = key_pos[None, :] < t[:, None]
        log_keep = jnp.where(causal, jax.nn.log_sigmoid(-z), 0.0)
        between = lax.cumsum(log_keep, axis=3, reverse=True) - log_keep
        att = jnp.where(causal, jnp.exp(jax.nn.log_sigmoid(z) + between), 0.0)
        return jnp.einsum('bhqk,bhkd->bhqd', att, vf)

    out = lax.map(block, (q_blocks, jnp.arange(nb)))
    out = jnp.moveaxis(out, 0, 2).reshape(b, h, s, hd)
    return jnp.transpose(out, (0, 2, 1, 3)).reshape(b, s, h * hd)

def hierarchical_moe(hin, w_group, b_group, w_router, b_router, w_gate, w_up, w_down):
    b, s, d = hin.shape
    xt = hin.reshape(b * s, d)
    xf = xt.astype(jnp.float32)
    g_prob = jax.nn.softmax(xf @ w_group.astype(jnp.float32) + b_group.astype(jnp.float32), -1)
    g_w, g_idx = lax.top_k(g_prob, 1)
    e_logits = jnp.einsum('td,gde->tge', xf, w_router.astype(jnp.float32)) + b_router.astype(jnp.float32)
    e_logits = jnp.take_along_axis(e_logits, g_idx[:, :, None], axis=1)[:, 0]
    e_val, e_idx = lax.top_k(e_logits, EXPERT_TOP_K)
    e_w = jax.nn.softmax(e_val, -1)
    flat_idx = g_idx * EXPERTS_PER_GROUP + e_idx
    gates = jnp.sum(jax.nn.one_hot(flat_idx, N_EXPERTS, dtype=jnp.float32)
                    * (g_w * e_w)[..., None], axis=1)
    y = jnp.zeros((b * s, d), jnp.float32)
    for e in range(N_EXPERTS):
        hid = jax.nn.silu(xt @ w_gate[e]) * (xt @ w_up[e])
        y = y + gates[:, e:e + 1] * (hid @ w_down[e]).astype(jnp.float32)
    return y.astype(hin.dtype).reshape(b, s, d)

def first_inputs(seed: int = 0) -> dict:
    key = jax.random.key(seed)
    ks = iter(jax.random.split(key, 32))

    def nrm(shape, scale):
        return scale * jax.random.normal(next(ks), shape, jnp.float32)

    d = D_MODEL
    ev_in = 3 * A_WIDTH + 2 * B_WIDTH
    od_in = 2 * C_WIDTH + 3 * D_WIDTH
    return {
        "x": nrm((BATCH, SEQ, d), 1.0),
        "c": nrm((BATCH, d), 1.0),
        "rel_bias": nrm((N_BUCKETS, A_HEADS), 0.5),
        "norm1_g": 1.0 + nrm((DEPTH, d), 0.1),
        "norm2_g": 1.0 + nrm((DEPTH, d), 0.1),
        "w_ada": nrm((DEPTH, d, 6 * d), 0.5 * d ** -0.5),
        "b_ada": nrm((DEPTH, 6 * d), 0.02),
        "ev_w_in": nrm((N_EVEN, d, ev_in), d ** -0.5),
        "ev_w_out": nrm((N_EVEN, A_WIDTH + B_WIDTH, d), (A_WIDTH + B_WIDTH) ** -0.5),
        "ev_gmlp_ln_g": 1.0 + nrm((N_EVEN, B_WIDTH), 0.1),
        "ev_gmlp_ln_b": nrm((N_EVEN, B_WIDTH), 0.02),
        "ev_w_s": nrm((N_EVEN, B_GROUPS, CHUNK, CHUNK), CHUNK ** -0.5),
        "ev_b_s": 1.0 + nrm((N_EVEN, B_GROUPS, CHUNK), 0.1),
        "od_w_in": nrm((N_ODD, d, od_in), d ** -0.5),
        "od_w_out": nrm((N_ODD, C_WIDTH + D_WIDTH, d), (C_WIDTH + D_WIDTH) ** -0.5),
        "od_w_dw": nrm((N_ODD, CONV_WIDTH, C_WIDTH), CONV_WIDTH ** -0.5),
        "od_b_dw": nrm((N_ODD, C_WIDTH), 0.02),
        "od_conv_ln_g": 1.0 + nrm((N_ODD, C_WIDTH), 0.1),
        "od_conv_ln_b": nrm((N_ODD, C_WIDTH), 0.02),
        "moe_w_group": nrm((DEPTH, d, N_GROUPS), d ** -0.5),
        "moe_b_group": nrm((DEPTH, N_GROUPS), 0.01),
        "moe_w_router": nrm((DEPTH, N_GROUPS, d, EXPERTS_PER_GROUP), d ** -0.5),
        "moe_b_router": nrm((DEPTH, N_GROUPS, EXPERTS_PER_GROUP), 0.01),
        "moe_w_gate": nrm((DEPTH, N_EXPERTS, d, D_EXPERT), d ** -0.5),
        "moe_w_up": nrm((DEPTH, N_EXPERTS, d, D_EXPERT), d ** -0.5),
        "moe_w_down": nrm((DEPTH, N_EXPERTS, D_EXPERT, d), D_EXPERT ** -0.5),
        "final_norm_g": 1.0 + nrm((d,), 0.1),
    }

def first_block(x, c, rel_bias, norm1_g, norm2_g, w_ada, b_ada, ev_w_in, ev_w_out,
              ev_gmlp_ln_g, ev_gmlp_ln_b, ev_w_s, ev_b_s, od_w_in, od_w_out, od_w_dw,
              od_b_dw, od_conv_ln_g, od_conv_ln_b, moe_w_group, moe_b_group, moe_w_router,
              moe_b_router, moe_w_gate, moe_w_up, moe_w_down, final_norm_g):
    b, s, _ = x.shape
    for layer in range(DEPTH):
        j = layer // 2
        mod = jax.nn.silu(c) @ w_ada[layer] + b_ada[layer]
        sh1, sc1, g1, sh2, sc2, g2 = jnp.split(mod[:, None, :], 6, axis=-1)
        hcur = rms_norm(x, norm1_g[layer]) * (1 + sc1) + sh1
        if layer % 2 == 0:
            proj = hcur @ ev_w_in[j]
            q, k, v, u, gv = jnp.split(
                proj, [A_WIDTH, 2 * A_WIDTH, 3 * A_WIDTH, 3 * A_WIDTH + B_WIDTH], axis=-1)
            o_a = dilated_attention(q.reshape(b, s, A_HEADS, HEAD_DIM),
                                    k.reshape(b, s, A_HEADS, HEAD_DIM),
                                    v.reshape(b, s, A_HEADS, HEAD_DIM), rel_bias)
            o_b = spatial_gating(u, gv, ev_gmlp_ln_g[j], ev_gmlp_ln_b[j], ev_w_s[j], ev_b_s[j])
            mix = jnp.concatenate([o_a.astype(x.dtype), o_b.astype(x.dtype)], -1) @ ev_w_out[j]
        else:
            proj = hcur @ od_w_in[j]
            a, gate, q, k, v = jnp.split(
                proj, [C_WIDTH, 2 * C_WIDTH, 2 * C_WIDTH + D_WIDTH, 2 * C_WIDTH + 2 * D_WIDTH], axis=-1)
            o_c = conv_module(a, gate, od_w_dw[j], od_b_dw[j], od_conv_ln_g[j], od_conv_ln_b[j])
            o_d = stick_breaking_attention(q.reshape(b, s, D_HEADS, HEAD_DIM),
                                           k.reshape(b, s, D_HEADS, HEAD_DIM),
                                           v.reshape(b, s, D_HEADS, HEAD_DIM))
            mix = jnp.concatenate([o_c.astype(x.dtype), o_d.astype(x.dtype)], -1) @ od_w_out[j]
        x = x + g1 * mix
        hcur = rms_norm(x, norm2_g[layer]) * (1 + sc2) + sh2
        x = x + g2 * hierarchical_moe(hcur, moe_w_group[layer], moe_b_group[layer],
                                      moe_w_router[layer], moe_b_router[layer],
                                      moe_w_gate[layer], moe_w_up[layer], moe_w_down[layer])
    return rms_norm(x, final_norm_g)


DEPTH_2 = 1

GRID_W = 64
D_A = D_MODEL
A_BLOCKS = 16
A_BW = D_A // A_BLOCKS
CONV_W = 4
RG_C = 8.0
N_HEADS = 16
D_B = N_HEADS * HEAD_DIM
WIN_R = 8
WIN_C = 16
IN_SPLITS = (D_A, D_A, D_B, D_B, D_B, D_B, D_MODEL, D_MODEL)
IN_COLS = sum(IN_SPLITS)


def rms_norm_2(x, g):
    x32 = x.astype(jnp.float32)
    y = x32 * lax.rsqrt(jnp.mean(x32 * x32, axis=-1, keepdims=True) + EPS)
    return (y * g.astype(jnp.float32)).astype(x.dtype)

def block_diag(x, w, b):
    B, S, C = x.shape
    xr = x.reshape(B, S, A_BLOCKS, A_BW)
    return jnp.einsum('bshi,hij->bshj', xr, w).reshape(B, S, C) + b

def centred_dwconv(x, w, b):
    C = x.shape[-1]
    y = lax.conv_general_dilated(
        x, w[:, None, :].astype(x.dtype), window_strides=(1,),
        padding=[(CONV_W // 2, CONV_W - 1 - CONV_W // 2)],
        dimension_numbers=('NWC', 'WIO', 'NWC'), feature_group_count=C)
    return y + b

def _lin_combine(e1, e2):
    a1, b1 = e1
    a2, b2 = e2
    return a1 * a2, a2 * b1 + b2

def rg_lru(x, w_r, b_r, w_i, b_i, lam, reverse):
    x32 = x.astype(jnp.float32)
    r = jax.nn.sigmoid(block_diag(x, w_r, b_r).astype(jnp.float32))
    i = jax.nn.sigmoid(block_diag(x, w_i, b_i).astype(jnp.float32))
    log_a = -RG_C * r * jax.nn.softplus(-lam.astype(jnp.float32))
    a = jnp.exp(log_a)
    u = jnp.sqrt(-jnp.expm1(2.0 * log_a)) * (i * x32)
    _, h = lax.associative_scan(_lin_combine, (a, u), axis=1, reverse=reverse)
    return h

def neighbourhood_attention(q, k, v, rpb):
    B, S, H, dh = q.shape
    rows = S // GRID_W
    win_r = min(WIN_R, rows)
    qg = q.reshape(B, rows, GRID_W, H, dh)
    kg = k.reshape(B, rows, GRID_W, H, dh)
    vg = v.reshape(B, rows, GRID_W, H, dh)
    cols = jnp.arange(GRID_W)
    c0 = jnp.clip(cols - WIN_C // 2, 0, GRID_W - WIN_C)
    cidx = c0[:, None] + jnp.arange(WIN_C)[None, :]
    dcol = cidx - cols[:, None] + (WIN_C - 1)
    scale = dh ** -0.5

    def row_fn(r):
        r0 = jnp.clip(r - win_r // 2, 0, rows - win_r)
        q_r = lax.dynamic_index_in_dim(qg, r, axis=1, keepdims=False)
        k_rows = lax.dynamic_slice_in_dim(kg, r0, win_r, axis=1)
        v_rows = lax.dynamic_slice_in_dim(vg, r0, win_r, axis=1)
        k_win = k_rows[:, :, cidx]
        v_win = v_rows[:, :, cidx]
        s = jnp.einsum('bqhd,bwqkhd->bhqwk', q_r, k_win).astype(jnp.float32) * scale
        drow = r0 + jnp.arange(win_r) - r + (WIN_R - 1)
        bias = rpb[:, drow][:, :, dcol]
        s = s + jnp.transpose(bias, (0, 2, 1, 3)).astype(jnp.float32)[None]
        p = jax.nn.softmax(s.reshape(B, H, GRID_W, win_r * WIN_C), axis=-1)
        p = p.reshape(B, H, GRID_W, win_r, WIN_C).astype(v.dtype)
        return jnp.einsum('bhqwk,bwqkhd->bqhd', p, v_win)

    out = lax.map(row_fn, jnp.arange(rows))
    return jnp.transpose(out, (1, 0, 2, 3, 4)).reshape(B, S, H * dh)

def second_inputs(seed: int = 0) -> dict:
    key = jax.random.key(seed)
    ks = jax.random.split(key, 26)
    n = lambda k, shp, s: jax.random.normal(k, shp, jnp.float32) * s

    def lam_init(k):
        a0 = jax.random.uniform(k, (DEPTH_2, D_A), jnp.float32, 0.9, 0.999)
        u = a0 ** (1.0 / RG_C)
        return jnp.log(u) - jnp.log1p(-u)

    return {
        "x": n(ks[0], (BATCH, SEQ, D_MODEL), 1.0),
        "c": n(ks[1], (BATCH, D_MODEL), 1.0),
        "g_pre": 1.0 + n(ks[2], (DEPTH_2, D_MODEL), 0.02),
        "w_c": n(ks[3], (DEPTH_2, D_MODEL, 3 * D_MODEL), D_MODEL ** -0.5),
        "b_c": n(ks[4], (DEPTH_2, 3 * D_MODEL), 0.02),
        "w_in": n(ks[5], (DEPTH_2, D_MODEL, IN_COLS), D_MODEL ** -0.5),
        "conv_w": n(ks[6], (DEPTH_2, CONV_W, D_A), CONV_W ** -0.5),
        "conv_b": n(ks[7], (DEPTH_2, D_A), 0.02),
        "w_r_f": n(ks[8], (DEPTH_2, A_BLOCKS, A_BW, A_BW), A_BW ** -0.5),
        "b_r_f": n(ks[9], (DEPTH_2, D_A), 0.02),
        "w_i_f": n(ks[10], (DEPTH_2, A_BLOCKS, A_BW, A_BW), A_BW ** -0.5),
        "b_i_f": n(ks[11], (DEPTH_2, D_A), 0.02),
        "lam_f": lam_init(ks[12]),
        "w_r_b": n(ks[13], (DEPTH_2, A_BLOCKS, A_BW, A_BW), A_BW ** -0.5),
        "b_r_b": n(ks[14], (DEPTH_2, D_A), 0.02),
        "w_i_b": n(ks[15], (DEPTH_2, A_BLOCKS, A_BW, A_BW), A_BW ** -0.5),
        "b_i_b": n(ks[16], (DEPTH_2, D_A), 0.02),
        "lam_b": lam_init(ks[17]),
        "rpb": n(ks[18], (DEPTH_2, N_HEADS, 2 * WIN_R - 1, 2 * WIN_C - 1), 0.1),
        "w_pa": n(ks[19], (DEPTH_2, D_A, D_MODEL), D_A ** -0.5),
        "w_pb": n(ks[20], (DEPTH_2, D_B, D_MODEL), D_B ** -0.5),
        "w_o": n(ks[21], (DEPTH_2, D_MODEL, D_MODEL), D_MODEL ** -0.5),
        "g_final": 1.0 + n(ks[22], (D_MODEL,), 0.02),
    }

def second_block(x, c, g_pre, w_c, b_c, w_in, conv_w, conv_b, w_r_f, b_r_f, w_i_f, b_i_f, lam_f,
              w_r_b, b_r_b, w_i_b, b_i_b, lam_b, rpb, w_pa, w_pb, w_o, g_final):
    B, S, D = x.shape
    split_pts = list(np.cumsum(IN_SPLITS)[:-1])
    for l in range(DEPTH_2):
        mod = jax.nn.silu(c) @ w_c[l] + b_c[l]
        shift, scl, gate = jnp.split(mod, 3, axis=-1)
        h = rms_norm_2(x, g_pre[l]) * (1.0 + scl[:, None, :]) + shift[:, None, :]

        proj = h @ w_in[l]
        xa, za, q, k, v, zb, ga, gb = jnp.split(proj, split_pts, axis=-1)

        xa = centred_dwconv(xa, conv_w[l], conv_b[l])
        h_fwd = rg_lru(xa, w_r_f[l], b_r_f[l], w_i_f[l], b_i_f[l], lam_f[l], reverse=False)
        h_bwd = rg_lru(xa, w_r_b[l], b_r_b[l], w_i_b[l], b_i_b[l], lam_b[l], reverse=True)
        y_a = (h_fwd + h_bwd).astype(x.dtype) * jax.nn.silu(za)
        y_a = y_a @ w_pa[l]

        qh = q.reshape(B, S, N_HEADS, HEAD_DIM)
        kh = k.reshape(B, S, N_HEADS, HEAD_DIM)
        vh = v.reshape(B, S, N_HEADS, HEAD_DIM)
        y_b = neighbourhood_attention(qh, kh, vh, rpb[l]) * jax.nn.silu(zb)
        y_b = y_b @ w_pb[l]

        merged = jax.nn.sigmoid(ga) * y_a + jax.nn.sigmoid(gb) * y_b
        x = x + gate[:, None, :] * (merged @ w_o[l])
    return rms_norm_2(x, g_final)


def setup_inputs(seed=0):
    out = dict(first_inputs(seed))
    for name, value in second_inputs(seed + 1).items():
        if name != "x":
            out[name + "_2"] = value
    return out


def reference(
    x, c, rel_bias, norm1_g, norm2_g, w_ada, b_ada, ev_w_in, ev_w_out, ev_gmlp_ln_g,
    ev_gmlp_ln_b, ev_w_s, ev_b_s, od_w_in, od_w_out, od_w_dw, od_b_dw, od_conv_ln_g,
    od_conv_ln_b, moe_w_group, moe_b_group, moe_w_router, moe_b_router, moe_w_gate, moe_w_up,
    moe_w_down, final_norm_g, c_2, g_pre_2, w_c_2, b_c_2, w_in_2, conv_w_2, conv_b_2, w_r_f_2,
    b_r_f_2, w_i_f_2, b_i_f_2, lam_f_2, w_r_b_2, b_r_b_2, w_i_b_2, b_i_b_2, lam_b_2, rpb_2,
    w_pa_2, w_pb_2, w_o_2, g_final_2,
):
    x = first_block(
        x, c, rel_bias, norm1_g, norm2_g, w_ada, b_ada, ev_w_in, ev_w_out, ev_gmlp_ln_g,
        ev_gmlp_ln_b, ev_w_s, ev_b_s, od_w_in, od_w_out, od_w_dw, od_b_dw, od_conv_ln_g,
        od_conv_ln_b, moe_w_group, moe_b_group, moe_w_router, moe_b_router, moe_w_gate,
        moe_w_up, moe_w_down, final_norm_g,
    )
    return second_block(
        x, c_2, g_pre_2, w_c_2, b_c_2, w_in_2, conv_w_2, conv_b_2, w_r_f_2, b_r_f_2, w_i_f_2,
        b_i_f_2, lam_f_2, w_r_b_2, b_r_b_2, w_i_b_2, b_i_b_2, lam_b_2, rpb_2, w_pa_2, w_pb_2,
        w_o_2, g_final_2,
    )


_drawn_inputs = setup_inputs


def setup_inputs(seed=0):
    import zlib

    import numpy as np

    out = dict(_drawn_inputs(seed))
    spreads = {}
    factors = {'ev_gmlp_ln_g': 3.842,
     'ev_gmlp_ln_b': 8.0,
     'ev_b_s': 2.827,
     'od_b_dw': 7.937,
     'od_conv_ln_g': 2.678,
     'od_conv_ln_b': 8.0,
     'moe_b_group': 8.0,
     'moe_b_router': 8.0,
     'g_pre_2': 3.391,
     'b_r_f_2': 50.764,
     'b_i_f_2': 29.635,
     'b_r_b_2': 59.419,
     'b_i_b_2': 29.833,
     'rpb_2': 8.0,
     'g_final_2': 8.53,
     'conv_b_2': 4.234}
    for name, (base, spread) in spreads.items():
        noise = np.random.default_rng([zlib.crc32(name.encode()), seed]).standard_normal(out[name].shape)
        drawn = base * np.exp(spread * noise) if base else spread * noise
        out[name] = __import__('jax').numpy.asarray(drawn.astype(out[name].dtype))
    for name, factor in factors.items():
        out[name] = (out[name] * factor).astype(out[name].dtype)
    return out
```

```python
from contextlib import ExitStack

import numpy as np
import concourse.bass as bass
from concourse import mybir

F32 = mybir.dt.float32
BF16 = mybir.dt.bfloat16
I32 = mybir.dt.int32
ALU = mybir.AluOpType
ACT = mybir.ActivationFunctionType
AX = mybir.AxisListType.X

P = 128
D = 1024
KT = D // P
S = 256
TT = S // P
HW = 512
EPS = 1e-6
NEG = -1e30
RING = 6
LAYERS = 2
EXPERTS = 16
PAIRS = EXPERTS // 2
SLOTS = 64
CAP = float(SLOTS)
LATE = min(EXPERTS, int(2 * S // (CAP + 1)))
CONV = 31
PAD = CONV - 1
ADA_SEG = 12
N_ADA = 2 * ADA_SEG + 6
GRID = 64
WIN = 16

CV_C, CV_C2, CV_N1, CV_N2, CV_GPRE = 120, 128, 136, 152, 168
CV_BDW, CV_LNG, CV_LNB, CV_CB2 = 176, 180, 184, 188
CV_RF, CV_IF, CV_RB, CV_IB, CV_LF, CV_LB = 196, 204, 212, 220, 228, 236
CV_DW, CV_CW2, CV_END = 244, 368, 400

K_ID, K_GE, K_LT, K_ONE, K_NEG, K_NAM, K_IOTA, K_W = 0, 128, 256, 384, 512, 640, 704, 768
K_END = 772
K2_MULT, K2_LE, K2_END = 0, 256, 384


def tables():
    i = np.arange(P)
    a = np.zeros((P, K_END), np.float32)
    a[:, K_ID:K_ID + P] = np.eye(P)
    a[:, K_GE:K_GE + P] = i[:, None] >= i[None, :]
    a[:, K_LT:K_LT + P] = i[:, None] < i[None, :]
    a[:, K_ONE:K_ONE + P] = 1.0
    a[:, K_NEG:K_NEG + P] = np.where(i[:, None] < i[None, :], 0.0, NEG)
    col = i % GRID
    first = np.clip(col - WIN // 2, 0, GRID - WIN)
    kc = np.arange(GRID)
    inside = (kc[None] >= first[:, None]) & (kc[None] < first[:, None] + WIN)
    a[:, K_NAM:K_NAM + GRID] = np.where(inside, 0.0, NEG)
    a[:, K_IOTA:K_IOTA + SLOTS] = np.where(np.arange(SLOTS) < CAP, np.arange(1, SLOTS + 1), -1)
    a[:, K_W:K_W + 4] = [4, 3, 2, 1]

    def branches(dist):
        n = (dist <= 128).astype(np.float32) + (dist % 4 == 0) + (dist % 16 == 0)
        return np.where(dist >= 0, n, 0.0)

    b = np.zeros((P, K2_END), np.float32)
    b[:, K2_MULT:K2_MULT + S] = branches(P + i[:, None] - np.arange(S)[None])
    b[:, K2_LE:K2_LE + P] = i[:, None] <= i[None, :]

    dist = 255 - np.arange(384)
    d = np.maximum(np.clip(dist, 0, None), 1).astype(np.float32)
    large = 16 + (np.log(d / 16) / np.log(2048 / 16) * 16).astype(np.int32)
    bucket = np.where(dist < 16, np.clip(dist, 0, None), np.minimum(large, 31))
    e = np.zeros((64, 384), np.float32)
    valid = branches(dist) > 0
    e[bucket[valid], np.nonzero(valid)[0]] = 1.0
    e[32] = np.where(valid, 0.0, NEG)
    return a, b, e


def stream():
    u = [("ada", n) for n in range(4)]
    u += [("ev", 0), ("ada", 4), ("ev", 1), ("ada", 5), ("ev", 2)]
    u += [("ev", 4), ("ada", 6), ("ev", 3), ("ada", 7)]
    u += [("ada", n) for n in range(8, 20)]
    u += [("evo", 0), ("evo", 1)]
    u += [("moe", 0)] * (6 * PAIRS)
    u += [("od", 0), ("od", 1), ("od", 2), ("od", 3), ("od", 4)]
    u += [("ada", n) for n in range(20, 28)]
    u += [("odo", 0), ("ada", 28), ("odo", 1), ("ada", 29)]
    u += [("moe", 1)] * (6 * PAIRS)
    u += [("in", n) for n in (0, 1, 4, 6, 8, 2, 3, 10, 11, 5, 7, 9, 12, 13)]
    u += [("pa", 0), ("pa", 1), ("in", 14), ("in", 15), ("pb", 0), ("pb", 1), ("wo", 0), ("wo", 1)]
    return u


def program(nc, a, out):
    ctx = ExitStack()
    with ctx:
        named = {}

        def sem(name):
            if name not in named:
                named[name] = ctx.enter_context(nc.semaphore(name))
            return named[name]

        def sb(name, shape, dt=F32):
            return ctx.enter_context(nc.sbuf_tensor(name, shape, dt))

        units = stream()
        moe_start = [units.index(("moe", layer)) for layer in range(LAYERS)]

        ring = sb("ring", [P, RING, 4096])
        x = sb("x", [P, TT, D])
        cv = sb("cv", [P, CV_END])
        mod = sb("mod", [P, N_ADA * 4])
        kc = sb("kc", [P, K_END])
        gate_bc = sb("gate_bc", [P, D])
        ada_part = sb("ada_part", [P, HW])
        c_rep = sb("c_rep", [P, 2, KT, 32])
        gs = sb("gs", [P, 5, 2, KT])
        small = sb("small", [P, 64])
        rw = sb("rw", [P, KT, 20])
        rb = sb("rb", [P, 20])
        gates_over = sb("gates_over", [P, TT, EXPERTS])
        gates = sb("gates", [P, TT, EXPERTS])
        late = sb("late", [P, LAYERS, 2, EXPERTS], I32)
        rgc = sb("rgc", [P, 48])
        rgt = sb("rgt", [P, 48])
        AR = 88 * 256
        arena = sb("arena", [P, AR])
        ps = [ctx.enter_context(nc.psum_tensor(f"bank{n}", [P, 512], F32)) for n in range(8)]

        def at(kb, *shape):
            n = int(np.prod(shape))
            v = arena[:, int(kb * 256):int(kb * 256) + n]
            if len(shape) == 2:
                v = v.rearrange("p (a b) -> p a b", b=shape[1])
            if len(shape) == 3:
                v = v.rearrange("p (a b c) -> p a b c", b=shape[1], c=shape[2])
            return v

        xn = at(0, TT, D)
        hT = at(8, KT, S)
        oT = at(16, KT, S)
        qT, kT, v_tok = at(24, 4, S), at(28, 4, S), at(32, TT, HW)
        gv, uT = at(36, TT, HW), at(40, 4, S)
        lng_bc, lnb_bc, bs_bc = at(44, HW), at(46, HW), at(48, 4, P)
        wsT, ws_raw = at(50, 4, P), at(52, 4, P)
        onehot, rel_ext, bias_rows = at(54, 384), at(55.5, 8), at(56, 384)
        stage = at(57.5, 4, P)
        bias_a = at(76, 8, S)
        k2 = at(84, K2_END)
        pr = at(60.5, 2, 512)
        prT = at(64.5, 512)
        aT, glT, hcT = at(36, 4, S), at(40, 4, S), at(44, 4, PAD + S)
        cacc, csq = at(48.5, 4, S), at(52.5, 4, S)
        crs = at(56.5, S)
        z_sb, e_sb, sp_sb, att_sb = at(60.5, 2, 384), at(63.5, 2, 384), at(66.5, 2, 384), at(69.5, 2, 384)
        gT = at(16, PAIRS, S)
        xgT = at(24, PAIRS, KT, P)
        pick, pick_g = at(56, TT, EXPERTS, SLOTS), at(64, TT, EXPERTS, SLOTS)
        rt = at(24, 1024)
        x_cur, g_cur, silu_g = at(56, KT, P), at(60, S), at(61, HW)
        hid, hidT, y_pair = at(64, HW), at(66, 4, P), at(68, D)
        o_w = [at(24, 4096), at(40, 4096), at(56, 4096)]
        o_hidT, o_silu = at(16, 4, S), at(20, 4, S)
        fn_bc = at(72, D)
        zbT = at(0, KT, S)
        xa_raw = at(36, KT, 3 + S)
        gaT = at(36, KT, S)
        xc = at(44.5, KT, S)
        gbT = at(44.5, KT, S)
        yaT = at(52.5, KT, S)
        rg_t, rg_ti, rg_root = ([at(66.5 + 2 * n + w, S) for w in range(2)] for n in range(3))
        rg_u, rg_hf, rg_hb, rg_inv, rg_dec = (at(kb, S) for kb in (72.5, 73.5, 74.5, 82, 83))
        bias_n = at(76, 2, 2, 6 * GRID)
        rg_w = at(84, 2, 4, P)
        gf_bc = at(24, D)

        ident = kc[:, K_ID:K_ID + P]
        ge = kc[:, K_GE:K_GE + P]
        lt = kc[:, K_LT:K_LT + P]
        ones = kc[:, K_ONE:K_ONE + P]
        neg_diag = kc[:, K_NEG:K_NEG + P]

        bias_dram = nc.dram_tensor("bias_rows_dram", (8, P, 384), F32, kind="Internal").ap()
        rpb_dram = nc.dram_tensor("rpb_rows_dram", (16, GRID, 7, P), F32, kind="Internal").ap()
        rpb_pad = at(70, 7, P)

        def bc(ap, shape):
            return ap.to_broadcast(shape)

        loaded = [sem(f"ring_loaded{n}") for n in range(RING)]
        bank_full = [sem(f"bank_full{n}") for n in range(4)]
        bank_free = [sem(f"bank_free{n}") for n in range(4)]
        unit_done = sem("unit_done")
        gather_taken = [sem("gather_taken_act"), sem("gather_taken_dve")]

        dense = {}
        for name in ("ev0 ev1 ev2 ev4 ev3 mixA gateA evo0 evo1 gateB "
                     "od0 od1 od2 od3 od4 gateC odo0 odo1 gateD "
                     "in0 in1 in4 in6 in8 in2 in3 in10 in11 in5 in7 in9 in12 in13 "
                     "pa0 pa1 in14 in15 pb0 pb1 gateE wo0 wo1").split():
            dense[name] = len(dense)

        unit_of = {f"{kind}{i}": n for n, (kind, i) in enumerate(units) if kind != "moe"}

        def full_at(eng, name, b):
            n = dense[name]
            k = 2 * (n % 2) + b
            if b and name in unit_of:
                eng.wait_ge(unit_done, unit_of[name] + 1)
            elif b:
                before = [m for m in dense if dense[m] <= n and dense[m] % 2 == n % 2 and m not in unit_of]
                eng.wait_ge(bank_full[k], len(before))
            else:
                eng.wait_ge(bank_full[k], n // 2 + 1)
            return ps[k], bank_free[k]

        def taken(eng, name):
            n = dense[name]
            for b in range(2):
                eng.wait_ge(bank_free[2 * (n % 2) + b], n // 2 + 1)

        block = ctx.enter_context(nc.Block())

        class Steps:

            def __init__(self, eng, name):
                self.eng, self.sem, self.n = eng, sem(name), 0

            def __call__(self, ins):
                ins.then_inc(self.sem, 1)
                self.n += 1

            def wait(self):
                self.eng.wait_ge(self.sem, self.n)

        SUMSQ, RSTD, NEGMAX, DEN, RDEN, BN, MV = 0, 2, 4, 8, 12, 16, 30

        w_of = {
            "ev": a["ev_w_in"][0], "evo": a["ev_w_out"][0], "od": a["od_w_in"][0], "odo": a["od_w_out"][0],
            "in": a["w_in_2"][0], "pa": a["w_pa_2"][0], "pb": a["w_pb_2"][0], "wo": a["w_o_2"][0],
        }

        @block.sync
        def _(sp):
            def fetch(n, src):
                if n >= RING:
                    sp.wait_ge(unit_done, n - RING + 1)
                sp.dma_start(ring[:, n % RING, :].rearrange("p (k c) -> p k c", c=src.shape[2]), src)\
                  .then_inc(loaded[n % RING], 16)

            def layout(w, c0):
                return w[:, c0:c0 + 512].rearrange("(k p) c -> p k c", p=P)

            n = 0
            while n < len(units):
                kind, i = units[n]
                if kind == "moe":
                    w_gate, w_up, w_down = (a[f"moe_w_{w}"][i] for w in ("gate", "up", "down"))
                    first = moe_start[i]
                    with sp.Fori(0, PAIRS) as j:
                        for m, (w, e) in enumerate([(w_gate, 0), (w_gate, 1), (w_up, 0), (w_up, 1),
                                                    (w_down, 0), (w_down, 1)]):
                            s = (first + m) % RING
                            sp.wait_ge(unit_done, j * RING + (first + m - RING + 1))
                            src = w[bass.ds(2 * j + e, 1)].rearrange("e (k p) c -> p (e k) c", p=P)
                            sp.dma_start(ring[:, s, :].rearrange("p (k c) -> p k c", c=src.shape[2]), src)\
                              .then_inc(loaded[s], 16)
                    n += 6 * PAIRS
                    continue
                if kind == "ada":
                    w = a["w_ada"][i // ADA_SEG] if i < 2 * ADA_SEG else a["w_c_2"][0]
                    fetch(n, layout(w, 512 * (i % ADA_SEG)))
                else:
                    fetch(n, layout(w_of[kind], 512 * i))
                n += 1

            sp.wait_ge(sem("out_ready"), 2)
            sp.dma_start(out.rearrange("b (t p) d -> p (b t) d", p=P), x[:, :, :]).then_inc(sem("out_sent"), 16)
            sp.wait_ge(sem("out_sent"), 16)

        @block.tensor
        def _(pe):
            unit = [0]

            def weights():
                n = unit[0]
                unit[0] += 1
                pe.wait_ge(loaded[n % RING], 16 * (n // RING + 1))
                return ring[:, n % RING, :].rearrange("p (k c) -> p k c", c=512)

            def bank_of(name, b):
                n = dense[name]
                k = 2 * (n % 2) + b
                if n >= 2:
                    pe.wait_ge(bank_free[k], n // 2)
                return k

            def by_channel(name, rhs):
                w = weights()
                for b in range(2):
                    k0 = bank_of(name, b)
                    for t in range(2):
                        c = (2 * b + t) * P
                        for k in range(KT):
                            mm = pe.matmul(ps[k0][:, t * S:(t + 1) * S], w[:, k, c:c + P], rhs[:, k, :],
                                           start=(k == 0), stop=(k == KT - 1))
                    mm.then_inc(unit_done if b else bank_full[k0], 1)

            def by_token(name, lhs):
                w = weights()
                for b in range(TT):
                    k0 = bank_of(name, b)
                    for k in range(KT):
                        mm = pe.matmul(ps[k0][:, :], lhs[:, k, b * P:(b + 1) * P], w[:, k, :],
                                       start=(k == 0), stop=(k == KT - 1))
                    mm.then_inc(unit_done if b else bank_full[k0], 1)

            ada = [0, 0]

            def ada_main():
                n = ada[0]
                ada[0] += 1
                w = weights()
                if n:
                    pe.wait_ge(sem("ada_ready"), n)
                else:
                    pe.wait_ge(sem("c_ready"), 1)
                for r in range(2):
                    for g in range(4):
                        mm = pe.matmul(ps[4][32 * g:32 * g + 32, :], c_rep[:, n // (2 * ADA_SEG), 4 * r + g, :],
                                       w[:, 4 * r + g, :], start=(r == 0), stop=(r == 1),
                                       tile_position=(0, 32 * g))
                mm.then_inc(unit_done, 1)

            def ada_columns():
                n = ada[1]
                ada[1] += 1
                pe.wait_ge(sem("ada_part_taken"), n + 1)
                for c in range(4):
                    mm = pe.matmul(ps[4][:, c:c + 1], ada_part[:, c * P:(c + 1) * P], ones[:, 0:1],
                                   start=True, stop=True)
                mm.then_inc(sem("ada_cols_full"), 1)

            def gate_rows(name):
                pe.wait_ge(sem("diag_ready"), "ABCDE".index(name[-1]) + 1)
                for b in range(2):
                    k0 = bank_of(name, b)
                    pe.matmul(ps[k0][:, :], ones, gate_bc[:, b * 512:(b + 1) * 512], start=True, stop=True)\
                      .then_inc(bank_full[k0], 1)

            def turn_x(r):
                pe.wait_ge(sem("xn_ready_act"), r + 1)
                pe.wait_ge(sem("xn_ready_dve"), r + 1)
                for b in range(4):
                    for k in (2 * b, 2 * b + 1):
                        for t in range(TT):
                            o = (k % 2) * S + t * P
                            mm = pe.transpose(ps[b][:, o:o + P], xn[:, t, k * P:(k + 1) * P], ident)
                    mm.then_inc(sem("turned"), 1)
                pe.wait_ge(sem("hT_act"), r + 1)
                pe.wait_ge(sem("hT_dve"), r + 1)

            pe.wait_ge(sem("kc_loaded"), 16)
            pe.wait_ge(sem("stage_loaded"), 16 * 25)
            for n, (lo, rows) in enumerate(((0, P), (P, 116), (CV_DW, 124), (CV_CW2, 32))):
                mm = pe.transpose(ps[5][:, n * P:n * P + rows], stage[0:rows, n, :], ident[0:rows, 0:rows])
            mm.then_inc(sem("cv_full"), 1)
            pe.wait_ge(sem("cv_ready"), 1)
            pe.wait_ge(sem("onehot_loaded"), 32)
            pe.wait_ge(sem("rel_ones"), 1)
            pe.matmul(ps[5][0:8, 0:384], rel_ext[0:64, :], onehot[0:64, :], start=True, stop=True)\
              .then_inc(sem("bias_full"), 1)
            pe.wait_ge(sem("ws_loaded"), 16)
            for g in range(4):
                mm = pe.transpose(ps[6][:, g * P:(g + 1) * P], ws_raw[:, g, :], ident)
            mm.then_inc(sem("ws_full"), 1)
            for n in range(4):
                ada_main()
                ada_columns()
            turn_x(0)

            head = [0]

            def scores(h, rows, kind):
                n = head[0]
                head[0] += 1
                bank = ps[6 + n % 2]
                if n >= 2:
                    pe.wait_ge(sem("o_taken"), n - 1)
                p0 = 64 * (h % 2)
                q, k = qT[p0:p0 + 64, h // 2 % 4, :], kT[p0:p0 + 64, h // 2 % 4, :]
                if kind == "dilated":
                    pe.matmul(bank[:, 0:S], q[:, P:S], k[:, :], start=True, stop=True)
                    mm = pe.matmul(bank[:, S:S + P], q[:, 0:P], k[:, 0:P], start=True, stop=True)
                elif kind == "stick":
                    pe.matmul(bank[:, 0:S], k[:, 0:P], q[:, :], start=True, stop=True)
                    mm = pe.matmul(bank[:, S:S + P], k[:, P:S], q[:, P:S], start=True, stop=True)
                else:
                    pe.matmul(bank[:, 0:S], q[:, 0:P], k[:, :], start=True, stop=True)
                    mm = pe.matmul(bank[:, S:2 * S], q[:, P:S], k[:, :], start=True, stop=True)
                mm.then_inc(sem("scores_full"), 1)

            def values(n, h, kind):
                pe.wait_ge(sem("probs_ready"), n + 1)
                bank, vt = ps[6 + n % 2], v_tok[:, :, 64 * (h % 8):64 * (h % 8) + 64]
                if kind == "stick":
                    sp_h = sp_sb[:, n % 2, :]
                    pe.matmul(ps[5][:, 0:S], ge, sp_h[:, 0:S], start=True, stop=True)
                    pe.matmul(ps[5][:, P:S], ones, sp_h[:, S:S + P], start=False, stop=True, skip_group_check=True)
                    mm = pe.matmul(ps[5][:, S:S + P], ge, sp_h[:, S:S + P], start=True, stop=True)
                    mm.then_inc(sem("probsT_full"), 1)
                    pe.wait_ge(sem("probsT_ready"), n + 1)
                    rhs = att_sb[:, n % 2, :]
                else:
                    p = pr[:, n % 2, :]
                    if kind == "dilated":
                        blocks = [p[:, S:S + P], p[:, 0:P], p[:, P:S]]
                    else:
                        blocks = [p[:, 0:P], p[:, S:S + P], p[:, P:S], p[:, S + P:2 * S]]
                    for m, blk in enumerate(blocks):
                        mm = pe.transpose(ps[5][:, m * P:(m + 1) * P], blk, ident)
                    mm.then_inc(sem("probsT_full"), 1)
                    pe.wait_ge(sem("probsT_ready"), n + 1)
                    rhs = prT
                o = bank[64 * (h % 2):64 * (h % 2) + 64, 0:S]
                if kind == "near":
                    pe.matmul(o, vt[:, 0, :], rhs[:, 0:S], start=True, stop=False)
                    mm = pe.matmul(o, vt[:, 1, :], rhs[:, S:2 * S], start=False, stop=True)
                else:
                    pe.matmul(o, vt[:, 0, :], rhs[:, 0:S], start=True, stop=True)
                    mm = pe.matmul(o[:, P:S], vt[:, 1, :], rhs[:, S:S + P], start=False, stop=True,
                                   skip_group_check=True)
                mm.then_inc(sem("o_full"), 1)

            def heads(lo, hi, kind, between, after=lambda h: None):
                base = head[0]
                scores(lo, 0, kind)
                for h in range(lo, hi):
                    if h + 1 < hi:
                        scores(h + 1, 0, kind)
                    between(h)
                    values(base + h - lo, h, kind)
                    after(h)

            def experts(layer):
                first = moe_start[layer]
                taken(pe, "gateB" if layer == 0 else "gateD")
                pe.wait_ge(sem("rw_loaded"), 16 * 7 * (layer + 1))
                for t in range(TT):
                    for k in range(KT):
                        mm = pe.matmul(ps[4][:, 20 * t:20 * t + 20], hT[:, k, t * P:(t + 1) * P], rw[:, k, :],
                                       start=(k == 0), stop=(k == KT - 1))
                mm.then_inc(sem("logits_full"), 1)
                pe.wait_ge(sem("mask_ready"), layer + 1)
                mask = rt[:, 512:512 + 32].rearrange("p (t e) -> p t e", e=EXPERTS)
                pe.matmul(ps[5][:, 0:16], lt, mask[:, 0, :], start=True, stop=True)
                pe.matmul(ps[5][:, 16:32], ones, mask[:, 0, :], start=True, stop=False)
                pe.matmul(ps[5][:, 16:32], lt, mask[:, 1, :], start=False, stop=True)\
                  .then_inc(sem("rank_full"), 1)
                pe.wait_ge(sem("over_ready"), layer + 1)
                pe.matmul(ps[4][:, 0:32], ones, rt[:, 576:608], start=True, stop=True)\
                  .then_inc(sem("over_full"), 1)
                pe.wait_ge(sem("late_ready"), layer + 1)
                pe.wait_ge(sem("pick_ready"), layer + 1)
                for q in range(16):
                    k, half = q // 2, q % 2
                    bank = ps[4 + q % 4]
                    if q >= 4:
                        pe.wait_ge(gather_taken[q % 2], 8 * layer + q // 2 - 1)
                    for t in range(TT):
                        mm = pe.matmul(bank[:, :], xn[:, t, k * P:(k + 1) * P],
                                       pick[:, t, 8 * half:8 * half + 8, :].rearrange("p e s -> p (e s)"),
                                       start=(t == 0), stop=(t == TT - 1))
                    mm.then_inc(sem("gather_full"), 1)
                pe.wait_ge(sem("pick_g_ready"), layer + 1)
                for b in range(4):
                    for m in range(2):
                        for t in range(TT):
                            src = pick_g[:, t, 4 * b + 2 * m:4 * b + 2 * m + 2, :].rearrange("p e s -> p (e s)")
                            o = m * S + t * P
                            mm = pe.transpose(ps[b][:, o:o + P], src, ident)
                    mm.then_inc(sem("gT_full"), 1)
                for q in range(2):
                    pe.wait_ge(gather_taken[q], 8 * layer + 8)
                pe.wait_ge(sem("gT_ready_act"), 2 * (layer + 1))
                pe.wait_ge(sem("gT_ready_dve"), 2 * (layer + 1))
                pe.wait_ge(sem("zeros_ready"), layer + 1)
                zero = hidT[:, 0:2, :].rearrange("p a b -> p (a b)").bitcast(BF16)
                for b in range(4):
                    mm = pe.matmul(ps[b][:, :], zero[:, 0:P], zero, start=True, stop=True, skip_group_check=True)

                def slot(m, j):
                    n = first + m
                    pe.wait_ge(loaded[n % RING], (j + (n // RING + 1)) * 16)
                    return ring[:, n % RING, :]

                done = PAIRS * layer

                def gate_up(j):
                    pe.wait_ge(sem("x_cur_ready"), j + (done + 1))
                    for bank, m0 in ((4, 0), (5, 2)):
                        w = [slot(m0 + e, j).rearrange("p (k c) -> p k c", c=512) for e in range(2)]
                        for k in range(KT):
                            for e in range(2):
                                mm = pe.matmul(ps[bank][64 * e:64 * e + 64, :], x_cur[:, k, 64 * e:64 * e + 64],
                                               w[e][:, k, :], start=(k == 0), stop=(k == KT - 1))
                        mm.then_inc(unit_done, 2)

                def scatter(j):
                    pe.wait_ge(sem("g_cur_ready"), j + (done + 1))
                    pe.wait_ge(sem("y_pair_act"), j + (done + 1))
                    pe.wait_ge(sem("y_pair_dve"), j + (done + 1))
                    for t in range(TT):
                        for half in range(2):
                            mm = pe.matmul(ps[2 * t + half][:, :], g_cur[:, t * P:(t + 1) * P],
                                           y_pair[:, half * 512:(half + 1) * 512], start=False, stop=True,
                                           skip_group_check=True)
                    mm.then_inc(sem("scattered"), 1)

                def down(j):
                    pe.wait_ge(sem("hid_ready"), j + (done + 1))
                    for f in range(4):
                        mm = pe.transpose(ps[6][:, f * P:(f + 1) * P], hid[:, f * P:(f + 1) * P], ident)
                    mm.then_inc(sem("hidT_full"), 1)
                    w = [slot(4 + e, j).rearrange("p (f c) -> p f c", c=D) for e in range(2)]
                    pe.wait_ge(sem("hidT_ready"), j + (done + 1))
                    for half in range(2):
                        for f in range(4):
                            for e in range(2):
                                mm = pe.matmul(ps[6 + half][64 * e:64 * e + 64, :], hidT[:, f, 64 * e:64 * e + 64],
                                               w[e][:, f, half * 512:(half + 1) * 512],
                                               start=(f == 0), stop=(f == 3))
                        if half == 0:
                            mm.then_inc(sem("down_full"), 1)
                        else:
                            mm.then_inc(unit_done, 2)

                gate_up(0)
                down(0)
                with pe.Fori(1, PAIRS) as j:
                    gate_up(j)
                    scatter(j - 1)
                    down(j)
                scatter(PAIRS - 1)
                unit[0] = first + 6 * PAIRS

            def overflow(layer):
                pe.wait_ge(sem("x_summed"), layer + 1)
                with pe.Fori(0, LATE) as j:
                    there = pe.value_load(late[0:1, layer, 0, bass.ds(j, 1)], min_val=0, max_val=1)
                    with pe.If(there > 0):
                        for m, w in enumerate(o_w[:2]):
                            pe.wait_ge(sem(f"o_loaded{layer}{m}"), j * 16 + 16)
                            wv = w.rearrange("p (k c) -> p k c", c=512)
                            for c in range(4):
                                for k in range(KT):
                                    mm = pe.matmul(ps[2 * m + c // 2][:, (c % 2) * S:(c % 2) * S + S],
                                                   wv[:, k, c * P:(c + 1) * P], hT[:, k, :],
                                                   start=(k == 0), stop=(k == KT - 1))
                        mm.then_inc(sem(f"o_hid_full{layer}"), 1)
                        pe.wait_ge(sem(f"o_hid_ready{layer}"), j + 1)
                        pe.wait_ge(sem(f"o_loaded{layer}2"), j * 16 + 16)
                        wv = o_w[2].rearrange("p (f c) -> p f c", c=D)
                        for t in range(TT):
                            for half in range(2):
                                for f in range(4):
                                    mm = pe.matmul(ps[4 + 2 * t + half][:, :], o_hidT[:, f, t * P:(t + 1) * P],
                                                   wv[:, f, half * 512:(half + 1) * 512],
                                                   start=(f == 0), stop=(f == 3))
                        mm.then_inc(sem(f"o_y_full{layer}"), 1)
                        pe.wait_ge(sem(f"o_y_taken{layer}"), j + 1)

            by_channel("ev0", hT)
            ada_main()
            by_channel("ev1", hT)
            ada_columns()
            ada_main()
            by_token("ev2", hT)
            ada_columns()
            for name in ("ev0", "ev1", "ev2"):
                taken(pe, name)

            def between_a(h):
                if h == 0:
                    by_token("ev4", hT)
                    ada_main()
                    ada_columns()
                elif h == 1:
                    by_channel("ev3", hT)
                    ada_main()
                    ada_columns()
                else:
                    for _ in range(2):
                        ada_main()
                        ada_columns()
                if h == 3:
                    pe.wait_ge(sem("gv_ready"), 1)
                    taken(pe, "ev3")
                    pe.wait_ge(sem("wsT_ready"), 1)
                    for b in range(2):
                        k0 = bank_of("mixA", b)
                        for g in (2 * b, 2 * b + 1):
                            for t in range(TT):
                                o = (g % 2) * S + t * P
                                mm = pe.matmul(ps[k0][:, o:o + P], gv[:, t, g * P:(g + 1) * P], wsT[:, g, :],
                                               start=True, stop=True)
                        mm.then_inc(bank_full[k0], 1)
                if h == 5:
                    gate_rows("gateA")

            heads(0, 8, "dilated", between_a)
            pe.wait_ge(sem("o_taken"), 8)
            pe.wait_ge(sem("o_b_ready"), 1)
            by_token("evo0", oT)
            by_token("evo1", oT)
            turn_x(1)
            gate_rows("gateB")
            experts(0)
            overflow(0)
            turn_x(2)

            by_channel("od0", hT)
            by_channel("od1", hT)
            by_channel("od2", hT)
            by_channel("od3", hT)
            by_token("od4", hT)
            for name in ("od2", "od3", "od4"):
                taken(pe, name)

            def between_b(h):
                if h == 2:
                    pe.wait_ge(sem("conv_ready"), 1)
                    for ct in range(4):
                        mm = pe.matmul(ps[0 + 2][:, 0:S], ones, cacc[:, ct, :], start=(ct == 0), stop=(ct == 3))
                    mm.then_inc(sem("mean_full"), 1)
                if h == 4:
                    pe.wait_ge(sem("csq_ready"), 1)
                    for ct in range(4):
                        mm = pe.matmul(ps[0 + 2][:, S:2 * S], ones, csq[:, ct, :], start=(ct == 0), stop=(ct == 3))
                    mm.then_inc(sem("var_full"), 1)
                ada_main()
                ada_columns()
                if h == 6:
                    pe.wait_ge(sem("crs_ready"), 1)
                    gate_rows("gateC")

            heads(0, 8, "stick", between_b)
            pe.wait_ge(sem("o_taken"), 16)
            pe.wait_ge(sem("o_c_ready"), 1)
            by_token("odo0", oT)
            ada_main()
            ada_columns()
            by_token("odo1", oT)
            ada_main()
            ada_columns()
            turn_x(3)
            gate_rows("gateD")
            experts(1)
            overflow(1)

            turn_x(4)
            by_channel("in0", hT)
            by_channel("in1", hT)
            by_channel("in4", hT)
            by_channel("in6", hT)
            by_token("in8", hT)
            for name in ("in4", "in6", "in8"):
                taken(pe, name)
            pe.wait_ge(sem("xc_ready"), 1)

            def recurrence_gates(ct, way):
                n = 2 * ct + way
                if n:
                    pe.wait_ge(sem("rg_gates_taken"), n)
                pe.wait_ge(sem(f"rg_w_loaded{ct % 2}"), 16 * 8 * (ct // 2 + 1))
                for g in range(2):
                    mm = pe.matmul(ps[4][:, g * S:(g + 1) * S], rg_w[:, ct % 2, 2 * way + g, :], xc[:, ct, :],
                                   start=True, stop=True)
                mm.then_inc(sem("rg_gates_full"), 1)

            def between_c(h):
                recurrence_gates(h, 0)
                if h == 0:
                    by_channel("in2", hT)
                if h == 1:
                    by_channel("in3", hT)
                if h == 3:
                    by_channel("in10", hT)
                if h == 5:
                    by_channel("in11", hT)

            heads(0, 8, "near", between_c, lambda h: recurrence_gates(h, 1))
            by_channel("in5", hT)
            by_channel("in7", hT)
            by_token("in9", hT)
            for name in ("in5", "in7", "in9"):
                taken(pe, name)

            def between_d(h):
                if h == 8:
                    by_channel("in12", hT)
                if h == 10:
                    by_channel("in13", hT)
                if h == 12:
                    pe.wait_ge(sem("ya_ready"), KT)
                    by_channel("pa0", yaT)
                if h == 14:
                    by_channel("pa1", yaT)

            heads(8, 16, "near", between_d)
            by_channel("in14", hT)
            by_channel("in15", hT)
            pe.wait_ge(sem("yb_ready"), 1)
            by_channel("pb0", oT)
            by_channel("pb1", oT)
            gate_rows("gateE")
            pe.wait_ge(sem("merged_ready"), 1)
            by_token("wo0", gaT)
            by_token("wo1", gaT)

        @block.scalar
        def _(act):
            step = Steps(act, "act_steps")

            act.dma_start(x[:, :, :], a["x"].rearrange("b (t p) d -> p (b t) d", p=P)).then_inc(sem("x_loaded"), 16)
            act.dma_start(kc[:, :], a["k_main"]).then_inc(sem("kc_loaded"), 16)

            def rows_of(ap):
                return ap.rearrange("l (r c) -> (l r) c", c=P)

            rows = [(0, rows_of(a["b_ada"]), 96), (96, rows_of(a["b_c_2"]), 24), (120, rows_of(a["c"]), 8)]
            place = CV_C2
            for name, n in (("c_2", 8), ("norm1_g", 16), ("norm2_g", 16), ("g_pre_2", 8), ("od_b_dw", 4),
                            ("od_conv_ln_g", 4), ("od_conv_ln_b", 4), ("conv_b_2", 8), ("b_r_f_2", 8),
                            ("b_i_f_2", 8), ("b_r_b_2", 8), ("b_i_b_2", 8), ("lam_f_2", 8), ("lam_b_2", 8)):
                rows.append((place, rows_of(a[name]), n))
                place += n
            assert place == CV_DW
            for j in range(4):
                rows.append((2 * P + CONV * j, a["od_w_dw"][0, :, j * P:(j + 1) * P], CONV))
                rows.append((3 * P + 8 * j, rows_of(a["conv_w_2"][0])[8 * j:8 * j + 8], 8))
            assert len(rows) == 25
            for r, src, n in rows:
                act.dma_start(stage[r % P:r % P + n, r // P, :], src).then_inc(sem("stage_loaded"), 16)
            act.dma_start(onehot[0:64, :], a["k_onehot"]).then_inc(sem("onehot_loaded"), 16)
            act.wait_ge(sem("rel_ones"), 1)
            act.dma_start(rel_ext[0:32, :], a["rel_bias"]).then_inc(sem("onehot_loaded"), 16)
            act.dma_start(ws_raw[:, :, :], a["ev_w_s"][0].rearrange("g t s -> t g s")).then_inc(sem("ws_loaded"), 16)

            def columns(bank):
                act.copy(cv[:, 0:CV_DW], ps[5][:, 0:CV_DW])
                act.copy(cv[:, CV_DW:CV_DW + 124], ps[5][:, 2 * P:2 * P + 124])
                act.copy(cv[:, CV_CW2:CV_END], ps[5][:, 3 * P:3 * P + 32]).then_inc(sem("cv_ready"), 1)

            act.wait_ge(sem("cv_full"), 1)
            columns(5)
            act.wait_ge(sem("cv_ready"), 1)
            for n, c0 in enumerate((CV_C, CV_C2)):
                ins = act.activation(c_rep[:, n, :, :], bc(cv[:, c0:c0 + KT].unsqueeze(2), [P, KT, 32]), ACT.Silu)
            ins.then_inc(sem("c_ready"), 1)

            step(act.activation(rgt[:, 0:16], cv[:, CV_LF:CV_LF + 16], ACT.Abs))
            step.wait()
            act.activation(rgt[:, 0:16], rgt[:, 0:16], ACT.Exp, scale=-1.0).then_inc(sem("lam_exp_ready"), 1)

            act.wait_ge(sem("bias_full"), 1)
            act.copy(bias_rows[0:8, :], ps[5][0:8, 0:384]).then_inc(sem("bias_rows_ready"), 1)
            act.wait_ge(sem("bias_rows_ready"), 1)
            act.dma_start(bias_dram, bc(bias_rows[0:8, :].unsqueeze(1), [8, P, 384]))\
               .then_inc(sem("bias_rows_sent"), 16)
            act.wait_ge(sem("bias_rows_sent"), 16)
            act.dma_start(bias_a[:, :, :], bass.AP(bias_dram.tensor, P - 1, [[383, P], [384 * P, 8], [1, S]]))\
               .then_inc(sem("bias_a_loaded"), 16)
            act.dma_start(k2[:, :], a["k_early"]).then_inc(sem("k2_loaded"), 16)
            for dst, src in ((lng_bc, a["ev_gmlp_ln_g"]), (lnb_bc, a["ev_gmlp_ln_b"])):
                act.dma_start(dst, src.partition_broadcast(P).rearrange("p l c -> p (l c)"))\
                   .then_inc(sem("gmlp_loaded"), 16)
            act.dma_start(bs_bc[:, :, :], a["ev_b_s"][0].partition_broadcast(P)).then_inc(sem("gmlp_loaded"), 16)

            def load_router(layer):
                with nc.allow_non_contiguous_dma(reason="rows of four logits"):
                    srcs = [a["moe_w_group"][layer]] + [a["moe_w_router"][layer, g] for g in range(4)]
                    for n, src in enumerate(srcs):
                        act.dma_start(rw[:, :, 4 * n:4 * n + 4], src.rearrange("(k p) g -> p k g", p=P))\
                           .then_inc(sem("rw_loaded"), 16)
                act.dma_start(rb[:, 0:4], a["moe_b_group"][layer].partition_broadcast(P))\
                   .then_inc(sem("rw_loaded"), 16)
                act.dma_start(rb[:, 4:20], a["moe_b_router"][layer].rearrange("g e -> (g e)").partition_broadcast(P))\
                   .then_inc(sem("rw_loaded"), 16)

            load_router(0)

            def square(s):
                for t in range(TT):
                    ins = act.activation(xn[:, t, :], x[:, t, :], ACT.Square,
                                         accum_out=small[:, SUMSQ + t:SUMSQ + t + 1])
                ins.then_inc(sem("sumsq_ready"), 1)

            def root(v, ready, done, n=1):
                act.wait_ge(sem(ready), n)
                act.activation(v, v, ACT.Sqrt).then_inc(sem(done), 1)

            def norm_root(s):
                root(small[:, RSTD:RSTD + 2], "ms_ready", "root_ready", s + 1)

            def normalise(s, r):
                norm_root(s)
                act.wait_ge(sem("rstd_ready"), s + 1)
                act.activation(xn[:, 1, :], x[:, 1, :], ACT.Copy, scale=small[:, RSTD + 1:RSTD + 2])\
                   .then_inc(sem("xn_ready_act"), 1)

            def turned(r):
                act.wait_ge(sem("gain_ready"), r + 1)
                sh = (0, 24, 48, 72, 96)[r]
                for b in (0, 2):
                    act.wait_ge(sem("turned"), 4 * r + b + 1)
                    for k in (2 * b, 2 * b + 1):
                        ins = act.activation(hT[:, k, :], ps[b][:, (k % 2) * S:(k % 2 + 1) * S], ACT.Identity,
                                             bias=mod[:, sh + k:sh + k + 1], scale=gs[:, r, 0, k:k + 1])
                ins.then_inc(sem("hT_act"), 1)

            parts = [0]

            def ada_part_copy():
                n = parts[0]
                parts[0] += 1
                act.wait_ge(unit_done, unit_of[f"ada{n}"] + 1)
                act.copy(ada_part[:, :], ps[4][:, :]).then_inc(sem("ada_part_taken"), 1)

            def take(name, b, dst, func=ACT.Copy, scale=1.0):
                src, free = full_at(act, name, b)
                v = src[:, :].rearrange("p (a b) -> p a b", b=dst.shape[2]) if len(dst.shape) == 3 else src[:, :]
                act.activation(dst, v, func, scale=scale).then_inc(free, 1)

            def both(name, dst, func=ACT.Copy, scale=1.0):
                take(name, 0, dst[:, 0:2, :], func, scale)
                take(name, 1, dst[:, 2:4, :], func, scale)

            def tokens(name, dst, func=ACT.Copy):
                for b in range(TT):
                    take(name, b, dst[:, b, :], func)

            head = [0]

            def softmax_exp(kind):
                n = head[0]
                head[0] += 1
                act.wait_ge(sem("max_ready"), softmaxes(n) + 1)
                p = pr[:, n % 2, :]
                width = (S, P) if kind == "dilated" else (S, S)
                for m in range(2):
                    c = NEGMAX + 2 * (n % 2) + m
                    kw = {} if kind == "dilated" else {
                        "accum_out": small[:, DEN + 2 * (n % 2) + m:DEN + 2 * (n % 2) + m + 1]}
                    ins = act.activation(p[:, m * S:m * S + width[m]], p[:, m * S:m * S + width[m]], ACT.Exp,
                                         bias=small[:, c:c + 1], **kw)
                ins.then_inc(sem("exp_ready"), 1)

            def softmaxes(n):
                return n if n < 8 else n - 8

            def softplus_parts():
                n = head[0]
                head[0] += 1
                act.wait_ge(sem("scores_full"), n + 1)
                bank, b = ps[6 + n % 2], n % 2
                act.copy(z_sb[:, b, :], bank[:, 0:384])
                step(act.activation(e_sb[:, b, :], bank[:, 0:384], ACT.Abs))
                step.wait()
                step(act.activation(e_sb[:, b, :], e_sb[:, b, :], ACT.Exp, scale=-1.0))
                step.wait()
                act.activation(e_sb[:, b, :], e_sb[:, b, :], ACT.Ln, bias=1.0).then_inc(sem("log_ready"), 1)

            def stick_exp(n):
                act.wait_ge(sem("stick_arg_ready"), n - 8 + 1)
                act.activation(att_sb[:, n % 2, :], att_sb[:, n % 2, :], ACT.Exp).then_inc(sem("probsT_ready"), 1)

            def turned_probs(n, width):
                act.wait_ge(sem("probsT_full"), n + 1)
                act.copy(prT[:, 0:width], ps[5][:, 0:width]).then_inc(sem("probsT_ready"), 1)

            def head_out(n, h, first):
                act.wait_ge(sem("o_full"), n + 1)
                p0 = 64 * (h % 2)
                act.copy(oT[p0:p0 + 64, first + h // 2, :], ps[6 + n % 2][p0:p0 + 64, 0:S]).then_inc(sem("o_taken"), 1)

            def gate_rows(name, scale=1.0):
                src, free = full_at(act, name, 0)
                act.activation(gate_bc[:, 0:512], src[:, :], ACT.Copy, scale=scale).then_inc(free, 1)

            def experts(layer):
                done = PAIRS * layer
                first = moe_start[layer]
                act.wait_ge(sem("route_max_ready"), 2 * layer + 1)
                act.activation(rt[:, 40:48], rt[:, 40:48], ACT.Exp).then_inc(sem("route_exp_ready"), 1)
                act.wait_ge(sem("route_max_ready"), 2 * layer + 2)
                act.activation(rt[:, 48:50], rt[:, 48:50], ACT.Exp).then_inc(sem("route_exp_ready"), 1)
                sh = (24, 72)[layer]
                for q in range(0, 16, 2):
                    k, half = q // 2, q % 2
                    act.wait_ge(sem("gather_full"), 16 * layer + q + 1)
                    ins = act.activation(xgT[:, 4 * half:4 * half + 4, k, :],
                                         ps[4 + q % 4][:, :].rearrange("p (a b) -> p a b", b=P), ACT.Identity,
                                         bias=mod[:, sh + k:sh + k + 1], scale=gs[:, 2 * layer + 1, 0, k:k + 1])
                    ins.then_inc(gather_taken[0], 1)
                for b in (0, 2):
                    act.wait_ge(sem("gT_full"), 4 * layer + b + 1)
                    act.copy(gT[:, 2 * b:2 * b + 2, :], ps[b][:, :].rearrange("p (a b) -> p a b", b=S))\
                       .then_inc(sem("gT_ready_act"), 1)
                with act.Fori(0, PAIRS) as j:
                    act.wait_ge(unit_done, j * 6 + (first + 2))
                    act.activation(silu_g, ps[4][:, :], ACT.Silu).then_inc(sem("silu_ready"), 1)
                    act.wait_ge(sem("hidT_full"), j + (done + 1))
                    act.copy(hidT[:, :, :], ps[6][:, :].rearrange("p (a b) -> p a b", b=P)).then_inc(sem("hidT_ready"), 1)
                    act.wait_ge(sem("down_full"), j + (done + 1))
                    act.copy(y_pair[:, 0:512], ps[6][:, :]).then_inc(sem("y_pair_act"), 1)

            def overflow(layer):
                act.wait_ge(sem("x_summed"), layer + 1)
                with act.Fori(0, LATE) as j:
                    there = act.value_load(late[0:1, layer, 0, bass.ds(j, 1)], min_val=0, max_val=1)
                    with act.If(there > 0):
                        act.wait_ge(sem(f"o_hid_full{layer}"), j + 1)
                        for b in range(2):
                            ins = act.activation(o_silu[:, 2 * b:2 * b + 2, :],
                                                 ps[b][:, :].rearrange("p (a b) -> p a b", b=S), ACT.Silu)
                        ins.then_inc(sem(f"o_silu_ready{layer}"), 1)

            act.wait_ge(sem("x_loaded"), 16)
            square(0)
            normalise(0, 0)
            for n in range(4):
                ada_part_copy()
            turned(0)

            take("ev0", 0, qT[:, 0:2, :], scale=0.125)
            ada_part_copy()
            take("ev1", 0, kT[:, 0:2, :])
            ada_part_copy()
            take("ev2", 0, v_tok[:, 0, :])
            softmax_exp("dilated")
            for h in range(8):
                if h < 7:
                    softmax_exp("dilated")
                if h == 0:
                    tokens("ev4", gv, ACT.Gelu_apprx_tanh)
                    ada_part_copy()
                elif h == 1:
                    both("ev3", uT, ACT.Gelu_apprx_tanh)
                    ada_part_copy()
                else:
                    ada_part_copy()
                    ada_part_copy()
                if h == 1:
                    root(small[:, MV + 4:MV + 6], "gv_var_ready", "gv_root_ready")
                if h == 5:
                    gate_rows("gateA")
                turned_probs(h, 384)
                head_out(h, h, 0)
            act.wait_ge(sem("x_ready"), 1)
            square(1)
            normalise(1, 1)
            turned(1)
            gate_rows("gateB")
            experts(0)
            act.wait_ge(sem("rb_used"), 1)
            load_router(1)
            overflow(0)

            act.wait_ge(sem("x_ready"), 2)
            square(2)
            normalise(2, 2)
            turned(2)
            both("od0", aT)
            both("od1", glT, ACT.Tanh, 0.5)
            both("od2", qT, scale=0.125)
            both("od3", kT)
            tokens("od4", v_tok)
            softplus_parts()
            for h in range(8):
                if h < 7:
                    softplus_parts()
                if h == 4:
                    act.wait_ge(sem("centred"), 1)
                    act.activation(csq[:, :, :], cacc[:, :, :], ACT.Square).then_inc(sem("csq_ready"), 1)
                ada_part_copy()
                if h == 4:
                    root(crs, "cvar_ready", "croot_ready")
                if h == 6:
                    gate_rows("gateC")
                stick_exp(8 + h)
                head_out(8 + h, h, 4)
            act.wait_ge(sem("conv_normed"), 1)
            for ct in range(4):
                ins = act.activation(oT[:, ct, :], cacc[:, ct, :], ACT.Silu,
                                     bias=cv[:, CV_LNB + ct:CV_LNB + ct + 1], scale=cv[:, CV_LNG + ct:CV_LNG + ct + 1])
            ins.then_inc(sem("o_c_ready"), 1)
            ada_part_copy()
            ada_part_copy()
            act.wait_ge(sem("x_ready"), 3)
            square(3)
            normalise(3, 3)
            turned(3)
            gate_rows("gateD")
            act.dma_start(fn_bc, a["final_norm_g"].partition_broadcast(P)).then_inc(sem("fn_loaded"), 16)
            experts(1)
            overflow(1)

            act.wait_ge(sem("x_ready"), 4)
            square(4)
            norm_root(4)
            act.wait_ge(sem("x_ready"), 5)
            square(5)
            normalise(5, 4)
            turned(4)
            for i, name in enumerate(("in0", "in1")):
                for b in range(2):
                    c = 4 * i + 2 * b
                    take(name, b, xa_raw[:, c:c + 2, 2:2 + S])
            both("in4", qT, scale=0.125)
            both("in6", kT)
            tokens("in8", v_tok)

            def half_tanh(name, dst, signal=None):
                for b in range(2):
                    if signal is None:
                        take(name, b, dst[:, 2 * b:2 * b + 2, :], ACT.Tanh, 0.5)
                        continue
                    src, _ = full_at(act, name, b)
                    act.activation(dst[:, 2 * b:2 * b + 2, :], src[:, :].rearrange("p (a b) -> p a b", b=S),
                                   ACT.Tanh, scale=0.5).then_inc(sem(signal), 1)

            def recurrence(ct, way):
                n = 2 * ct + way
                act.wait_ge(sem("rg_gates_full"), n + 1)
                if ct:
                    act.wait_ge(sem("rg_u_ready"), n - 1)
                t, t_i = rg_t[way], rg_ti[way]
                hr, hi = 16 + 16 * way + ct, 24 + 16 * way + ct
                step(act.activation(t, ps[4][:, 0:S], ACT.Tanh, scale=0.5, bias=rgc[:, hr:hr + 1]))
                act.activation(t_i, ps[4][:, S:2 * S], ACT.Tanh, scale=0.5, bias=rgc[:, hi:hi + 1])\
                   .then_inc(sem("rg_gates_taken"), 1)
                step.wait()
                c = 8 * way + ct
                step(act.activation(t, t, ACT.Tanh, scale=rgc[:, c:c + 1], bias=rgc[:, c:c + 1]))

            def recurrence_roots():
                step.wait()
                for way in range(2):
                    act.activation(rg_root[way], rg_t[way], ACT.Sqrt).then_inc(sem("rg_root_ready"), 1)

            def near(h, between):
                if h % 8 != 7:
                    softmax_exp("near")
                between(h)
                turned_probs(8 + 8 + h, 512)
                head_out(8 + 8 + h, h, 0)

            def between_c(h):
                recurrence(h, 0)
                if h in (0, 1):
                    half_tanh(f"in{2 + h}", yaT[:, 4 * h:4 * h + 4, :], "z_tanh")
                if h in (3, 5):
                    i = (h - 3) // 2
                    half_tanh(f"in{10 + i}", zbT[:, 4 * i:4 * i + 4, :], "z_tanh")

            act.wait_ge(sem("rgc_ready"), 1)
            softmax_exp("near")
            for h in range(8):
                near(h, between_c)
                recurrence(h, 1)
                recurrence_roots()
            both("in5", qT, scale=0.125)
            both("in7", kT)
            tokens("in9", v_tok)

            def between_d(h):
                if h in (8, 10):
                    i = (h - 8) // 2
                    half_tanh(f"in{12 + i}", gaT[:, 4 * i:4 * i + 4, :])

            softmax_exp("near")
            for h in range(8, 16):
                near(h, between_d)
            act.wait_ge(sem("ya_ready"), KT)
            half_tanh("in14", gbT[:, 0:4, :])
            half_tanh("in15", gbT[:, 4:8, :])
            gate_rows("gateE", 0.5)
            act.dma_start(gf_bc, a["g_final_2"].partition_broadcast(P)).then_inc(sem("gf_loaded"), 16)
            act.wait_ge(sem("x_ready"), 6)
            square(6)
            norm_root(6)
            act.wait_ge(sem("rstd_ready"), 7)
            act.activation(x[:, 1, :], x[:, 1, :], ACT.Copy, scale=small[:, RSTD + 1:RSTD + 2])\
               .then_inc(sem("x_scaled_act"), 1)

        @block.vector
        def _(dve):
            step = Steps(dve, "dve_steps")

            def stt(out_, in0, scalar, in1, op0, op1):
                return dve.scalar_tensor_tensor(out_, in0, scalar, in1, op0, op1)

            def ttr(out_, in0, in1, op0, op1, start, acc):
                return dve.tensor_tensor_reduce(out_, in0, in1, 1.0, start, op0, op1, acc)

            def rstd(s):
                dve.wait_ge(sem("sumsq_ready"), s + 1)
                dve.tensor_scalar(small[:, RSTD:RSTD + 2], small[:, SUMSQ:SUMSQ + 2], 1.0 / D, EPS,
                                  ALU.mult, ALU.add).then_inc(sem("ms_ready"), 1)
                dve.wait_ge(sem("root_ready"), s + 1)
                dve.reciprocal(small[:, RSTD:RSTD + 2], small[:, RSTD:RSTD + 2]).then_inc(sem("rstd_ready"), 1)
                dve.wait_ge(sem("rstd_ready"), s + 1)

            def normalise(s):
                rstd(s)
                dve.tensor_scalar(xn[:, 0, :], x[:, 0, :], small[:, RSTD:RSTD + 1], None, ALU.mult)\
                   .then_inc(sem("xn_ready_dve"), 1)

            def gain(r):
                sc = (8, 32, 56, 80, 104)[r]
                g = (CV_N1, CV_N2, CV_N1 + 8, CV_N2 + 8, CV_GPRE)[r]
                dve.wait_ge(sem("ada_ready"), (4, 10, 16, 22, 28)[r])
                stt(gs[:, r, 0, :], mod[:, sc:sc + 8], 1.0, cv[:, g:g + 8], ALU.add, ALU.mult)\
                   .then_inc(sem("gain_ready"), 1)

            def turned(r):
                dve.wait_ge(sem("gain_ready"), r + 1)
                sh = (0, 24, 48, 72, 96)[r]
                for b in (1, 3):
                    dve.wait_ge(sem("turned"), 4 * r + b + 1)
                    for k in (2 * b, 2 * b + 1):
                        ins = dve.tensor_scalar(hT[:, k, :], ps[b][:, (k % 2) * S:(k % 2 + 1) * S],
                                                gs[:, r, 0, k:k + 1], mod[:, sh + k:sh + k + 1], ALU.mult, ALU.add)
                ins.then_inc(sem("hT_dve"), 1)

            cols = [0]

            def ada_cols():
                n = cols[0]
                cols[0] += 1
                dve.wait_ge(sem("ada_cols_full"), n + 1)
                stt(mod[:, 4 * n:4 * n + 4], ps[4][:, 0:4], 1.0 / 32, cv[:, 4 * n:4 * n + 4], ALU.mult, ALU.add)\
                   .then_inc(sem("ada_ready"), 1)

            def take(name, b, dst, scale=1.0):
                src, free = full_at(dve, name, b)
                v = src[:, :].rearrange("p (a b) -> p a b", b=dst.shape[2]) if len(dst.shape) == 3 else src[:, :]
                dve.tensor_scalar(dst, v, scale, None, ALU.mult).then_inc(free, 1)

            def diagonals(name):
                n = "ABCDE".index(name[-1])
                c0 = (16, 40, 64, 88, 112)[n]
                dve.wait_ge(sem("ada_ready"), (6, 12, 18, 24, 30)[n])
                for k in range(KT):
                    ins = dve.tensor_scalar(gate_bc[:, k * P:(k + 1) * P], ident, mod[:, c0 + k:c0 + k + 1], None,
                                            ALU.mult)
                ins.then_inc(sem("diag_ready"), 1)

            def gate_rows(name, scale=1.0):
                src, free = full_at(dve, name, 1)
                dve.tensor_scalar(gate_bc[:, 512:1024], src[:, :], scale, None, ALU.mult).then_inc(free, 1)

            def add_mixed(names, tmp):
                for half, name in enumerate(names):
                    cols_ = slice(half * 512, half * 512 + 512)
                    for b in range(TT):
                        src, free = full_at(dve, name, b)
                        dve.tensor_tensor(tmp[b], src[:, :], gate_bc[:, cols_], ALU.mult).then_inc(free, 1)
                    for b in range(TT):
                        n = dense[name]
                        dve.wait_ge(bank_free[2 * (n % 2) + b], n // 2 + 1)
                        ins = dve.tensor_tensor(x[:, b, cols_], x[:, b, cols_], tmp[b], ALU.add)
                        if half == 0:
                            step(ins)
                    if half == 0:
                        step.wait()
                ins.then_inc(sem("x_ready"), 1)

            head = [0]

            def softmaxes(n):
                return n if n < 8 else n - 8

            def score_max(kind):
                n = head[0]
                h = n if kind == "dilated" else n - 16
                dve.wait_ge(sem("scores_full"), n + 1)
                bank, p = ps[6 + n % 2], pr[:, n % 2, :]
                c = NEGMAX + 2 * (n % 2)
                if kind == "dilated":
                    both = ((slice(0, S), bias_a[:, h, :]), (slice(S, S + P), bias_a[:, h, P:S]))
                else:
                    nb = bias_n[:, (h // 2) % 2, h % 2, :]
                    both = ((slice(0, S), nb[:, 2 * GRID:2 * GRID + S]), (slice(S, 2 * S), nb[:, 0:S]))
                for m, (cut, bias) in enumerate(both):
                    step(ttr(p[:, cut], bank[:, cut], bias, ALU.add, ALU.max, -3e38, small[:, c + m:c + m + 1]))
                step.wait()
                dve.tensor_scalar(small[:, c:c + 2], small[:, c:c + 2], -1.0, None, ALU.mult)\
                   .then_inc(sem("max_ready"), 1)

            def score_probs(kind):
                n = head[0]
                head[0] += 1
                dve.wait_ge(sem("exp_ready"), softmaxes(n) + 1)
                p, d, r = pr[:, n % 2, :], DEN + 2 * (n % 2), RDEN + 2 * (n % 2)
                cuts = (slice(0, S), slice(S, S + P) if kind == "dilated" else slice(S, 2 * S))
                if kind == "dilated":
                    many = (k2[:, K2_MULT:K2_MULT + S], k2[:, K2_MULT + P:K2_MULT + S])
                    for m in range(2):
                        step(ttr(p[:, cuts[m]], p[:, cuts[m]], many[m], ALU.mult, ALU.add, 0.0,
                                 small[:, d + m:d + m + 1]))
                    step.wait()
                step(dve.reciprocal(small[:, r:r + 2], small[:, d:d + 2]))
                step.wait()
                for m in range(2):
                    ins = dve.tensor_scalar(p[:, cuts[m]], p[:, cuts[m]], small[:, r + m:r + m + 1], None, ALU.mult)
                ins.then_inc(sem("probs_ready"), 1)

            def diag_blocks(t):
                return bass.AP(t.tensor, t.offset, [list(t.ap[0]), [S, 2], [1, P]])

            def softplus():
                n = head[0]
                head[0] += 1
                b = n % 2
                dve.wait_ge(sem("log_ready"), n - 8 + 1)
                step(stt(sp_sb[:, b, :], z_sb[:, b, :], 0.0, e_sb[:, b, :], ALU.max, ALU.add))
                step.wait()
                v = diag_blocks(sp_sb[:, b, :])
                dve.tensor_tensor(v, v, bc(lt.unsqueeze(1), [P, 2, P]), ALU.mult).then_inc(sem("probs_ready"), 1)

            def stick_arg(n):
                b = n % 2
                dve.wait_ge(sem("probsT_full"), n + 1)
                step(dve.tensor_tensor(att_sb[:, b, :], z_sb[:, b, :], ps[5][:, 0:384], ALU.subtract))
                step.wait()
                v = diag_blocks(att_sb[:, b, :])
                dve.tensor_tensor(v, v, bc(neg_diag.unsqueeze(1), [P, 2, P]), ALU.add)\
                   .then_inc(sem("stick_arg_ready"), 1)

            def first_max(vals, width, at_, out_):
                m = rt[:, at_:at_ + 2]
                step(dve.tensor_reduce(m, vals, AX, ALU.max))
                step.wait()
                eq = rt[:, at_ + 2:at_ + 10].rearrange("p (t e) -> p t e", e=4)
                step(dve.tensor_tensor(eq, vals, bc(m.unsqueeze(2), [P, TT, 4]), ALU.is_equal))
                step.wait()
                step(dve.tensor_tensor(eq, eq, bc(kc[:, K_W:K_W + 4].unsqueeze(1), [P, TT, 4]), ALU.mult))
                step.wait()
                km = rt[:, at_ + 10:at_ + 12]
                step(dve.tensor_reduce(km, eq, AX, ALU.max))
                step.wait()
                step(dve.tensor_tensor(out_, eq, bc(km.unsqueeze(2), [P, TT, 4]), ALU.is_equal))
                step.wait()
                return m

            def late_list(layer):
                left, has, place = rt[:, 612:628], rt[:, 628:644], rt[:, 644:660]
                step(dve.tensor_reduce(left, ps[4][:, 0:32].rearrange("p (t e) -> p e t", e=EXPERTS), AX, ALU.add))
                step.wait()
                step(dve.tensor_scalar(has, left, 1.0, None, ALU.min))
                step.wait()
                step(dve.tensor_tensor_scan(place, ones[:, 0:EXPERTS], has, 0.0, ALU.mult, ALU.add))
                step.wait()
                step(dve.tensor_tensor(place, place, has, ALU.mult))
                step.wait()
                n = [P, EXPERTS, EXPERTS]
                at_place = rt[:, 660:660 + EXPERTS * EXPERTS].rearrange("p (j e) -> p j e", e=EXPERTS)
                count = kc[:, K_IOTA:K_IOTA + EXPERTS]
                step(dve.tensor_tensor(at_place, bc(place.unsqueeze(1), n), bc(count.unsqueeze(2), n), ALU.is_equal))
                step.wait()
                step(dve.tensor_reduce(has, at_place, AX, ALU.add))
                step.wait()
                step(stt(at_place, bc(count.unsqueeze(1), n), -1.0, at_place, ALU.add, ALU.mult))
                step.wait()
                step(dve.tensor_reduce(left, at_place, AX, ALU.add))
                step.wait()
                step(dve.tensor_copy(late[:, layer, 0, :], has))
                dve.tensor_copy(late[:, layer, 1, :], left).then_inc(sem("late_ready"), 1)

            def route(layer):
                lg = rt[:, 0:40].rearrange("p (t c) -> p t c", c=20)
                dve.wait_ge(sem("logits_full"), layer + 1)
                dve.wait_ge(sem("rw_loaded"), 16 * 7 * (layer + 1))
                ins = dve.tensor_tensor(lg, ps[4][:, 0:40].rearrange("p (t c) -> p t c", c=20),
                                        bc(rb[:, :].unsqueeze(1), [P, TT, 20]), ALU.add)
                ins.then_inc(sem("rb_used"), 1)
                dve.wait_ge(sem("rb_used"), layer + 1)
                t4 = [P, TT, 4]

                def tile4(at_):
                    return rt[:, at_:at_ + 8].rearrange("p (t e) -> p t e", e=4)

                group = tile4(100)
                gm = first_max(lg[:, :, 0:4], 4, 110, group)
                ex = tile4(40)
                dve.tensor_tensor(ex, lg[:, :, 0:4], bc(gm.unsqueeze(2), t4), ALU.subtract)\
                   .then_inc(sem("route_max_ready"), 1)
                by_group = rt[:, 130:162].rearrange("p (t e g) -> p t e g", e=4, g=4)
                for t in range(TT):
                    step(dve.tensor_tensor(by_group[:, t], lg[:, t, 4:20].rearrange("p (g e) -> p e g", e=4),
                                           bc(group[:, t, :].unsqueeze(1), [P, 4, 4]), ALU.mult))
                step.wait()
                own = tile4(170)
                step(dve.tensor_reduce(own, by_group, AX, ALU.add))
                step.wait()
                one, two, rest = tile4(180), tile4(190), tile4(200)
                m1 = first_max(own, 4, 210, one)
                step(stt(rest, one, NEG, own, ALU.mult, ALU.add))
                step.wait()
                m2 = first_max(rest, 4, 230, two)
                e2 = rt[:, 48:50]
                dve.tensor_tensor(e2, m2, m1, ALU.subtract).then_inc(sem("route_max_ready"), 1)
                dve.wait_ge(sem("route_exp_ready"), 2 * layer + 2)
                gw, w1, w2 = rt[:, 250:252], rt[:, 252:254], rt[:, 254:256]
                step(dve.tensor_reduce(gw, ex, AX, ALU.add))
                step(dve.tensor_scalar(w1, e2, 1.0, None, ALU.add))
                step.wait()
                step(dve.tensor_tensor(w1, w1, gw, ALU.mult))
                step.wait()
                step(dve.reciprocal(w1, w1))
                step.wait()
                step(dve.tensor_tensor(w2, w1, e2, ALU.mult))
                step.wait()
                g1, g2, both = tile4(260), tile4(270), tile4(280)
                step(dve.tensor_tensor(g1, one, bc(w1.unsqueeze(2), t4), ALU.mult))
                step(dve.tensor_tensor(g2, two, bc(w2.unsqueeze(2), t4), ALU.mult))
                step(dve.tensor_tensor(both, one, two, ALU.add))
                step.wait()
                step(dve.tensor_tensor(g1, g1, g2, ALU.add))
                step.wait()
                mask = rt[:, 512:544].rearrange("p (t e) -> p t e", e=EXPERTS)
                for t in range(TT):
                    for dst, src in ((gates, g1), (mask, both)):
                        step(dve.tensor_tensor(dst[:, t, :].rearrange("p (g e) -> p g e", e=4),
                                               bc(group[:, t, :].unsqueeze(2), [P, 4, 4]),
                                               bc(src[:, t, :].unsqueeze(1), [P, 4, 4]), ALU.mult))
                step.wait()
                dve.tensor_copy(rt[:, 610:611], rt[:, 512:513]).then_inc(sem("mask_ready"), 1)
                key = rt[:, 544:576]
                dve.wait_ge(sem("rank_full"), layer + 1)
                step(stt(key, ps[5][:, 0:32], 1.0, rt[:, 512:544], ALU.add, ALU.mult))
                step.wait()
                flat = gates[:, :, :].rearrange("p t e -> p (t e)")
                step(stt(gates_over[:, :, :].rearrange("p t e -> p (t e)"), key, CAP, flat, ALU.is_gt, ALU.mult))
                dve.tensor_scalar(rt[:, 576:608], key, CAP, None, ALU.is_gt).then_inc(sem("over_ready"), 1)
                dve.wait_ge(sem("over_full"), layer + 1)
                late_list(layer)
                pick_f = pick[:, :, :, :].rearrange("p t e s -> p (t e) s")
                pick_gf = pick_g[:, :, :, :].rearrange("p t e s -> p (t e) s")
                wide = [P, TT * EXPERTS, SLOTS]
                dve.tensor_tensor(pick_f, bc(key.unsqueeze(2), wide),
                                  bc(kc[:, K_IOTA:K_IOTA + SLOTS].unsqueeze(1), wide), ALU.is_equal)\
                   .then_inc(sem("pick_ready"), 1)
                dve.wait_ge(sem("pick_ready"), layer + 1)
                dve.tensor_tensor(pick_gf, pick_f, bc(flat.unsqueeze(2), wide), ALU.mult)\
                   .then_inc(sem("pick_g_ready"), 1)

            def experts(layer):
                done, first = PAIRS * layer, moe_start[layer]
                sh = (24, 72)[layer]
                route(layer)
                for q in range(1, 16, 2):
                    k, half = q // 2, q % 2
                    dve.wait_ge(sem("gather_full"), 16 * layer + q + 1)
                    dve.tensor_scalar(xgT[:, 4 * half:4 * half + 4, k, :],
                                      ps[4 + q % 4][:, :].rearrange("p (a b) -> p a b", b=P),
                                      gs[:, 2 * layer + 1, 0, k:k + 1], mod[:, sh + k:sh + k + 1],
                                      ALU.mult, ALU.add).then_inc(gather_taken[1], 1)
                for b in (1, 3):
                    dve.wait_ge(sem("gT_full"), 4 * layer + b + 1)
                    dve.tensor_copy(gT[:, 2 * b:2 * b + 2, :], ps[b][:, :].rearrange("p (a b) -> p a b", b=S))\
                       .then_inc(sem("gT_ready_dve"), 1)
                dve.memset(hidT[:, 0:2, :], 0.0).then_inc(sem("zeros_ready"), 1)
                with dve.Fori(0, PAIRS) as j:
                    dve.wait_ge(unit_done, j * 6 + (first + 4))
                    dve.wait_ge(sem("silu_ready"), j + (done + 1))
                    dve.tensor_tensor(hid, silu_g, ps[5][:, :], ALU.mult).then_inc(sem("hid_ready"), 1)
                    dve.wait_ge(unit_done, j * 6 + (first + 6))
                    dve.tensor_copy(y_pair[:, 512:1024], ps[7][:, :]).then_inc(sem("y_pair_dve"), 1)
                dve.wait_ge(sem("scattered"), PAIRS * (layer + 1))
                for half in range(2):
                    tmp = (silu_g, hid)
                    for t in range(TT):
                        step(dve.tensor_tensor(tmp[t], ps[2 * t + half][:, :], gate_bc[:, half * 512:half * 512 + 512],
                                               ALU.mult))
                    step.wait()
                    for t in range(TT):
                        xv = x[:, t, half * 512:half * 512 + 512]
                        ins = dve.tensor_tensor(xv, xv, tmp[t], ALU.add)
                        if half == 0 or t == 0:
                            step(ins)
                    if half == 0:
                        step.wait()
                ins.then_inc(sem("x_summed"), 1)

            def overflow(layer):
                dve.wait_ge(sem("x_summed"), layer + 1)
                with dve.Fori(0, LATE) as j:
                    there = dve.value_load(late[0:1, layer, 0, bass.ds(j, 1)], min_val=0, max_val=1)
                    with dve.If(there > 0):
                        dve.wait_ge(sem(f"o_silu_ready{layer}"), j + 1)
                        for b in range(2):
                            ins = dve.tensor_tensor(o_hidT[:, 2 * b:2 * b + 2, :], o_silu[:, 2 * b:2 * b + 2, :],
                                                    ps[2 + b][:, :].rearrange("p (a b) -> p a b", b=S), ALU.mult)
                        ins.then_inc(sem(f"o_hid_ready{layer}"), 1)
                        expert = dve.value_load(late[0:1, layer, 1, bass.ds(j, 1)], min_val=0, max_val=EXPERTS - 1)
                        for t in range(TT):
                            dve.tensor_copy(small[:, 50 + t:51 + t], gates_over[:, t, bass.ds(expert, 1)])\
                               .then_inc(sem(f"o_steps{layer}"), 1)
                        dve.wait_ge(sem(f"o_steps{layer}"), j * 10 + TT)
                        dve.wait_ge(sem(f"o_y_full{layer}"), j + 1)
                        n = TT
                        for t in range(TT):
                            for half in range(2):
                                cut = slice(half * 512, half * 512 + 512)
                                stt(ada_part[:, :], ps[4 + 2 * t + half][:, :], small[:, 50 + t:51 + t],
                                    gate_bc[:, cut], ALU.mult, ALU.mult).then_inc(sem(f"o_steps{layer}"), 1)
                                dve.wait_ge(sem(f"o_steps{layer}"), j * 10 + (n + 1))
                                ins = dve.tensor_tensor(x[:, t, cut], x[:, t, cut], ada_part[:, :], ALU.add)
                                n += 2
                                if n < 8 + TT:
                                    ins.then_inc(sem(f"o_steps{layer}"), 1)
                                    dve.wait_ge(sem(f"o_steps{layer}"), j * 10 + n)
                        ins.then_inc(sem(f"o_y_taken{layer}"), 1)
                        dve.wait_ge(sem(f"o_y_taken{layer}"), j + 1)
                        dve.memset(small[:, 60:61], 0.0).then_inc(sem(f"o_steps{layer}"), 1)
                dve.tensor_copy(small[:, 52:53], small[:, RSTD:RSTD + 1]).then_inc(sem("x_ready"), 1)

            dve.memset(rel_ext[0:32, :], 0.0)
            dve.memset(rel_ext[32:64, :], 1.0).then_inc(sem("rel_ones"), 1)
            dve.wait_ge(sem("x_loaded"), 16)
            normalise(0)
            dve.wait_ge(sem("cv_ready"), 1)
            for n in range(4):
                ada_cols()
            gain(0)
            turned(0)
            dve.wait_ge(sem("ws_full"), 1)
            dve.wait_ge(sem("k2_loaded"), 16)
            dve.tensor_tensor(wsT[:, :, :], ps[6][:, :].rearrange("p (a b) -> p a b", b=P),
                              bc(k2[:, K2_LE:K2_LE + P].unsqueeze(1), [P, 4, P]), ALU.mult)\
               .then_inc(sem("wsT_ready"), 1)

            e, s_, s2 = rgt[:, 0:16], rgt[:, 16:32], rgt[:, 32:48]
            two_sp = rgc[:, 0:16]
            dve.wait_ge(sem("lam_exp_ready"), 1)
            step(dve.tensor_scalar(s_, e, 2.0, None, ALU.add))
            step.wait()
            step(dve.reciprocal(s_, s_))
            step.wait()
            step(dve.tensor_tensor(s_, s_, e, ALU.mult))
            step.wait()
            step(dve.tensor_tensor(s2, s_, s_, ALU.mult))
            step.wait()
            step(dve.tensor_scalar(two_sp, s2, 1.0 / 17, 1.0 / 15, ALU.mult, ALU.add))
            for k in range(13, 0, -2):
                step.wait()
                step(dve.tensor_tensor(two_sp, two_sp, s2, ALU.mult))
                step.wait()
                step(dve.tensor_scalar(two_sp, two_sp, 1.0 / k, None, ALU.add))
            step.wait()
            step(stt(two_sp, two_sp, 4.0, s_, ALU.mult, ALU.mult))
            step(dve.tensor_scalar(e, cv[:, CV_LF:CV_LF + 16], -2.0, 0.0, ALU.mult, ALU.max))
            step.wait()
            step(dve.tensor_tensor(two_sp, two_sp, e, ALU.add))
            dve.tensor_scalar(rgc[:, 16:48], cv[:, CV_RF:CV_RF + 32], 0.5, None, ALU.mult)\
               .then_inc(sem("rgc_ready"), 1)

            take("ev0", 1, qT[:, 2:4, :], 0.125)
            ada_cols()
            take("ev1", 1, kT[:, 2:4, :])
            ada_cols()
            take("ev2", 1, v_tok[:, 1, :])
            dve.wait_ge(sem("bias_a_loaded"), 16)
            score_max("dilated")
            score_probs("dilated")
            for h in range(8):
                if h < 7:
                    score_max("dilated")
                    score_probs("dilated")
                ada_cols()
                if h >= 2:
                    ada_cols()
                if h == 1:
                    dve.wait_ge(sem("gmlp_loaded"), 48)
                    taken(dve, "ev4")
                    mv = small[:, MV:MV + 4]
                    for t in range(TT):
                        step(dve.bn_stats(small[:, BN + 6 * t:BN + 6 * t + 6], gv[:, t, :]))
                    step.wait()
                    for t in range(TT):
                        step(dve.bn_aggr(mv[:, 2 * t:2 * t + 2], small[:, BN + 6 * t:BN + 6 * t + 6]))
                    step.wait()
                    rs = small[:, MV + 4:MV + 6]
                    dve.tensor_scalar(rs, mv.rearrange("p (t c) -> p t c", c=2)[:, :, 1], EPS, None, ALU.add)\
                       .then_inc(sem("gv_var_ready"), 1)
                    dve.wait_ge(sem("gv_root_ready"), 1)
                    step(dve.reciprocal(rs, rs))
                    step.wait()
                    for t in range(TT):
                        step(dve.tensor_scalar(gv[:, t, :], gv[:, t, :], mv[:, 2 * t:2 * t + 1], rs[:, t:t + 1],
                                               ALU.subtract, ALU.mult))
                    step.wait()
                    step(dve.tensor_tensor(gv[:, :, :], gv[:, :, :], bc(lng_bc.unsqueeze(1), [P, TT, HW]), ALU.mult))
                    step.wait()
                    dve.tensor_tensor(gv[:, :, :], gv[:, :, :], bc(lnb_bc.unsqueeze(1), [P, TT, HW]), ALU.add)\
                       .then_inc(sem("gv_ready"), 1)
                if h == 3:
                    taken(dve, "ev3")
                    for b in range(2):
                        src, free = full_at(dve, "mixA", b)
                        o = oT[:, 4 + 2 * b:6 + 2 * b, :]
                        for g in range(2):
                            ins = dve.tensor_tensor(o[:, g, :].rearrange("p (t c) -> p t c", c=P),
                                                    src[:, g * S:(g + 1) * S].rearrange("p (t c) -> p t c", c=P),
                                                    bc(bs_bc[:, 2 * b + g, :].unsqueeze(1), [P, TT, P]), ALU.add)
                            if g == 0:
                                step(ins)
                        ins.then_inc(free, 1)
                        step.wait()
                        n = dense["mixA"]
                        dve.wait_ge(bank_free[2 * (n % 2) + b], n // 2 + 1)
                        ins = dve.tensor_tensor(o, o, uT[:, 2 * b:2 * b + 2, :], ALU.mult)
                        if b == 0:
                            step(ins)
                    ins.then_inc(sem("o_b_ready"), 1)
                    diagonals("gateA")
                if h == 5:
                    gate_rows("gateA")
            dve.wait_ge(sem("rpb_sent"), 16)
            taken(dve, "gateA")
            add_mixed(("evo0", "evo1"), (pr[:, 0, :], pr[:, 1, :]))
            gain(1)
            normalise(1)
            diagonals("gateB")
            turned(1)
            gate_rows("gateB")
            taken(dve, "gateB")
            experts(0)
            overflow(0)

            normalise(2)
            gain(2)
            turned(2)
            dve.memset(hcT[:, :, 0:PAD], 0.0)
            step(dve.tensor_scalar(cv[:, CV_DW:CV_DW + 124], cv[:, CV_DW:CV_DW + 124], 0.5, None, ALU.mult))
            taken(dve, "od0")
            taken(dve, "od1")
            step(stt(hcT[:, :, PAD:PAD + S], glT[:, :, :], 1.0, aT[:, :, :], ALU.add, ALU.mult))
            step.wait()
            for two in (0, 2):
                for j in range(CONV):
                    for ct in (two, two + 1):
                        w = cv[:, CV_DW + CONV * ct + j:CV_DW + CONV * ct + j + 1]
                        if j == 0:
                            ins = dve.tensor_scalar(cacc[:, ct, :], hcT[:, ct, 0:S], w,
                                                    cv[:, CV_BDW + ct:CV_BDW + ct + 1], ALU.mult, ALU.add)
                        else:
                            dve.wait_ge(step.sem, step.n - 1)
                            ins = stt(cacc[:, ct, :], hcT[:, ct, j:j + S], w, cacc[:, ct, :], ALU.mult, ALU.add)
                        step(ins)
            step.wait()
            dve.tensor_copy(small[:, 53:54], small[:, 52:53]).then_inc(sem("conv_ready"), 1)

            softplus()
            for h in range(8):
                if h < 7:
                    softplus()
                if h == 2:
                    dve.wait_ge(sem("mean_full"), 1)
                    stt(cacc[:, :, :], bc(ps[2][:, 0:S].unsqueeze(1), [P, 4, S]), -1.0 / HW, cacc[:, :, :],
                        ALU.mult, ALU.add).then_inc(sem("centred"), 1)
                if h == 4:
                    dve.wait_ge(sem("var_full"), 1)
                    dve.tensor_scalar(crs, ps[2][:, S:2 * S], 1.0 / HW, EPS, ALU.mult, ALU.add)\
                       .then_inc(sem("cvar_ready"), 1)
                    dve.wait_ge(sem("croot_ready"), 1)
                    dve.reciprocal(crs, crs).then_inc(sem("crs_ready"), 1)
                    dve.wait_ge(sem("crs_ready"), 1)
                    dve.tensor_tensor(cacc[:, :, :], cacc[:, :, :], bc(crs.unsqueeze(1), [P, 4, S]), ALU.mult)\
                       .then_inc(sem("conv_normed"), 1)
                ada_cols()
                if h == 5:
                    diagonals("gateC")
                if h == 6:
                    gate_rows("gateC")
                stick_arg(8 + h)
            ada_cols()
            ada_cols()
            taken(dve, "gateC")
            add_mixed(("odo0", "odo1"), (pr[:, 0, :], pr[:, 1, :]))
            gain(3)
            normalise(3)
            diagonals("gateD")
            turned(3)
            gate_rows("gateD")
            taken(dve, "gateD")
            experts(1)
            overflow(1)

            rstd(4)
            dve.wait_ge(sem("fn_loaded"), 16)
            for t in range(TT):
                ins = stt(x[:, t, :], x[:, t, :], small[:, RSTD + t:RSTD + t + 1], fn_bc, ALU.mult, ALU.mult)
                if t == 0:
                    step(ins)
            ins.then_inc(sem("x_ready"), 1)
            normalise(5)
            gain(4)
            turned(4)
            dve.memset(xa_raw[:, :, 0:2], 0.0)
            step(dve.memset(xa_raw[:, :, 2 + S:3 + S], 0.0))
            taken(dve, "in0")
            taken(dve, "in1")
            step.wait()
            for j in range(4):
                for ct in range(KT):
                    w = cv[:, CV_CW2 + 8 * j + ct:CV_CW2 + 8 * j + ct + 1]
                    if j == 0:
                        ins = dve.tensor_scalar(xc[:, ct, :], xa_raw[:, ct, 0:S], w,
                                                cv[:, CV_CB2 + ct:CV_CB2 + ct + 1], ALU.mult, ALU.add)
                    else:
                        if ct == 0:
                            step.wait()
                        ins = stt(xc[:, ct, :], xa_raw[:, ct, j:j + S], w, xc[:, ct, :], ALU.mult, ALU.add)
                    if j < 3 or ct < KT - 1:
                        step(ins)
            ins.then_inc(sem("xc_ready"), 1)

            def silu(name, b, dst, n):
                src, free = full_at(dve, name, b)
                dve.wait_ge(sem("z_tanh"), n + 1)
                stt(dst, dst, 1.0, src[:, :].rearrange("p (a b) -> p a b", b=S), ALU.add, ALU.mult).then_inc(free, 1)

            def recurrence(ct, way):
                n = 2 * ct + way
                t, t_i, root, u, h_f, h_b, inv, dec = (rg_t[way], rg_ti[way], rg_root[way], rg_u, rg_hf, rg_hb,
                                                       rg_inv, rg_dec)
                dve.wait_ge(sem("rg_root_ready"), n + 1)
                step(dve.tensor_scalar(inv, t, 1.0, None, ALU.add))
                step.wait()
                step(dve.reciprocal(inv, inv))
                step(stt(t_i, t_i, 1.0, xc[:, ct, :], ALU.add, ALU.mult))
                step.wait()
                step(dve.tensor_scalar(dec, inv, 2.0, -1.0, ALU.mult, ALU.add))
                step(dve.tensor_tensor(root, root, inv, ALU.mult))
                step.wait()
                dve.tensor_tensor(u, root, t_i, ALU.mult).then_inc(sem("rg_u_ready"), 1)
                dve.wait_ge(sem("rg_u_ready"), n + 1)

                def way_of(v):
                    if way == 0:
                        return v
                    return bass.AP(v.tensor, v.offset + S - 1, [list(v.ap[0]), [-1, S]])

                step(dve.tensor_tensor_scan(way_of(h_b if way else h_f), way_of(dec), way_of(u), 0.0,
                                            ALU.mult, ALU.add))
                step.wait()
                if way:
                    taken(dve, "in2" if ct < 4 else "in3")
                    step(dve.tensor_tensor(h_f, h_f, h_b, ALU.add))
                    step.wait()
                    stt(yaT[:, ct, :], h_f, 0.5, yaT[:, ct, :], ALU.mult, ALU.mult).then_inc(sem("ya_ready"), 1)

            def next_bias(h):
                b = (h // 2) % 2
                dve.wait_ge(sem(f"bias_n_loaded{b}"), 64 * (h // 4 + 1))
                v = bias_n[:, b, :, :].rearrange("p h (i c) -> p (h i) c", c=GRID)
                step(dve.tensor_tensor(v, v, bc(kc[:, K_NAM:K_NAM + GRID].unsqueeze(1), [P, 12, GRID]), ALU.add))
                step.wait()

            def near(h):
                if h % 8 != 7:
                    if (h + 1) % 2 == 0:
                        next_bias(h + 1)
                    score_max("near")
                    score_probs("near")

            next_bias(0)
            score_max("near")
            score_probs("near")
            for h in range(8):
                if h >= 1:
                    recurrence(h - 1, 0)
                near(h)
                if h in (0, 1):
                    for b in range(2):
                        silu(f"in{2 + h}", b, yaT[:, 4 * h + 2 * b:4 * h + 2 * b + 2, :], 2 * h + b)
                if h in (3, 5):
                    i = (h - 3) // 2
                    for b in range(2):
                        silu(f"in{10 + i}", b, zbT[:, 4 * i + 2 * b:4 * i + 2 * b + 2, :], 4 + 2 * i + b)
                if h >= 1:
                    recurrence(h - 1, 1)
            recurrence(7, 0)
            recurrence(7, 1)
            next_bias(8)
            score_max("near")
            score_probs("near")

            def gated(name, i, g, last):
                for b in range(2):
                    src, free = full_at(dve, name, b)
                    v = src[:, :].rearrange("p (a b) -> p a b", b=S)
                    gv_ = g[:, 4 * i + 2 * b:4 * i + 2 * b + 2, :]
                    stt(gv_, gv_, 1.0, v, ALU.add, ALU.mult).then_inc(free, 1)
                    if last:
                        n = dense[name]
                        dve.wait_ge(bank_free[2 * (n % 2) + b], n // 2 + 1)
                        m = gaT[:, 4 * i + 2 * b:4 * i + 2 * b + 2, :]
                        ins = dve.tensor_tensor(m, m, gv_, ALU.add)
                        if i == 1 and b == 1:
                            ins.then_inc(sem("merged_ready"), 1)
                        else:
                            step(ins)

            for h in range(8, 16):
                near(h)
                if h in (12, 14):
                    i = (h - 12) // 2
                    taken(dve, f"in{12 + i}")
                    gated(f"pa{i}", i, gaT, False)
            dve.wait_ge(sem("o_taken"), 32)
            for i in range(2):
                taken(dve, f"in{10 + i}")
            stt(oT[:, :, :], oT[:, :, :], 0.5, zbT[:, :, :], ALU.mult, ALU.mult).then_inc(sem("yb_ready"), 1)
            diagonals("gateE")
            taken(dve, "pa1")
            for i in range(2):
                taken(dve, f"in{14 + i}")
                gated(f"pb{i}", i, gbT, True)
            gate_rows("gateE", 0.5)
            taken(dve, "gateE")
            add_mixed(("wo0", "wo1"), (pr[:, 0, :], pr[:, 1, :]))
            rstd(6)
            dve.wait_ge(sem("gf_loaded"), 16)
            stt(x[:, 0, :], x[:, 0, :], small[:, RSTD:RSTD + 1], gf_bc, ALU.mult, ALU.mult)\
                .then_inc(sem("out_ready"), 1)
            dve.wait_ge(sem("x_scaled_act"), 1)
            dve.tensor_tensor(x[:, 1, :], x[:, 1, :], gf_bc, ALU.mult).then_inc(sem("out_ready"), 1)

        @block.gpsimd
        def _(pool):
            pool.memset(rpb_pad[0:16, :, :], 0.0).then_inc(sem("rpb_zero"), 1)
            pool.wait_ge(sem("rpb_zero"), 1)
            with nc.allow_non_contiguous_dma(reason="short rows"):
                pool.dma_start(rpb_pad[0:16, :, 48:79], a["rpb_2"][0, :, 4:11, :]).then_inc(sem("rpb_loaded"), 16)
            pool.wait_ge(sem("rpb_loaded"), 16)
            rows = rpb_pad[0:16, :, :].rearrange("h i c -> h (i c)").unsqueeze(1)
            pool.dma_start(rpb_dram.rearrange("h q i c -> h q (i c)"), bc(rows, [16, GRID, 7 * P]))\
                .then_inc(sem("rpb_sent"), 16)
            pool.wait_ge(sem("rpb_sent"), 16)

            def experts(layer):
                done, first = PAIRS * layer, moe_start[layer]
                for q in range(2):
                    pool.wait_ge(gather_taken[q], 8 * layer + 8)
                pool.wait_ge(sem("gT_ready_act"), 2 * (layer + 1))
                pool.wait_ge(sem("gT_ready_dve"), 2 * (layer + 1))

                def copies(j):
                    pool.tensor_copy(x_cur[:, :, :], xgT[:, j, :, :] if isinstance(j, int)
                                     else xgT[:, bass.ds(j, 1), :, :].rearrange("p a k c -> p (a k) c"))\
                        .then_inc(sem("x_cur_ready"), 1)

                def weights_copy(j):
                    pool.tensor_copy(g_cur, gT[:, j, :] if isinstance(j, int)
                                     else gT[:, bass.ds(j, 1), :].rearrange("p a c -> p (a c)"))\
                        .then_inc(sem("g_cur_ready"), 1)

                copies(0)
                weights_copy(0)
                with pool.Fori(1, PAIRS) as j:
                    pool.wait_ge(unit_done, j * 6 + (first - 6 + 4))
                    copies(j)
                    pool.wait_ge(sem("scattered"), j + done)
                    weights_copy(j)

            def overflow(layer):
                pool.wait_ge(sem("x_summed"), layer + 1)

                def load(j):
                    which = late[0:1, layer, 1, bass.ds(j, 1)] if not isinstance(j, int) else late[0:1, layer, 1, 0:1]
                    expert = pool.value_load(which, min_val=0, max_val=EXPERTS - 1)
                    for m, w in enumerate((a["moe_w_gate"], a["moe_w_up"], a["moe_w_down"])):
                        src = w[layer][bass.ds(expert, 1)].rearrange("e (k p) c -> p (e k) c", p=P)
                        pool.dma_start(o_w[m].rearrange("p (k c) -> p k c", c=src.shape[2]), src)\
                            .then_inc(sem(f"o_loaded{layer}{m}"), 16)

                there = pool.value_load(late[0:1, layer, 0, 0:1], min_val=0, max_val=1)
                with pool.If(there > 0):
                    load(0)
                with pool.Fori(1, LATE) as j:
                    there = pool.value_load(late[0:1, layer, 0, bass.ds(j, 1)], min_val=0, max_val=1)
                    with pool.If(there > 0):
                        pool.wait_ge(sem(f"o_y_taken{layer}"), j)
                        load(j)

            def load_bias(pair):
                with nc.allow_non_contiguous_dma(reason="one row per query"):
                    for half, h in ((0, 0), (0, 1), (1, 0), (1, 1)):
                        src = bass.AP(rpb_dram.tensor, (2 * pair + h) * GRID * 7 * P + (1 - half) * P + GRID - 1,
                                      [[7 * P - 1, GRID], [P, 6], [1, GRID]])
                        dst = bias_n[64 * half:64 * half + 64, pair % 2, h, :].rearrange("p (i c) -> p i c", c=GRID)
                        pool.dma_start(dst, src).then_inc(sem(f"bias_n_loaded{pair % 2}"), 16)

            def load_gates(ct):
                for s_, name in enumerate(("w_r_f_2", "w_i_f_2", "w_r_b_2", "w_i_b_2")):
                    for half in range(2):
                        cut = slice(64 * half, 64 * half + 64)
                        pool.dma_start(rg_w[cut, ct % 2, s_, cut], a[name][0, 2 * ct + half])\
                            .then_inc(sem(f"rg_w_loaded{ct % 2}"), 16)

            experts(0)
            overflow(0)
            pool.memset(rg_w[:, :, :, :], 0.0).then_inc(sem("rg_w_zero"), 1)
            pool.wait_ge(sem("rg_w_zero"), 1)
            for n in range(2):
                load_bias(n)
                load_gates(n)
            experts(1)
            overflow(1)
            for h in range(12):
                if h % 2 == 0:
                    pool.wait_ge(sem("max_ready"), 8 + h + 2)
                    load_bias(h // 2 + 2)
                if h < KT - 2:
                    pool.wait_ge(sem("rg_gates_full"), 2 * h + 2)
                    load_gates(h + 2)


_INS = ["x", "c", "rel_bias", "norm1_g", "norm2_g", "w_ada", "b_ada", "ev_w_in", "ev_w_out", "ev_gmlp_ln_g",
        "ev_gmlp_ln_b", "ev_w_s", "ev_b_s", "od_w_in", "od_w_out", "od_w_dw", "od_b_dw", "od_conv_ln_g",
        "od_conv_ln_b", "moe_w_group", "moe_b_group", "moe_w_router", "moe_b_router", "moe_w_gate", "moe_w_up",
        "moe_w_down", "final_norm_g", "c_2", "g_pre_2", "w_c_2", "b_c_2", "w_in_2", "conv_w_2", "conv_b_2",
        "w_r_f_2", "b_r_f_2", "w_i_f_2", "b_i_f_2", "lam_f_2", "w_r_b_2", "b_r_b_2", "w_i_b_2", "b_i_b_2",
        "lam_b_2", "rpb_2", "w_pa_2", "w_pb_2", "w_o_2", "g_final_2"]


def kernel(**inputs):
    import concourse.bacc as bacc
    from concourse.bass_utils import run_bass_kernel_spmd

    nc = bacc.Bacc("TRN2", target_bir_lowering=False, num_devices=1)
    main, early, onehot = tables()
    arrays = {name: np.ascontiguousarray(inputs[name]) for name in _INS}
    arrays |= {"k_main": main, "k_early": early, "k_onehot": onehot}
    sent, aps = {}, {}
    for name, v in arrays.items():
        sent[f"in_{name}"] = v
        aps[name] = nc.dram_tensor(f"in_{name}", v.shape, mybir.dt.from_np(v.dtype), kind="ExternalInput").ap()
    out = nc.dram_tensor("out_0", (1, S, D), F32, kind="ExternalOutput").ap()
    program(nc, aps, out)
    r = run_bass_kernel_spmd(nc, [sent], core_ids=[0])
    return r.results[0]["out_0"]
```

```python
from contextlib import ExitStack

import numpy as np
import concourse.bass as bass
from concourse import mybir

F32 = mybir.dt.float32
BF16 = mybir.dt.bfloat16
I32 = mybir.dt.int32
ALU = mybir.AluOpType
ACT = mybir.ActivationFunctionType
AX = mybir.AxisListType.X

P = 128
D = 1024
KT = D // P
S = 256
TT = S // P
HW = 512
EPS = 1e-6
NEG = -1e30
RING = 6
LAYERS = 2
EXPERTS = 16
PAIRS = EXPERTS // 2
CHUNK = 32
CHUNKS = P // CHUNK
LATE = 2 * S // 65
CONV = 31
PAD = CONV - 1
ADA_SEG = 12
TWO_A, TWO_B = 5, 4
N_ADA = 2 * ADA_SEG + 6
GRID = 64
WIN = 16

CV_C, CV_C2, CV_N1, CV_N2, CV_GPRE = 120, 128, 136, 152, 168
CV_BDW, CV_LNG, CV_LNB, CV_CB2 = 176, 180, 184, 188
CV_RF, CV_IF, CV_RB, CV_IB, CV_LF, CV_LB = 196, 204, 212, 220, 228, 236
CV_DW, CV_CW2, CV_END = 244, 368, 400

K_ID, K_GE, K_LT, K_ONE, K_NEG, K_NAM, K_IOTA, K_W = 0, 128, 256, 384, 512, 640, 704, 832
K_END = 836
K2_MULT, K2_LE, K2_END = 0, 256, 384


def tables():
    i = np.arange(P)
    a = np.zeros((P, K_END), np.float32)
    a[:, K_ID:K_ID + P] = np.eye(P)
    a[:, K_GE:K_GE + P] = i[:, None] >= i[None, :]
    a[:, K_LT:K_LT + P] = i[:, None] < i[None, :]
    a[:, K_ONE:K_ONE + P] = 1.0
    a[:, K_NEG:K_NEG + P] = np.where(i[:, None] < i[None, :], 0.0, NEG)
    col = i % GRID
    first = np.clip(col - WIN // 2, 0, GRID - WIN)
    kc = np.arange(GRID)
    inside = (kc[None] >= first[:, None]) & (kc[None] < first[:, None] + WIN)
    a[:, K_NAM:K_NAM + GRID] = np.where(inside, 0.0, NEG)
    a[:, K_IOTA:K_IOTA + P] = np.arange(1, P + 1)
    a[:, K_W:K_W + 4] = [4, 3, 2, 1]

    def branches(dist):
        n = (dist <= 128).astype(np.float32) + (dist % 4 == 0) + (dist % 16 == 0)
        return np.where(dist >= 0, n, 0.0)

    b = np.zeros((P, K2_END), np.float32)
    b[:, K2_MULT:K2_MULT + S] = branches(P + i[:, None] - np.arange(S)[None])
    b[:, K2_LE:K2_LE + P] = i[:, None] <= i[None, :]

    dist = 255 - np.arange(384)
    d = np.maximum(np.clip(dist, 0, None), 1).astype(np.float32)
    large = 16 + (np.log(d / 16) / np.log(2048 / 16) * 16).astype(np.int32)
    bucket = np.where(dist < 16, np.clip(dist, 0, None), np.minimum(large, 31))
    e = np.zeros((64, 384), np.float32)
    valid = branches(dist) > 0
    e[bucket[valid], np.nonzero(valid)[0]] = 1.0
    e[32] = np.where(valid, 0.0, NEG)
    return a, b, e


def stream():
    u = [("ada", n) for n in range(4)]
    u += [("ev", 0), ("ada", 4), ("ev", 1), ("ada", 5), ("ev", 2)]
    u += [("ev", 4), ("ada", 6), ("ev", 3), ("ada", 7)]
    u += [("ada", n) for n in range(8, 17)]
    u += [("evo", 0), ("evo", 1)]
    u += [("moe", 0)] * (6 * PAIRS)
    u += [("od", 0), ("od", 1), ("od", 2), ("od", 3), ("od", 4)]
    u += [("ada", n) for n in range(17, 29)]
    u += [("odo", 0), ("ada", 29), ("odo", 1)]
    u += [("moe", 1)] * (6 * PAIRS)
    u += [("in", n) for n in (0, 1, 4, 6, 8, 2, 3, 10, 11, 12, 13, 5, 7, 9, 14)]
    u += [("pa", 0), ("pa", 1), ("in", 15), ("pb", 0), ("pb", 1), ("wo", 0), ("wo", 1)]
    return u


def program(nc, a, out):
    ctx = ExitStack()
    with ctx:
        named = {}

        def sem(name):
            if name not in named:
                named[name] = ctx.enter_context(nc.semaphore(name))
            return named[name]

        def sb(name, shape, dt=F32):
            return ctx.enter_context(nc.sbuf_tensor(name, shape, dt))

        units = stream()
        moe_start = [units.index(("moe", layer)) for layer in range(LAYERS)]

        ring = sb("ring", [P, RING, 4096])
        x = sb("x", [P, TT, D])
        cv = sb("cv", [P, CV_END])
        mod = sb("mod", [P, N_ADA * 4])
        kc = sb("kc", [P, K_END])
        gate_bc = sb("gate_bc", [P, D])
        ada_part = sb("ada_part", [P, HW])
        c_rep = sb("c_rep", [P, 2, KT, 32])
        gs = sb("gs", [P, 5, 2, KT])
        small = sb("small", [P, 64])
        rw = sb("rw", [P, KT, 20])
        rb = sb("rb", [P, 20])
        gates_over = sb("gates_over", [P, TT, EXPERTS])
        gates = sb("gates", [P, TT, EXPERTS])
        late = sb("late", [P, LAYERS, 2, EXPERTS], I32)
        split = sb("split", [P, LAYERS, CHUNKS - 1, PAIRS], I32)
        rgc = sb("rgc", [P, 48])
        rgt = sb("rgt", [P, 48])
        AR = 88 * 256
        arena = sb("arena", [P, AR])
        ps = [ctx.enter_context(nc.psum_tensor(f"bank{n}", [P, 512], F32)) for n in range(8)]

        def at(kb, *shape):
            n = int(np.prod(shape))
            v = arena[:, int(kb * 256):int(kb * 256) + n]
            if len(shape) == 2:
                v = v.rearrange("p (a b) -> p a b", b=shape[1])
            if len(shape) == 3:
                v = v.rearrange("p (a b c) -> p a b c", b=shape[1], c=shape[2])
            return v

        xn = at(0, TT, D)
        hT = at(8, KT, S)
        oT = at(16, KT, S)
        qT, kT, v_tok = at(24, 4, S), at(28, 4, S), at(32, TT, HW)
        gv, uT = at(36, TT, HW), at(40, 4, S)
        lng_bc, lnb_bc, bs_bc = at(44, HW), at(46, HW), at(48, 4, P)
        wsT, ws_raw = at(50, 4, P), at(52, 4, P)
        onehot, rel_ext, bias_rows = at(54, 384), at(55.5, 8), at(56, 384)
        stage = at(57.5, 4, P)
        bias_a = at(76, 8, S)
        k2 = at(84, K2_END)
        pr = at(60.5, 2, 512)
        prT = at(64.5, 512)
        aT, glT, hcT = at(36, 4, S), at(40, 4, S), at(44, 4, PAD + S)
        cacc, csq = at(48.5, 4, S), at(52.5, 4, S)
        crs = at(56.5, S)
        z_sb, e_sb, sp_sb, att_sb = at(60.5, 2, 384), at(63.5, 2, 384), at(66.5, 2, 384), at(69.5, 2, 384)
        rt = at(24, 1024)
        is_slot = at(28, TT, 2, P)
        pick, pick_g = at(30, TT, P), at(31, TT, P)
        x_cur, g_cur, silu_g = at(56, KT, P), at(60, S), at(61, HW)
        hid, hidT, y_pair = at(64, HW), at(66, 4, P), at(68, D)
        o_w = [at(24, 4096), at(40, 4096), at(56, 4096)]
        o_hidT, o_silu = at(16, 4, S), at(20, 4, S)
        fn_bc = at(72, D)
        zbT = at(0, KT, S)
        xa_raw = at(36, KT, 3 + S)
        gaT = at(36, KT, S)
        xc = at(44.5, KT, S)
        gbT = at(44.5, KT, S)
        yaT = at(52.5, KT, S)
        rg_t, rg_ti, rg_root = ([at(66.5 + 2 * n + w, S) for w in range(2)] for n in range(3))
        rg_u, rg_hf, rg_hb, rg_inv, rg_dec = (at(kb, S) for kb in (72.5, 73.5, 74.5, 82, 83))
        bias_n = at(76, 2, 2, 6 * GRID)
        rg_w = at(84, 2, 4, P)
        gf_bc = at(24, D)

        ident = kc[:, K_ID:K_ID + P]
        ge = kc[:, K_GE:K_GE + P]
        lt = kc[:, K_LT:K_LT + P]
        ones = kc[:, K_ONE:K_ONE + P]
        neg_diag = kc[:, K_NEG:K_NEG + P]

        bias_dram = nc.dram_tensor("bias_rows_dram", (8, P, 384), F32, kind="Internal").ap()
        rpb_dram = nc.dram_tensor("rpb_rows_dram", (16, GRID, 7, P), F32, kind="Internal").ap()
        rpb_pad = at(32, 7, P)

        def bc(ap, shape):
            return ap.to_broadcast(shape)

        loaded = [sem(f"ring_loaded{n}") for n in range(RING)]
        bank_full = [sem(f"bank_full{n}") for n in range(4)]
        bank_free = [sem(f"bank_free{n}") for n in range(4)]
        unit_done = sem("unit_done")


        dense = {}
        for name in ("ev0 ev1 ev2 ev4 ev3 mixA gateA evo0 evo1 gateB "
                     "od0 od1 od2 od3 od4 gateC odo0 odo1 gateD "
                     "in0 in1 in4 in6 in8 in2 in3 in10 in11 in12 in13 in5 in7 in9 "
                     "in14 pa0 pa1 in15 pb0 pb1 gateE wo0 wo1").split():
            dense[name] = len(dense)

        unit_of = {f"{kind}{i}": n for n, (kind, i) in enumerate(units) if kind != "moe"}

        def full_at(eng, name, b):
            n = dense[name]
            k = 2 * (n % 2) + b
            if b and name in unit_of:
                eng.wait_ge(unit_done, unit_of[name] + 1)
            elif b:
                before = [m for m in dense if dense[m] <= n and dense[m] % 2 == n % 2 and m not in unit_of]
                eng.wait_ge(bank_full[k], len(before))
            else:
                eng.wait_ge(bank_full[k], n // 2 + 1)
            return ps[k], bank_free[k]

        def taken(eng, name):
            n = dense[name]
            for b in range(2):
                eng.wait_ge(bank_free[2 * (n % 2) + b], n // 2 + 1)

        between_near = {0: "in2", 1: "in3", 2: "in10", 3: "in11", 5: "in12", 6: "in13",
                        8: "in14", 10: "pa0", 12: "pa1", 14: "in15"}

        block = ctx.enter_context(nc.Block())

        class Steps:

            def __init__(self, eng, name):
                self.eng, self.sem, self.n = eng, sem(name), 0

            def __call__(self, ins):
                ins.then_inc(self.sem, 1)
                self.n += 1

            def wait(self):
                self.eng.wait_ge(self.sem, self.n)

        SUMSQ, RSTD, NEGMAX, DEN, RDEN, BN, MV = 0, 2, 4, 8, 12, 16, 30

        w_of = {
            "ev": a["ev_w_in"][0], "evo": a["ev_w_out"][0], "od": a["od_w_in"][0], "odo": a["od_w_out"][0],
            "in": a["w_in_2"][0], "pa": a["w_pa_2"][0], "pb": a["w_pb_2"][0], "wo": a["w_o_2"][0],
        }

        def rows_of(ap):
            return ap.rearrange("l (r c) -> (l r) c", c=P)

        rows = [(0, rows_of(a["b_ada"]), 96), (96, rows_of(a["b_c_2"]), 24), (120, rows_of(a["c"]), 8)]
        place = CV_C2
        for name, n in (("c_2", 8), ("norm1_g", 16), ("norm2_g", 16), ("g_pre_2", 8), ("od_b_dw", 4),
                        ("od_conv_ln_g", 4), ("od_conv_ln_b", 4), ("conv_b_2", 8), ("b_r_f_2", 8),
                        ("b_i_f_2", 8), ("b_r_b_2", 8), ("b_i_b_2", 8), ("lam_f_2", 8), ("lam_b_2", 8)):
            rows.append((place, rows_of(a[name]), n))
            place += n
        assert place == CV_DW
        for j in range(4):
            rows.append((2 * P + CONV * j, a["od_w_dw"][0, :, j * P:(j + 1) * P], CONV))
            rows.append((3 * P + 8 * j, rows_of(a["conv_w_2"][0])[8 * j:8 * j + 8], 8))
        assert len(rows) == 25

        def load_rows(eng, some):
            for r, src, n in some:
                eng.dma_start(stage[r % P:r % P + n, r // P, :], src).then_inc(sem("stage_loaded"), 16)

        @block.sync
        def _(sp):
            def fetch(n, src):
                if n >= RING:
                    sp.wait_ge(unit_done, n - RING + 1)
                if n == 1:
                    load_rows(sp, rows[1::2])
                    sp.wait_ge(sem("stage_loaded"), 16 * 25)
                sp.dma_start(ring[:, n % RING, :].rearrange("p (k c) -> p k c", c=src.shape[2]), src)\
                  .then_inc(loaded[n % RING], 16)

            def layout(w, c0):
                return w[:, c0:c0 + 512].rearrange("(k p) c -> p k c", p=P)

            n = 0
            while n < len(units):
                kind, i = units[n]
                if kind == "moe":
                    w_gate, w_up, w_down = (a[f"moe_w_{w}"][i] for w in ("gate", "up", "down"))
                    first = moe_start[i]
                    with sp.Fori(0, PAIRS) as j:
                        for m, (w, e) in enumerate([(w_gate, 0), (w_gate, 1), (w_up, 0), (w_up, 1),
                                                    (w_down, 0), (w_down, 1)]):
                            s = (first + m) % RING
                            sp.wait_ge(unit_done, j * RING + (first + m - RING + 1))
                            src = w[bass.ds(2 * j + e, 1)].rearrange("e (k p) c -> p (e k) c", p=P)
                            sp.dma_start(ring[:, s, :].rearrange("p (k c) -> p k c", c=src.shape[2]), src)\
                              .then_inc(loaded[s], 16)
                    n += 6 * PAIRS
                    continue
                if kind == "ada":
                    w = a["w_ada"][i // ADA_SEG] if i < 2 * ADA_SEG else a["w_c_2"][0]
                    fetch(n, layout(w, 512 * (i % ADA_SEG)))
                else:
                    fetch(n, layout(w_of[kind], 512 * i))
                n += 1

            sp.wait_ge(sem("out_ready"), 2)
            sp.dma_start(out.rearrange("b (t p) d -> p (b t) d", p=P), x[:, :, :]).then_inc(sem("out_sent"), 16)
            sp.wait_ge(sem("out_sent"), 16)

        @block.tensor
        def _(pe):
            unit = [0]

            def weights():
                n = unit[0]
                unit[0] += 1
                pe.wait_ge(loaded[n % RING], 16 * (n // RING + 1))
                return ring[:, n % RING, :].rearrange("p (k c) -> p k c", c=512)

            def bank_of(name, b):
                n = dense[name]
                k = 2 * (n % 2) + b
                if n >= 2:
                    pe.wait_ge(bank_free[k], n // 2)
                return k

            def by_channel(name, rhs):
                w = weights()
                for b in range(2):
                    k0 = bank_of(name, b)
                    for t in range(2):
                        c = (2 * b + t) * P
                        for k in range(KT):
                            mm = pe.matmul(ps[k0][:, t * S:(t + 1) * S], w[:, k, c:c + P], rhs[:, k, :],
                                           start=(k == 0), stop=(k == KT - 1))
                    mm.then_inc(unit_done if b else bank_full[k0], 1)

            def by_token(name, lhs):
                w = weights()
                for b in range(TT):
                    k0 = bank_of(name, b)
                    for k in range(KT):
                        mm = pe.matmul(ps[k0][:, :], lhs[:, k, b * P:(b + 1) * P], w[:, k, :],
                                       start=(k == 0), stop=(k == KT - 1))
                    mm.then_inc(unit_done if b else bank_full[k0], 1)

            ada = [0, 0]

            def ada_main():
                n = ada[0]
                ada[0] += 1
                w = weights()
                if n:
                    pe.wait_ge(sem("ada_ready"), n)
                else:
                    pe.wait_ge(sem("c_ready"), 1)
                for r in range(2):
                    for g in range(4):
                        mm = pe.matmul(ps[4][32 * g:32 * g + 32, :], c_rep[:, n // (2 * ADA_SEG), 4 * r + g, :],
                                       w[:, 4 * r + g, :], start=(r == 0), stop=(r == 1),
                                       tile_position=(0, 32 * g))
                mm.then_inc(unit_done, 1)

            def ada_columns():
                n = ada[1]
                ada[1] += 1
                pe.wait_ge(sem("ada_part_taken"), n + 1)
                for c in range(4):
                    mm = pe.matmul(ps[4][:, c:c + 1], ada_part[:, c * P:(c + 1) * P], ones[:, 0:1],
                                   start=True, stop=True)
                mm.then_inc(sem("ada_cols_full"), 1)

            def gate_rows(name):
                pe.wait_ge(sem("diag_ready"), "ABCDE".index(name[-1]) + 1)
                for b in range(2):
                    k0 = bank_of(name, b)
                    pe.matmul(ps[k0][:, :], ones, gate_bc[:, b * 512:(b + 1) * 512], start=True, stop=True)\
                      .then_inc(bank_full[k0], 1)

            def turn_x(r):
                pe.wait_ge(sem("xn_ready_act"), r + 1)
                pe.wait_ge(sem("xn_ready_dve"), r + 1)
                for b in range(4):
                    for k in (2 * b, 2 * b + 1):
                        for t in range(TT):
                            o = (k % 2) * S + t * P
                            mm = pe.transpose(ps[b][:, o:o + P], xn[:, t, k * P:(k + 1) * P], ident)
                    mm.then_inc(sem("turned"), 1)
                pe.wait_ge(sem("hT_act"), r + 1)
                pe.wait_ge(sem("hT_dve"), r + 1)

            pe.wait_ge(sem("kc_loaded"), 16)
            pe.wait_ge(sem("stage_loaded"), 16 * 25)
            for n, (lo, rows) in enumerate(((0, P), (P, 116), (CV_DW, 124), (CV_CW2, 32))):
                mm = pe.transpose(ps[5][:, n * P:n * P + rows], stage[0:rows, n, :], ident[0:rows, 0:rows])
            mm.then_inc(sem("cv_full"), 1)
            pe.wait_ge(sem("cv_ready"), 1)
            pe.wait_ge(sem("onehot_loaded"), 32)
            pe.wait_ge(sem("rel_ones"), 1)
            pe.matmul(ps[5][0:8, 0:384], rel_ext[0:64, :], onehot[0:64, :], start=True, stop=True)\
              .then_inc(sem("bias_full"), 1)
            pe.wait_ge(sem("ws_loaded"), 16)
            for g in range(4):
                mm = pe.transpose(ps[6][:, g * P:(g + 1) * P], ws_raw[:, g, :], ident)
            mm.then_inc(sem("ws_full"), 1)
            for n in range(4):
                ada_main()
                ada_columns()
            turn_x(0)

            head = [0]

            def scores(h, rows, kind):
                n = head[0]
                head[0] += 1
                bank = ps[6 + n % 2]
                if n >= 2:
                    pe.wait_ge(sem("o_taken"), n - 1)
                p0 = 64 * (h % 2)
                q, k = qT[p0:p0 + 64, h // 2 % 4, :], kT[p0:p0 + 64, h // 2 % 4, :]
                if kind == "dilated":
                    pe.matmul(bank[:, 0:S], q[:, P:S], k[:, :], start=True, stop=True)
                    mm = pe.matmul(bank[:, S:S + P], q[:, 0:P], k[:, 0:P], start=True, stop=True)
                elif kind == "stick":
                    pe.matmul(bank[:, 0:S], k[:, 0:P], q[:, :], start=True, stop=True)
                    mm = pe.matmul(bank[:, S:S + P], k[:, P:S], q[:, P:S], start=True, stop=True)
                else:
                    pe.matmul(bank[:, 0:S], q[:, 0:P], k[:, :], start=True, stop=True)
                    mm = pe.matmul(bank[:, S:2 * S], q[:, P:S], k[:, :], start=True, stop=True)
                mm.then_inc(sem("scores_full"), 1)

            def turn(n, kind):
                pe.wait_ge(sem("probs_ready"), n + 1)
                if kind == "stick":
                    sp_h = sp_sb[:, n % 2, :]
                    pe.matmul(ps[5][:, 0:S], ge, sp_h[:, 0:S], start=True, stop=True)
                    pe.matmul(ps[5][:, P:S], ones, sp_h[:, S:S + P], start=False, stop=True, skip_group_check=True)
                    mm = pe.matmul(ps[5][:, S:S + P], ge, sp_h[:, S:S + P], start=True, stop=True)
                    mm.then_inc(sem("probsT_full"), 1)
                else:
                    p = pr[:, n % 2, :]
                    if kind == "dilated":
                        blocks = [p[:, S:S + P], p[:, 0:P], p[:, P:S]]
                    else:
                        blocks = [p[:, 0:P], p[:, S:S + P], p[:, P:S], p[:, S + P:2 * S]]
                    for m, blk in enumerate(blocks):
                        mm = pe.transpose(ps[5][:, m * P:(m + 1) * P], blk, ident)
                    mm.then_inc(sem("probsT_full"), 1)

            def values(n, h, kind):
                pe.wait_ge(sem("probsT_ready"), n + 1)
                bank, vt = ps[6 + n % 2], v_tok[:, :, 64 * (h % 8):64 * (h % 8) + 64]
                rhs = att_sb[:, n % 2, :] if kind == "stick" else prT
                o = bank[64 * (h % 2):64 * (h % 2) + 64, 0:S]
                if kind == "near":
                    pe.matmul(o, vt[:, 0, :], rhs[:, 0:S], start=True, stop=False)
                    mm = pe.matmul(o, vt[:, 1, :], rhs[:, S:2 * S], start=False, stop=True)
                else:
                    pe.matmul(o, vt[:, 0, :], rhs[:, 0:S], start=True, stop=True)
                    mm = pe.matmul(o[:, P:S], vt[:, 1, :], rhs[:, S:S + P], start=False, stop=True,
                                   skip_group_check=True)
                mm.then_inc(sem("o_full"), 1)

            def heads(lo, hi, kind, between, after=lambda h: None, mid=lambda h: None):
                base = head[0]
                scores(lo, 0, kind)
                for h in range(lo, hi):
                    if h + 1 < hi:
                        scores(h + 1, 0, kind)
                    between(h)
                    turn(base + h - lo, kind)
                    mid(h)
                    values(base + h - lo, h, kind)
                    after(h)

            def experts(layer):
                first = moe_start[layer]
                taken(pe, "gateB" if layer == 0 else "gateD")
                pe.wait_ge(sem("rw_loaded"), 16 * 7 * (layer + 1))
                for t in range(TT):
                    for k in range(KT):
                        mm = pe.matmul(ps[4][:, 20 * t:20 * t + 20], hT[:, k, t * P:(t + 1) * P], rw[:, k, :],
                                       start=(k == 0), stop=(k == KT - 1))
                mm.then_inc(sem("logits_full"), 1)
                pe.wait_ge(sem("mask_ready"), layer + 1)
                mask = rt[:, 512:512 + 32].rearrange("p (t e) -> p t e", e=EXPERTS)
                pe.matmul(ps[5][:, 0:16], lt, mask[:, 0, :], start=True, stop=True)
                pe.matmul(ps[5][:, 16:32], ones, mask[:, 0, :], start=True, stop=False)
                pe.matmul(ps[5][:, 16:32], lt, mask[:, 1, :], start=False, stop=True)
                pe.matmul(ps[5][:, 32:48], ones, mask[:, 0, :], start=True, stop=False)
                pe.matmul(ps[5][:, 32:48], ones, mask[:, 1, :], start=False, stop=True)\
                  .then_inc(sem("rank_full"), 1)
                pe.wait_ge(sem("over_ready"), layer + 1)
                pe.matmul(ps[4][:, 0:32], ones, rt[:, 576:608], start=True, stop=True)\
                  .then_inc(sem("over_full"), 1)
                pe.wait_ge(sem("zeros_ready"), layer + 1)
                zero = hidT[:, 0:2, :].rearrange("p a b -> p (a b)").bitcast(BF16)
                for b in range(4):
                    mm = pe.matmul(ps[b][:, :], zero[:, 0:P], zero, start=True, stop=True, skip_group_check=True)

                def landed(m, j):
                    n = first + m
                    pe.wait_ge(loaded[n % RING], (j + (n // RING + 1)) * 16)

                done = PAIRS * layer

                def gather(j):
                    pe.wait_ge(sem("pick_ready"), j + (done + 1))
                    for b in range(2):
                        for k in range(4 * b, 4 * b + 4):
                            for t in range(TT):
                                mm = pe.matmul(ps[6 + b][:, (k % 4) * P:(k % 4 + 1) * P],
                                               xn[:, t, k * P:(k + 1) * P], pick[:, t, :],
                                               start=(t == 0), stop=(t == TT - 1))
                        mm.then_inc(sem("gather_full"), 1)

                def by_split(splits, emit):
                    for n in range(1, CHUNKS):
                        with pe.If(splits[n - 1] > 0):
                            emit(n)

                def chunks(bank, lhs, k, m0, cut, n, start, stop):
                    s0 = (first + m0) % RING
                    groups = {1: ((0, 32, 0), (32, 32, 1), (64, 64, 1)), 2: ((0, 64, 0), (64, 64, 1)),
                              3: ((0, 64, 0), (64, 32, 0), (96, 32, 1))}[n]
                    for col, width, e in groups:
                        mm = pe.matmul(bank[col:col + width, :], lhs[:, k, col:col + width], ring[:, s0 + e, cut],
                                       start=start, stop=stop, tile_position=(0, col))
                    return mm

                def gate_up(j, splits):
                    pe.wait_ge(sem("x_cur_act"), j + (done + 1))
                    pe.wait_ge(sem("x_cur_dve"), j + (done + 1))
                    if not isinstance(j, int) or j:
                        pe.wait_ge(sem("g_cur_ready"), j + done)
                    def products(n):
                        for bank, m0 in ((4, 0), (5, 2)):
                            landed(m0, j)
                            landed(m0 + 1, j)
                            for k in range(KT):
                                mm = chunks(ps[bank], x_cur, k, m0, slice(k * 512, k * 512 + 512), n,
                                            k == 0, k == KT - 1)
                            mm.then_inc(unit_done, 2)

                    by_split(splits, products)

                def scatter(j):
                    for t in range(TT):
                        for half in range(2):
                            mm = pe.matmul(ps[2 * t + half][:, :], g_cur[:, t * P:(t + 1) * P],
                                           y_pair[:, half * 512:(half + 1) * 512], start=False, stop=True,
                                           skip_group_check=True)
                    mm.then_inc(sem("scattered"), 1)

                def results(j):
                    pe.wait_ge(sem("g_cur_ready"), j + (done + 1))
                    pe.wait_ge(sem("y_pair_act"), j + (done + 1))
                    pe.wait_ge(sem("y_pair_dve"), j + (done + 1))

                def down(j, splits, last=False):
                    pe.wait_ge(sem("hid_ready"), j + (done + 1))
                    for f in range(4):
                        mm = pe.transpose(ps[4][:, f * P:(f + 1) * P], hid[:, f * P:(f + 1) * P], ident)
                    mm.then_inc(sem("hidT_full"), 1)
                    pe.wait_ge(sem("pick_g_ready"), j + (done + 1))
                    for t in range(TT):
                        mm = pe.transpose(ps[5][:, t * P:(t + 1) * P], pick_g[:, t, :], ident)
                    mm.then_inc(sem("gT_full"), 1)
                    landed(4, j)
                    landed(5, j)
                    pe.wait_ge(sem("hidT_ready"), j + (done + 1))
                    if not last:
                        pe.wait_ge(sem("x_cur_act"), j + (done + 2))
                        pe.wait_ge(sem("x_cur_dve"), j + (done + 2))
                    def products(n):
                        for half in range(2):
                            for f in range(4):
                                mm = chunks(ps[6 + half], hidT, f, 4,
                                            slice(f * D + half * 512, f * D + half * 512 + 512), n,
                                            f == 0, f == 3)
                            if half == 0:
                                mm.then_inc(sem("down_full"), 1)
                            else:
                                mm.then_inc(unit_done, 2)

                    by_split(splits, products)

                def splits_of(j):
                    col = slice(j, j + 1) if isinstance(j, int) else bass.ds(j, 1)
                    return [pe.value_load(split[0:1, layer, n, col], min_val=0, max_val=1) for n in range(3)]

                gather(0)
                pe.wait_ge(sem("late_ready"), layer + 1)
                splits = splits_of(0)
                gate_up(0, splits)
                gather(1)
                down(0, splits)
                with pe.Fori(1, PAIRS - 1) as j:
                    splits = splits_of(j)
                    gate_up(j, splits)
                    results(j - 1)
                    gather(j + 1)
                    scatter(j - 1)
                    down(j, splits)
                splits = splits_of(PAIRS - 1)
                gate_up(PAIRS - 1, splits)
                results(PAIRS - 2)
                scatter(PAIRS - 2)
                down(PAIRS - 1, splits, last=True)
                results(PAIRS - 1)
                scatter(PAIRS - 1)
                unit[0] = first + 6 * PAIRS

            def overflow(layer):
                some = pe.value_load(late[0:1, layer, 0, 0:1], min_val=0, max_val=1)
                with pe.If(some > 0):
                    pe.wait_ge(sem("x_summed"), layer + 1)
                    late_experts(layer)

            def late_experts(layer):
                with pe.Fori(0, LATE) as j:
                    there = pe.value_load(late[0:1, layer, 0, bass.ds(j, 1)], min_val=0, max_val=1)
                    with pe.If(there > 0):
                        for m, w in enumerate(o_w[:2]):
                            pe.wait_ge(sem(f"o_loaded{layer}{m}"), j * 16 + 16)
                            wv = w.rearrange("p (k c) -> p k c", c=512)
                            for c in range(4):
                                for k in range(KT):
                                    mm = pe.matmul(ps[2 * m + c // 2][:, (c % 2) * S:(c % 2) * S + S],
                                                   wv[:, k, c * P:(c + 1) * P], hT[:, k, :],
                                                   start=(k == 0), stop=(k == KT - 1))
                        mm.then_inc(sem(f"o_hid_full{layer}"), 1)
                        pe.wait_ge(sem(f"o_hid_ready{layer}"), j + 1)
                        pe.wait_ge(sem(f"o_loaded{layer}2"), j * 16 + 16)
                        wv = o_w[2].rearrange("p (f c) -> p f c", c=D)
                        for t in range(TT):
                            for half in range(2):
                                for f in range(4):
                                    mm = pe.matmul(ps[4 + 2 * t + half][:, :], o_hidT[:, f, t * P:(t + 1) * P],
                                                   wv[:, f, half * 512:(half + 1) * 512],
                                                   start=(f == 0), stop=(f == 3))
                        mm.then_inc(sem(f"o_y_full{layer}"), 1)
                        pe.wait_ge(sem(f"o_y_taken{layer}"), j + 1)

            by_channel("ev0", hT)
            ada_main()
            by_channel("ev1", hT)
            ada_columns()
            ada_main()
            by_token("ev2", hT)
            ada_columns()
            for name in ("ev0", "ev1", "ev2"):
                taken(pe, name)

            def between_a(h):
                if h == 0:
                    by_token("ev4", hT)
                elif h == 1:
                    by_channel("ev3", hT)
                elif h > TWO_A:
                    ada_columns()
                if h == 3:
                    pe.wait_ge(sem("gv_ready"), 1)
                    taken(pe, "ev3")
                    pe.wait_ge(sem("wsT_ready"), 1)
                    for b in range(2):
                        k0 = bank_of("mixA", b)
                        for g in (2 * b, 2 * b + 1):
                            for t in range(TT):
                                o = (g % 2) * S + t * P
                                mm = pe.matmul(ps[k0][:, o:o + P], gv[:, t, g * P:(g + 1) * P], wsT[:, g, :],
                                               start=True, stop=True)
                        mm.then_inc(bank_full[k0], 1)
                if h == 5:
                    gate_rows("gateA")

            def after_a(h):
                ada_columns()
                if h >= TWO_A:
                    ada_main()

            heads(0, 8, "dilated", between_a, after_a, lambda h: ada_main())
            ada_columns()
            pe.wait_ge(sem("o_taken"), 8)
            pe.wait_ge(sem("o_b_ready"), 1)
            by_token("evo0", oT)
            by_token("evo1", oT)
            turn_x(1)
            gate_rows("gateB")
            experts(0)
            overflow(0)
            turn_x(2)

            by_channel("od0", hT)
            by_channel("od1", hT)
            by_channel("od2", hT)
            by_channel("od3", hT)
            by_token("od4", hT)
            for name in ("od2", "od3", "od4"):
                taken(pe, name)

            def mid_b(h):
                if h > TWO_B:
                    ada_columns()
                if h == 5:
                    pe.wait_ge(sem("conv_ready"), 1)
                    for ct in range(4):
                        mm = pe.matmul(ps[2][:, 0:S], ones, cacc[:, ct, :], start=(ct == 0), stop=(ct == 3))
                    mm.then_inc(sem("mean_full"), 1)
                if h == 6:
                    pe.wait_ge(sem("csq_ready"), 1)
                    for ct in range(4):
                        mm = pe.matmul(ps[2][:, S:2 * S], ones, csq[:, ct, :], start=(ct == 0), stop=(ct == 3))
                    mm.then_inc(sem("var_full"), 1)
                ada_main()
                if h == 7:
                    pe.wait_ge(sem("crs_ready"), 1)
                    gate_rows("gateC")

            def after_b(h):
                ada_columns()
                if h >= TWO_B:
                    ada_main()

            heads(0, 8, "stick", lambda h: None, after_b, mid_b)
            ada_columns()
            pe.wait_ge(sem("o_taken"), 16)
            pe.wait_ge(sem("o_c_ready"), 1)
            by_token("odo0", oT)
            ada_main()
            ada_columns()
            by_token("odo1", oT)
            turn_x(3)
            gate_rows("gateD")
            experts(1)
            overflow(1)

            turn_x(4)
            by_channel("in0", hT)
            by_channel("in1", hT)
            by_channel("in4", hT)
            by_channel("in6", hT)
            by_token("in8", hT)
            for name in ("in4", "in6", "in8"):
                taken(pe, name)
            pe.wait_ge(sem("xc_ready"), 1)

            def recurrence_gates(ct, way):
                n = 2 * ct + way
                if n:
                    pe.wait_ge(sem("rg_gates_taken"), n)
                pe.wait_ge(sem(f"rg_w_loaded{ct % 2}"), 16 * 8 * (ct // 2 + 1))
                for g in range(2):
                    mm = pe.matmul(ps[4][:, g * S:(g + 1) * S], rg_w[:, ct % 2, 2 * way + g, :], xc[:, ct, :],
                                   start=True, stop=True)
                mm.then_inc(sem("rg_gates_full"), 1)

            def between_c(h):
                recurrence_gates(h, 0)
                if h in between_near:
                    by_channel(between_near[h], hT)

            heads(0, 8, "near", between_c, lambda h: recurrence_gates(h, 1))
            by_channel("in5", hT)
            by_channel("in7", hT)
            by_token("in9", hT)
            for name in ("in5", "in7", "in9"):
                taken(pe, name)

            def between_d(h):
                if h == 10:
                    pe.wait_ge(sem("ya_ready"), KT)
                if h in between_near:
                    name = between_near[h]
                    by_channel(name, yaT if name.startswith("pa") else hT)

            heads(8, 16, "near", between_d)
            pe.wait_ge(sem("yb_ready"), 1)
            by_channel("pb0", oT)
            by_channel("pb1", oT)
            gate_rows("gateE")
            pe.wait_ge(sem("merged_ready"), 1)
            by_token("wo0", gaT)
            by_token("wo1", gaT)

        @block.scalar
        def _(act):
            step = Steps(act, "act_steps")

            act.dma_start(x[:, :, :], a["x"].rearrange("b (t p) d -> p (b t) d", p=P)).then_inc(sem("x_loaded"), 16)
            act.dma_start(kc[:, :], a["k_main"]).then_inc(sem("kc_loaded"), 16)

            load_rows(act, rows[0::2])
            act.dma_start(onehot[0:64, :], a["k_onehot"]).then_inc(sem("onehot_loaded"), 16)
            act.wait_ge(sem("rel_ones"), 1)
            act.dma_start(rel_ext[0:32, :], a["rel_bias"]).then_inc(sem("onehot_loaded"), 16)
            act.dma_start(ws_raw[:, :, :], a["ev_w_s"][0].rearrange("g t s -> t g s")).then_inc(sem("ws_loaded"), 16)

            act.wait_ge(sem("cv_full"), 1)
            act.copy(cv[:, 0:CV_DW], ps[5][:, 0:CV_DW])
            act.copy(cv[:, CV_DW:CV_DW + 124], ps[5][:, 2 * P:2 * P + 124])
            act.copy(cv[:, CV_CW2:CV_END], ps[5][:, 3 * P:3 * P + 32]).then_inc(sem("cv_ready"), 1)
            act.wait_ge(sem("cv_ready"), 1)
            for n, c0 in enumerate((CV_C, CV_C2)):
                ins = act.activation(c_rep[:, n, :, :], bc(cv[:, c0:c0 + KT].unsqueeze(2), [P, KT, 32]), ACT.Silu)
            ins.then_inc(sem("c_ready"), 1)

            step(act.activation(rgt[:, 0:16], cv[:, CV_LF:CV_LF + 16], ACT.Abs))
            step.wait()
            act.activation(rgt[:, 0:16], rgt[:, 0:16], ACT.Exp, scale=-1.0).then_inc(sem("lam_exp_ready"), 1)

            act.wait_ge(sem("bias_full"), 1)
            act.copy(bias_rows[0:8, :], ps[5][0:8, 0:384]).then_inc(sem("bias_rows_ready"), 1)

            def square(s):
                for t in range(TT):
                    ins = act.activation(xn[:, t, :], x[:, t, :], ACT.Square,
                                         accum_out=small[:, SUMSQ + t:SUMSQ + t + 1])
                ins.then_inc(sem("sumsq_ready"), 1)

            def root(v, ready, done, n=1):
                act.wait_ge(sem(ready), n)
                act.activation(v, v, ACT.Sqrt).then_inc(sem(done), 1)

            def norm_root(s):
                root(small[:, RSTD:RSTD + 2], "ms_ready", "root_ready", s + 1)

            def normalise(s, r):
                norm_root(s)
                act.wait_ge(sem("rstd_ready"), s + 1)
                act.activation(xn[:, 1, :], x[:, 1, :], ACT.Copy, scale=small[:, RSTD + 1:RSTD + 2])\
                   .then_inc(sem("xn_ready_act"), 1)

            def turned(r):
                act.wait_ge(sem("gain_ready"), r + 1)
                sh = (0, 24, 48, 72, 96)[r]
                for b in (0, 2):
                    act.wait_ge(sem("turned"), 4 * r + b + 1)
                    for k in (2 * b, 2 * b + 1):
                        ins = act.activation(hT[:, k, :], ps[b][:, (k % 2) * S:(k % 2 + 1) * S], ACT.Identity,
                                             bias=mod[:, sh + k:sh + k + 1], scale=gs[:, r, 0, k:k + 1])
                ins.then_inc(sem("hT_act"), 1)

            parts = [0]

            def ada_part_copy():
                n = parts[0]
                parts[0] += 1
                act.wait_ge(unit_done, unit_of[f"ada{n}"] + 1)
                act.copy(ada_part[:, :], ps[4][:, :]).then_inc(sem("ada_part_taken"), 1)

            def take(name, b, dst, func=ACT.Copy, scale=1.0):
                src, free = full_at(act, name, b)
                v = src[:, :].rearrange("p (a b) -> p a b", b=dst.shape[2]) if len(dst.shape) == 3 else src[:, :]
                act.activation(dst, v, func, scale=scale).then_inc(free, 1)

            def both(name, dst, func=ACT.Copy, scale=1.0):
                take(name, 0, dst[:, 0:2, :], func, scale)
                take(name, 1, dst[:, 2:4, :], func, scale)

            def tokens(name, dst, func=ACT.Copy):
                for b in range(TT):
                    take(name, b, dst[:, b, :], func)

            head = [0]

            def softmax_exp(kind):
                n = head[0]
                head[0] += 1
                act.wait_ge(sem("max_ready"), softmaxes(n) + 1)
                p = pr[:, n % 2, :]
                width = (S, P) if kind == "dilated" else (S, S)
                for m in range(2):
                    c = NEGMAX + 2 * (n % 2) + m
                    kw = {} if kind == "dilated" else {
                        "accum_out": small[:, DEN + 2 * (n % 2) + m:DEN + 2 * (n % 2) + m + 1]}
                    ins = act.activation(p[:, m * S:m * S + width[m]], p[:, m * S:m * S + width[m]], ACT.Exp,
                                         bias=small[:, c:c + 1], **kw)
                ins.then_inc(sem("exp_ready"), 1)

            def softmaxes(n):
                return n if n < 8 else n - 8

            def softplus_parts():
                n = head[0]
                head[0] += 1
                act.wait_ge(sem("scores_full"), n + 1)
                bank, b = ps[6 + n % 2], n % 2
                act.copy(z_sb[:, b, :], bank[:, 0:384])
                step(act.activation(e_sb[:, b, :], bank[:, 0:384], ACT.Abs))
                step.wait()
                step(act.activation(e_sb[:, b, :], e_sb[:, b, :], ACT.Exp, scale=-1.0))
                step.wait()
                act.activation(e_sb[:, b, :], e_sb[:, b, :], ACT.Ln, bias=1.0).then_inc(sem("log_ready"), 1)

            def stick_exp(n):
                act.wait_ge(sem("stick_arg_ready"), n - 8 + 1)
                act.activation(att_sb[:, n % 2, :], att_sb[:, n % 2, :], ACT.Exp).then_inc(sem("probsT_ready"), 1)

            def turned_probs(n, width):
                act.wait_ge(sem("probsT_full"), n + 1)
                act.copy(prT[:, 0:width], ps[5][:, 0:width]).then_inc(sem("probsT_ready"), 1)

            def head_out(n, h, first):
                act.wait_ge(sem("o_full"), n + 1)
                p0 = 64 * (h % 2)
                act.copy(oT[p0:p0 + 64, first + h // 2, :], ps[6 + n % 2][p0:p0 + 64, 0:S]).then_inc(sem("o_taken"), 1)

            def gate_rows(name, scale=1.0):
                src, free = full_at(act, name, 0)
                act.activation(gate_bc[:, 0:512], src[:, :], ACT.Copy, scale=scale).then_inc(free, 1)

            def experts(layer):
                done = PAIRS * layer
                first = moe_start[layer]
                act.wait_ge(sem("route_max_ready"), 2 * layer + 1)
                act.activation(rt[:, 40:48], rt[:, 40:48], ACT.Exp).then_inc(sem("route_exp_ready"), 1)
                act.wait_ge(sem("route_max_ready"), 2 * layer + 2)
                act.activation(rt[:, 48:50], rt[:, 48:50], ACT.Exp).then_inc(sem("route_exp_ready"), 1)

                def tokens_taken(j):
                    sh = (24, 72)[layer]
                    act.wait_ge(sem("gather_full"), 2 * j + (2 * done + 1))
                    for k in range(4):
                        ins = act.activation(x_cur[:, k, :], ps[6][:, k * P:(k + 1) * P], ACT.Identity,
                                             bias=mod[:, sh + k:sh + k + 1],
                                             scale=gs[:, 2 * layer + 1, 0, k:k + 1])
                    ins.then_inc(sem("x_cur_act"), 1)

                def pair(j, last=False):
                    act.wait_ge(unit_done, j * 6 + (first + 2))
                    act.activation(silu_g, ps[4][:, :], ACT.Silu).then_inc(sem("silu_ready"), 1)
                    if not last:
                        tokens_taken(j + 1)
                    act.wait_ge(sem("hidT_full"), j + (done + 1))
                    act.copy(hidT[:, :, :], ps[4][:, :].rearrange("p (a b) -> p a b", b=P)).then_inc(sem("hidT_ready"), 1)
                    act.wait_ge(sem("gT_full"), j + (done + 1))
                    if not isinstance(j, int) or j:
                        act.wait_ge(sem("scattered"), j + done)
                    act.copy(g_cur, ps[5][:, 0:S]).then_inc(sem("g_cur_ready"), 1)
                    act.wait_ge(sem("down_full"), j + (done + 1))
                    act.copy(y_pair[:, 0:512], ps[6][:, :]).then_inc(sem("y_pair_act"), 1)

                tokens_taken(0)
                pair(0)
                with act.Fori(1, PAIRS - 1) as j:
                    pair(j)
                pair(PAIRS - 1, last=True)

            def overflow(layer):
                act.wait_ge(sem("late_ready"), layer + 1)
                some = act.value_load(late[0:1, layer, 0, 0:1], min_val=0, max_val=1)
                with act.If(some > 0):
                    act.wait_ge(sem("x_summed"), layer + 1)
                    late_experts(layer)

            def late_experts(layer):
                with act.Fori(0, LATE) as j:
                    there = act.value_load(late[0:1, layer, 0, bass.ds(j, 1)], min_val=0, max_val=1)
                    with act.If(there > 0):
                        act.wait_ge(sem(f"o_hid_full{layer}"), j + 1)
                        for b in range(2):
                            ins = act.activation(o_silu[:, 2 * b:2 * b + 2, :],
                                                 ps[b][:, :].rearrange("p (a b) -> p a b", b=S), ACT.Silu)
                        ins.then_inc(sem(f"o_silu_ready{layer}"), 1)

            act.wait_ge(sem("x_loaded"), 16)
            square(0)
            normalise(0, 0)
            for n in range(4):
                ada_part_copy()
            turned(0)

            take("ev0", 0, qT[:, 0:2, :], scale=0.125)
            ada_part_copy()
            take("ev1", 0, kT[:, 0:2, :])
            ada_part_copy()
            take("ev2", 0, v_tok[:, 0, :])
            softmax_exp("dilated")
            for h in range(8):
                if h < 7:
                    softmax_exp("dilated")
                if h == 0:
                    tokens("ev4", gv, ACT.Gelu_apprx_tanh)
                elif h == 1:
                    both("ev3", uT, ACT.Gelu_apprx_tanh)
                if h == 1:
                    root(small[:, MV + 4:MV + 6], "gv_var_ready", "gv_root_ready")
                if h == 5:
                    gate_rows("gateA")
                turned_probs(h, 384)
                ada_part_copy()
                head_out(h, h, 0)
                if h >= TWO_A:
                    ada_part_copy()
            act.wait_ge(sem("x_ready"), 1)
            square(1)
            normalise(1, 1)
            turned(1)
            gate_rows("gateB")
            experts(0)
            overflow(0)

            act.wait_ge(sem("x_ready"), 2)
            square(2)
            normalise(2, 2)
            turned(2)
            act.wait_ge(sem("rpb_sent"), 16)
            both("od0", aT)
            both("od1", glT, ACT.Tanh, 0.5)
            both("od2", qT, scale=0.125)
            both("od3", kT)
            tokens("od4", v_tok)
            softplus_parts()
            for h in range(8):
                stick_exp(8 + h)
                if h < 7:
                    softplus_parts()
                if h == 6:
                    act.wait_ge(sem("centred"), 1)
                    act.activation(csq[:, :, :], cacc[:, :, :], ACT.Square).then_inc(sem("csq_ready"), 1)
                ada_part_copy()
                if h == 6:
                    root(crs, "cvar_ready", "croot_ready")
                if h == 7:
                    gate_rows("gateC")
                head_out(8 + h, h, 4)
                if h >= TWO_B:
                    ada_part_copy()
            act.wait_ge(sem("conv_normed"), 1)
            for ct in range(4):
                ins = act.activation(oT[:, ct, :], cacc[:, ct, :], ACT.Silu,
                                     bias=cv[:, CV_LNB + ct:CV_LNB + ct + 1], scale=cv[:, CV_LNG + ct:CV_LNG + ct + 1])
            ins.then_inc(sem("o_c_ready"), 1)
            ada_part_copy()
            act.wait_ge(sem("x_ready"), 3)
            square(3)
            normalise(3, 3)
            turned(3)
            gate_rows("gateD")
            act.dma_start(fn_bc, a["final_norm_g"].partition_broadcast(P)).then_inc(sem("fn_loaded"), 16)
            experts(1)
            overflow(1)

            act.wait_ge(sem("x_ready"), 4)
            square(4)
            norm_root(4)
            act.wait_ge(sem("x_ready"), 5)
            square(5)
            normalise(5, 4)
            turned(4)
            for i, name in enumerate(("in0", "in1")):
                for b in range(2):
                    c = 4 * i + 2 * b
                    take(name, b, xa_raw[:, c:c + 2, 2:2 + S])
            both("in4", qT, scale=0.125)
            both("in6", kT)
            tokens("in8", v_tok)

            def half_tanh(name, dst, signal=None):
                for b in range(2):
                    if signal is None:
                        take(name, b, dst[:, 2 * b:2 * b + 2, :], ACT.Tanh, 0.5)
                        continue
                    src, _ = full_at(act, name, b)
                    act.activation(dst[:, 2 * b:2 * b + 2, :], src[:, :].rearrange("p (a b) -> p a b", b=S),
                                   ACT.Tanh, scale=0.5).then_inc(sem(signal), 1)

            def recurrence(ct, way):
                n = 2 * ct + way
                act.wait_ge(sem("rg_gates_full"), n + 1)
                if ct:
                    act.wait_ge(sem("rg_u_ready"), n - 1)
                t, t_i = rg_t[way], rg_ti[way]
                hr, hi = 16 + 16 * way + ct, 24 + 16 * way + ct
                step(act.activation(t, ps[4][:, 0:S], ACT.Tanh, scale=0.5, bias=rgc[:, hr:hr + 1]))
                act.activation(t_i, ps[4][:, S:2 * S], ACT.Tanh, scale=0.5, bias=rgc[:, hi:hi + 1])\
                   .then_inc(sem("rg_gates_taken"), 1)
                step.wait()
                c = 8 * way + ct
                step(act.activation(t, t, ACT.Tanh, scale=rgc[:, c:c + 1], bias=rgc[:, c:c + 1]))

            def recurrence_roots():
                step.wait()
                for way in range(2):
                    act.activation(rg_root[way], rg_t[way], ACT.Sqrt).then_inc(sem("rg_root_ready"), 1)

            def near(h, between):
                if h % 8 != 7:
                    softmax_exp("near")
                between(h)
                turned_probs(8 + 8 + h, 512)
                head_out(8 + 8 + h, h, 0)

            def between_c(h):
                recurrence(h, 0)
                if h in (0, 1):
                    half_tanh(f"in{2 + h}", yaT[:, 4 * h:4 * h + 4, :], "z_tanh")
                if h in (2, 3):
                    half_tanh(f"in{8 + h}", zbT[:, 4 * (h - 2):4 * (h - 2) + 4, :], "z_tanh")
                if h in (5, 6):
                    half_tanh(f"in{7 + h}", gaT[:, 4 * (h - 5):4 * (h - 5) + 4, :])

            act.wait_ge(sem("rgc_ready"), 1)
            softmax_exp("near")
            for h in range(8):
                near(h, between_c)
                recurrence(h, 1)
                recurrence_roots()
            both("in5", qT, scale=0.125)
            both("in7", kT)
            tokens("in9", v_tok)

            def between_d(h):
                if h == 8:
                    act.wait_ge(sem("ya_ready"), KT)
                    half_tanh("in14", gbT[:, 0:4, :])
                if h == 14:
                    half_tanh("in15", gbT[:, 4:8, :])

            softmax_exp("near")
            for h in range(8, 16):
                near(h, between_d)
            gate_rows("gateE", 0.5)
            act.dma_start(gf_bc, a["g_final_2"].partition_broadcast(P)).then_inc(sem("gf_loaded"), 16)
            act.wait_ge(sem("x_ready"), 6)
            square(6)
            norm_root(6)
            act.wait_ge(sem("rstd_ready"), 7)
            act.activation(x[:, 1, :], x[:, 1, :], ACT.Copy, scale=small[:, RSTD + 1:RSTD + 2])\
               .then_inc(sem("x_scaled_act"), 1)

        @block.vector
        def _(dve):
            step = Steps(dve, "dve_steps")

            def stt(out_, in0, scalar, in1, op0, op1):
                return dve.scalar_tensor_tensor(out_, in0, scalar, in1, op0, op1)

            def ttr(out_, in0, in1, op0, op1, start, acc):
                return dve.tensor_tensor_reduce(out_, in0, in1, 1.0, start, op0, op1, acc)

            def rstd(s):
                dve.wait_ge(sem("sumsq_ready"), s + 1)
                dve.tensor_scalar(small[:, RSTD:RSTD + 2], small[:, SUMSQ:SUMSQ + 2], 1.0 / D, EPS,
                                  ALU.mult, ALU.add).then_inc(sem("ms_ready"), 1)
                dve.wait_ge(sem("root_ready"), s + 1)
                dve.reciprocal(small[:, RSTD:RSTD + 2], small[:, RSTD:RSTD + 2]).then_inc(sem("rstd_ready"), 1)
                dve.wait_ge(sem("rstd_ready"), s + 1)

            def normalise(s):
                rstd(s)
                dve.tensor_scalar(xn[:, 0, :], x[:, 0, :], small[:, RSTD:RSTD + 1], None, ALU.mult)\
                   .then_inc(sem("xn_ready_dve"), 1)

            def gain(r):
                sc = (8, 32, 56, 80, 104)[r]
                g = (CV_N1, CV_N2, CV_N1 + 8, CV_N2 + 8, CV_GPRE)[r]
                dve.wait_ge(sem("ada_ready"), (4, 10, 16, 22, 28)[r])
                stt(gs[:, r, 0, :], mod[:, sc:sc + 8], 1.0, cv[:, g:g + 8], ALU.add, ALU.mult)\
                   .then_inc(sem("gain_ready"), 1)

            def turned(r):
                dve.wait_ge(sem("gain_ready"), r + 1)
                sh = (0, 24, 48, 72, 96)[r]
                for b in (1, 3):
                    dve.wait_ge(sem("turned"), 4 * r + b + 1)
                    for k in (2 * b, 2 * b + 1):
                        ins = dve.tensor_scalar(hT[:, k, :], ps[b][:, (k % 2) * S:(k % 2 + 1) * S],
                                                gs[:, r, 0, k:k + 1], mod[:, sh + k:sh + k + 1], ALU.mult, ALU.add)
                ins.then_inc(sem("hT_dve"), 1)

            cols = [0]

            def ada_cols():
                n = cols[0]
                cols[0] += 1
                dve.wait_ge(sem("ada_cols_full"), n + 1)
                stt(mod[:, 4 * n:4 * n + 4], ps[4][:, 0:4], 1.0 / 32, cv[:, 4 * n:4 * n + 4], ALU.mult, ALU.add)\
                   .then_inc(sem("ada_ready"), 1)

            def take(name, b, dst, scale=1.0):
                src, free = full_at(dve, name, b)
                v = src[:, :].rearrange("p (a b) -> p a b", b=dst.shape[2]) if len(dst.shape) == 3 else src[:, :]
                dve.tensor_scalar(dst, v, scale, None, ALU.mult).then_inc(free, 1)

            def diagonals(name):
                n = "ABCDE".index(name[-1])
                c0 = (16, 40, 64, 88, 112)[n]
                dve.wait_ge(sem("ada_ready"), (6, 12, 18, 24, 30)[n])
                for k in range(KT):
                    ins = dve.tensor_scalar(gate_bc[:, k * P:(k + 1) * P], ident, mod[:, c0 + k:c0 + k + 1], None,
                                            ALU.mult)
                ins.then_inc(sem("diag_ready"), 1)

            def gate_rows(name, scale=1.0):
                src, free = full_at(dve, name, 1)
                dve.tensor_scalar(gate_bc[:, 512:1024], src[:, :], scale, None, ALU.mult).then_inc(free, 1)

            def add_mixed(names, tmp):
                for half, name in enumerate(names):
                    cols_ = slice(half * 512, half * 512 + 512)
                    for b in range(TT):
                        src, free = full_at(dve, name, b)
                        dve.tensor_tensor(tmp[b], src[:, :], gate_bc[:, cols_], ALU.mult).then_inc(free, 1)
                    for b in range(TT):
                        n = dense[name]
                        dve.wait_ge(bank_free[2 * (n % 2) + b], n // 2 + 1)
                        ins = dve.tensor_tensor(x[:, b, cols_], x[:, b, cols_], tmp[b], ALU.add)
                        if half == 0:
                            step(ins)
                    if half == 0:
                        step.wait()
                ins.then_inc(sem("x_ready"), 1)

            head = [0]

            def softmaxes(n):
                return n if n < 8 else n - 8

            def score_max(kind):
                n = head[0]
                h = n if kind == "dilated" else n - 16
                dve.wait_ge(sem("scores_full"), n + 1)
                bank, p = ps[6 + n % 2], pr[:, n % 2, :]
                c = NEGMAX + 2 * (n % 2)
                if kind == "dilated":
                    both = ((slice(0, S), bias_a[:, h, :]), (slice(S, S + P), bias_a[:, h, P:S]))
                else:
                    nb = bias_n[:, (h // 2) % 2, h % 2, :]
                    both = ((slice(0, S), nb[:, 2 * GRID:2 * GRID + S]), (slice(S, 2 * S), nb[:, 0:S]))
                for m, (cut, bias) in enumerate(both):
                    step(ttr(p[:, cut], bank[:, cut], bias, ALU.add, ALU.max, -3e38, small[:, c + m:c + m + 1]))
                step.wait()
                dve.tensor_scalar(small[:, c:c + 2], small[:, c:c + 2], -1.0, None, ALU.mult)\
                   .then_inc(sem("max_ready"), 1)

            def score_probs(kind):
                n = head[0]
                head[0] += 1
                dve.wait_ge(sem("exp_ready"), softmaxes(n) + 1)
                p, d, r = pr[:, n % 2, :], DEN + 2 * (n % 2), RDEN + 2 * (n % 2)
                cuts = (slice(0, S), slice(S, S + P) if kind == "dilated" else slice(S, 2 * S))
                if kind == "dilated":
                    many = (k2[:, K2_MULT:K2_MULT + S], k2[:, K2_MULT + P:K2_MULT + S])
                    for m in range(2):
                        step(ttr(p[:, cuts[m]], p[:, cuts[m]], many[m], ALU.mult, ALU.add, 0.0,
                                 small[:, d + m:d + m + 1]))
                    step.wait()
                step(dve.reciprocal(small[:, r:r + 2], small[:, d:d + 2]))
                step.wait()
                for m in range(2):
                    ins = dve.tensor_scalar(p[:, cuts[m]], p[:, cuts[m]], small[:, r + m:r + m + 1], None, ALU.mult)
                ins.then_inc(sem("probs_ready"), 1)

            def diag_blocks(t):
                return bass.AP(t.tensor, t.offset, [list(t.ap[0]), [S, 2], [1, P]])

            def softplus():
                n = head[0]
                head[0] += 1
                b = n % 2
                dve.wait_ge(sem("log_ready"), n - 8 + 1)
                step(stt(sp_sb[:, b, :], z_sb[:, b, :], 0.0, e_sb[:, b, :], ALU.max, ALU.add))
                step.wait()
                v = diag_blocks(sp_sb[:, b, :])
                dve.tensor_tensor(v, v, bc(lt.unsqueeze(1), [P, 2, P]), ALU.mult).then_inc(sem("probs_ready"), 1)

            def stick_arg(n):
                b = n % 2
                dve.wait_ge(sem("probsT_full"), n + 1)
                step(dve.tensor_tensor(att_sb[:, b, :], z_sb[:, b, :], ps[5][:, 0:384], ALU.subtract))
                step.wait()
                v = diag_blocks(att_sb[:, b, :])
                dve.tensor_tensor(v, v, bc(neg_diag.unsqueeze(1), [P, 2, P]), ALU.add)\
                   .then_inc(sem("stick_arg_ready"), 1)

            def first_max(vals, width, at_, out_):
                m = rt[:, at_:at_ + 2]
                step(dve.tensor_reduce(m, vals, AX, ALU.max))
                step.wait()
                eq = rt[:, at_ + 2:at_ + 10].rearrange("p (t e) -> p t e", e=4)
                step(dve.tensor_tensor(eq, vals, bc(m.unsqueeze(2), [P, TT, 4]), ALU.is_equal))
                step.wait()
                step(dve.tensor_tensor(eq, eq, bc(kc[:, K_W:K_W + 4].unsqueeze(1), [P, TT, 4]), ALU.mult))
                step.wait()
                km = rt[:, at_ + 10:at_ + 12]
                step(dve.tensor_reduce(km, eq, AX, ALU.max))
                step.wait()
                step(dve.tensor_tensor(out_, eq, bc(km.unsqueeze(2), [P, TT, 4]), ALU.is_equal))
                step.wait()
                return m

            def late_list(layer):
                left, has, place = rt[:, 612:628], rt[:, 628:644], rt[:, 644:660]
                step(dve.tensor_reduce(left, ps[4][:, 0:32].rearrange("p (t e) -> p e t", e=EXPERTS), AX, ALU.add))
                step.wait()
                step(dve.tensor_scalar(has, left, 1.0, None, ALU.min))
                step.wait()
                step(dve.tensor_tensor_scan(place, ones[:, 0:EXPERTS], has, 0.0, ALU.mult, ALU.add))
                step.wait()
                step(dve.tensor_tensor(place, place, has, ALU.mult))
                step.wait()
                n = [P, EXPERTS, EXPERTS]
                at_place = rt[:, 660:660 + EXPERTS * EXPERTS].rearrange("p (j e) -> p j e", e=EXPERTS)
                count = kc[:, K_IOTA:K_IOTA + EXPERTS]
                step(dve.tensor_tensor(at_place, bc(place.unsqueeze(1), n), bc(count.unsqueeze(2), n), ALU.is_equal))
                step.wait()
                step(dve.tensor_reduce(has, at_place, AX, ALU.add))
                step.wait()
                step(stt(at_place, bc(count.unsqueeze(1), n), -1.0, at_place, ALU.add, ALU.mult))
                step.wait()
                step(dve.tensor_reduce(left, at_place, AX, ALU.add))
                step.wait()
                step(dve.tensor_copy(late[:, layer, 0, :], has))
                dve.tensor_copy(late[:, layer, 1, :], left).then_inc(sem("late_ready"), 1)

            def route(layer):
                lg = rt[:, 0:40].rearrange("p (t c) -> p t c", c=20)
                dve.wait_ge(sem("logits_full"), layer + 1)
                dve.wait_ge(sem("rw_loaded"), 16 * 7 * (layer + 1))
                ins = dve.tensor_tensor(lg, ps[4][:, 0:40].rearrange("p (t c) -> p t c", c=20),
                                        bc(rb[:, :].unsqueeze(1), [P, TT, 20]), ALU.add)
                ins.then_inc(sem("rb_used"), 1)
                dve.wait_ge(sem("rb_used"), layer + 1)
                t4 = [P, TT, 4]

                def tile4(at_):
                    return rt[:, at_:at_ + 8].rearrange("p (t e) -> p t e", e=4)

                group = tile4(100)
                gm = first_max(lg[:, :, 0:4], 4, 110, group)
                ex = tile4(40)
                dve.tensor_tensor(ex, lg[:, :, 0:4], bc(gm.unsqueeze(2), t4), ALU.subtract)\
                   .then_inc(sem("route_max_ready"), 1)
                by_group = rt[:, 130:162].rearrange("p (t e g) -> p t e g", e=4, g=4)
                for t in range(TT):
                    step(dve.tensor_tensor(by_group[:, t], lg[:, t, 4:20].rearrange("p (g e) -> p e g", e=4),
                                           bc(group[:, t, :].unsqueeze(1), [P, 4, 4]), ALU.mult))
                step.wait()
                own = tile4(170)
                step(dve.tensor_reduce(own, by_group, AX, ALU.add))
                step.wait()
                one, two, rest = tile4(180), tile4(190), tile4(200)
                m1 = first_max(own, 4, 210, one)
                step(stt(rest, one, NEG, own, ALU.mult, ALU.add))
                step.wait()
                m2 = first_max(rest, 4, 230, two)
                e2 = rt[:, 48:50]
                dve.tensor_tensor(e2, m2, m1, ALU.subtract).then_inc(sem("route_max_ready"), 1)
                dve.wait_ge(sem("route_exp_ready"), 2 * layer + 2)
                gw, w1, w2 = rt[:, 250:252], rt[:, 252:254], rt[:, 254:256]
                step(dve.tensor_reduce(gw, ex, AX, ALU.add))
                step(dve.tensor_scalar(w1, e2, 1.0, None, ALU.add))
                step.wait()
                step(dve.tensor_tensor(w1, w1, gw, ALU.mult))
                step.wait()
                step(dve.reciprocal(w1, w1))
                step.wait()
                step(dve.tensor_tensor(w2, w1, e2, ALU.mult))
                step.wait()
                g1, g2, both = tile4(260), tile4(270), tile4(280)
                step(dve.tensor_tensor(g1, one, bc(w1.unsqueeze(2), t4), ALU.mult))
                step(dve.tensor_tensor(g2, two, bc(w2.unsqueeze(2), t4), ALU.mult))
                step(dve.tensor_tensor(both, one, two, ALU.add))
                step.wait()
                step(dve.tensor_tensor(g1, g1, g2, ALU.add))
                step.wait()
                mask = rt[:, 512:544].rearrange("p (t e) -> p t e", e=EXPERTS)
                for t in range(TT):
                    for dst, src in ((gates, g1), (mask, both)):
                        step(dve.tensor_tensor(dst[:, t, :].rearrange("p (g e) -> p g e", e=4),
                                               bc(group[:, t, :].unsqueeze(2), [P, 4, 4]),
                                               bc(src[:, t, :].unsqueeze(1), [P, 4, 4]), ALU.mult))
                step.wait()
                dve.tensor_copy(rt[:, 610:611], rt[:, 512:513]).then_inc(sem("mask_ready"), 1)
                key, key_of = rt[:, 544:576], rt[:, 544:576].rearrange("p (t j a) -> p t j a", t=TT, a=2)
                mask_of = rt[:, 512:544].rearrange("p (t j a) -> p t j a", t=TT, a=2)
                other = rt[:, 620:636].rearrange("p (j c) -> p j c", c=2)
                slots = rt[:, 636:652].rearrange("p (j a) -> p j a", a=2)
                number, n_other = rt[:, 652:668], rt[:, 668:676]
                dve.wait_ge(sem("rank_full"), layer + 1)
                step(dve.tensor_copy(number, ps[5][:, 32:48]))
                step(stt(key, ps[5][:, 0:32], 1.0, rt[:, 512:544], ALU.add, ALU.mult))
                step.wait()
                number_of = number.rearrange("p (j a) -> p j a", a=2)
                for c in range(2):
                    step(dve.tensor_scalar(other[:, :, c], number_of[:, :, 0], float(CHUNK * (c + 1)), None, ALU.is_le))
                step.wait()
                step(dve.tensor_copy(split[:, layer, 0, :], other[:, :, 0]))
                step(dve.tensor_tensor(rt[:, 708:716], other[:, :, 1], other[:, :, 0], ALU.subtract))
                step(dve.tensor_scalar(rt[:, 716:724], other[:, :, 1], -1.0, 1.0, ALU.mult, ALU.add))
                step(dve.tensor_tensor(n_other, other[:, :, 0], other[:, :, 1], ALU.add))
                step.wait()
                step(dve.tensor_copy(split[:, layer, 1:3, :], rt[:, 708:724].rearrange("p (n j) -> p n j", j=PAIRS)))
                step.wait()
                step(dve.tensor_scalar(slots[:, :, 0], n_other, -float(CHUNK), 3.0 * CHUNK, ALU.mult, ALU.add))
                step(dve.tensor_scalar(slots[:, :, 1], n_other, float(CHUNK), float(CHUNK), ALU.mult, ALU.add))
                step.wait()
                over, within = rt[:, 576:608], rt[:, 676:708]
                slots_bc = bc(rt[:, 636:652].unsqueeze(1), [P, TT, EXPERTS])

                def by_tile(v):
                    return v.rearrange("p (t e) -> p t e", e=EXPERTS)

                step(dve.tensor_tensor(by_tile(within), by_tile(key), slots_bc, ALU.is_le))
                dve.tensor_tensor(by_tile(over), by_tile(key), slots_bc, ALU.is_gt).then_inc(sem("over_ready"), 1)
                dve.wait_ge(sem("over_ready"), layer + 1)
                step(dve.tensor_tensor(gates_over[:, :, :], by_tile(over), gates[:, :, :], ALU.mult))
                for t in range(TT):
                    step(stt(key_of[:, t, :, 1], mask_of[:, t, :, 1], float(P + 1), key_of[:, t, :, 1],
                             ALU.mult, ALU.subtract))
                step.wait()
                step(dve.tensor_tensor(key, key, within, ALU.mult))
                step.wait()
            def experts(layer):
                done, first = PAIRS * layer, moe_start[layer]
                sh = (24, 72)[layer]
                dve.memset(hidT[:, 0:2, :], 0.0).then_inc(sem("zeros_ready"), 1)
                route(layer)
                key = rt[:, 544:576].rearrange("p (t e) -> p t e", e=EXPERTS)
                wide = [P, TT, 2, P]

                def of_pair(v, j):
                    cols_ = slice(2 * j, 2 * j + 2) if isinstance(j, int) else bass.ds(2 * j, 2)
                    return bc(v[:, :, cols_].unsqueeze(3), wide)

                def picks(j):
                    step_(dve.tensor_tensor(is_slot[:, :, :, :], of_pair(key, j),
                                            bc(kc[:, K_IOTA:K_IOTA + P].unsqueeze(1).unsqueeze(1), wide),
                                            ALU.is_equal), j, 1)
                    dve.tensor_tensor(pick[:, :, :], is_slot[:, :, 0, :], is_slot[:, :, 1, :], ALU.add)\
                       .then_inc(sem("pick_ready"), 1)

                def weighted_picks(j):
                    dve.wait_ge(sem("pick_ready"), j + (done + 1))
                    step_(dve.tensor_tensor(is_slot[:, :, :, :], is_slot[:, :, :, :], of_pair(gates, j), ALU.mult),
                          j, 2)
                    dve.tensor_tensor(pick_g[:, :, :], is_slot[:, :, 0, :], is_slot[:, :, 1, :], ALU.add)\
                       .then_inc(sem("pick_g_ready"), 1)

                def step_(ins, j, n):
                    ins.then_inc(sem("pick_steps"), 1)
                    dve.wait_ge(sem("pick_steps"), 2 * j + (2 * done + n))

                def tokens_taken(j):
                    dve.wait_ge(sem("gather_full"), 2 * j + (2 * done + 2))
                    for k in range(4, 8):
                        ins = dve.tensor_scalar(x_cur[:, k, :], ps[7][:, (k - 4) * P:(k - 3) * P],
                                                gs[:, 2 * layer + 1, 0, k:k + 1], mod[:, sh + k:sh + k + 1],
                                                ALU.mult, ALU.add)
                    ins.then_inc(sem("x_cur_dve"), 1)

                def pair(j, last=False):
                    if not last:
                        dve.wait_ge(sem("gather_full"), 2 * j + (2 * done + 2))
                        dve.wait_ge(sem("pick_g_ready"), j + (done + 1))
                        picks(j + 1)
                    dve.wait_ge(unit_done, j * 6 + (first + 4))
                    dve.wait_ge(sem("silu_ready"), j + (done + 1))
                    dve.tensor_tensor(hid, silu_g, ps[5][:, :], ALU.mult).then_inc(sem("hid_ready"), 1)
                    if not last:
                        tokens_taken(j + 1)
                        dve.wait_ge(sem("gT_full"), j + (done + 1))
                        weighted_picks(j + 1)
                    dve.wait_ge(unit_done, j * 6 + (first + 6))
                    dve.tensor_copy(y_pair[:, 512:1024], ps[7][:, :]).then_inc(sem("y_pair_dve"), 1)

                picks(0)
                weighted_picks(0)
                dve.wait_ge(sem("over_full"), layer + 1)
                late_list(layer)
                tokens_taken(0)
                pair(0)
                with dve.Fori(1, PAIRS - 1) as j:
                    pair(j)
                pair(PAIRS - 1, last=True)
                some = dve.value_load(late[0:1, layer, 0, 0:1], min_val=0, max_val=1)
                dve.wait_ge(sem("scattered"), PAIRS * (layer + 1))
                for half in range(2):
                    tmp = (silu_g, hid)
                    for t in range(TT):
                        step(dve.tensor_tensor(tmp[t], ps[2 * t + half][:, :], gate_bc[:, half * 512:half * 512 + 512],
                                               ALU.mult))
                    step.wait()
                    for t in range(TT):
                        xv = x[:, t, half * 512:half * 512 + 512]
                        ins = dve.tensor_tensor(xv, xv, tmp[t], ALU.add)
                        if half == 0 or t == 0:
                            step(ins)
                    if half == 0:
                        step.wait()
                ins.then_inc(sem("x_summed"), 1)
                return some

            def overflow(layer, some):
                dve.wait_ge(sem("x_summed"), layer + 1)
                with dve.If(some > 0):
                    late_experts(layer)
                dve.tensor_copy(small[:, 52:53], small[:, RSTD:RSTD + 1]).then_inc(sem("x_ready"), 1)

            def late_experts(layer):
                with dve.Fori(0, LATE) as j:
                    there = dve.value_load(late[0:1, layer, 0, bass.ds(j, 1)], min_val=0, max_val=1)
                    with dve.If(there > 0):
                        dve.wait_ge(sem(f"o_silu_ready{layer}"), j + 1)
                        for b in range(2):
                            ins = dve.tensor_tensor(o_hidT[:, 2 * b:2 * b + 2, :], o_silu[:, 2 * b:2 * b + 2, :],
                                                    ps[2 + b][:, :].rearrange("p (a b) -> p a b", b=S), ALU.mult)
                        ins.then_inc(sem(f"o_hid_ready{layer}"), 1)
                        expert = dve.value_load(late[0:1, layer, 1, bass.ds(j, 1)], min_val=0, max_val=EXPERTS - 1)
                        for t in range(TT):
                            dve.tensor_copy(small[:, 50 + t:51 + t], gates_over[:, t, bass.ds(expert, 1)])\
                               .then_inc(sem(f"o_steps{layer}"), 1)
                        dve.wait_ge(sem(f"o_steps{layer}"), j * 10 + TT)
                        dve.wait_ge(sem(f"o_y_full{layer}"), j + 1)
                        n = TT
                        for t in range(TT):
                            for half in range(2):
                                cut = slice(half * 512, half * 512 + 512)
                                stt(ada_part[:, :], ps[4 + 2 * t + half][:, :], small[:, 50 + t:51 + t],
                                    gate_bc[:, cut], ALU.mult, ALU.mult).then_inc(sem(f"o_steps{layer}"), 1)
                                dve.wait_ge(sem(f"o_steps{layer}"), j * 10 + (n + 1))
                                ins = dve.tensor_tensor(x[:, t, cut], x[:, t, cut], ada_part[:, :], ALU.add)
                                n += 2
                                if n < 8 + TT:
                                    ins.then_inc(sem(f"o_steps{layer}"), 1)
                                    dve.wait_ge(sem(f"o_steps{layer}"), j * 10 + n)
                        ins.then_inc(sem(f"o_y_taken{layer}"), 1)
                        dve.wait_ge(sem(f"o_y_taken{layer}"), j + 1)
                        dve.memset(small[:, 60:61], 0.0).then_inc(sem(f"o_steps{layer}"), 1)

            dve.memset(rel_ext[0:32, :], 0.0)
            dve.memset(rel_ext[32:64, :], 1.0).then_inc(sem("rel_ones"), 1)
            dve.wait_ge(sem("x_loaded"), 16)
            normalise(0)
            dve.wait_ge(sem("cv_ready"), 1)
            for n in range(4):
                ada_cols()
            gain(0)
            turned(0)
            dve.wait_ge(sem("ws_full"), 1)
            dve.wait_ge(sem("k2_loaded"), 16)
            dve.tensor_tensor(wsT[:, :, :], ps[6][:, :].rearrange("p (a b) -> p a b", b=P),
                              bc(k2[:, K2_LE:K2_LE + P].unsqueeze(1), [P, 4, P]), ALU.mult)\
               .then_inc(sem("wsT_ready"), 1)

            e, s_, s2 = rgt[:, 0:16], rgt[:, 16:32], rgt[:, 32:48]
            two_sp = rgc[:, 0:16]
            dve.wait_ge(sem("lam_exp_ready"), 1)
            step(dve.tensor_scalar(s_, e, 2.0, None, ALU.add))
            step.wait()
            step(dve.reciprocal(s_, s_))
            step.wait()
            step(dve.tensor_tensor(s_, s_, e, ALU.mult))
            step.wait()
            step(dve.tensor_tensor(s2, s_, s_, ALU.mult))
            step.wait()
            step(dve.tensor_scalar(two_sp, s2, 1.0 / 17, 1.0 / 15, ALU.mult, ALU.add))
            for k in range(13, 0, -2):
                step.wait()
                step(dve.tensor_tensor(two_sp, two_sp, s2, ALU.mult))
                step.wait()
                step(dve.tensor_scalar(two_sp, two_sp, 1.0 / k, None, ALU.add))
            step.wait()
            step(stt(two_sp, two_sp, 4.0, s_, ALU.mult, ALU.mult))
            step(dve.tensor_scalar(e, cv[:, CV_LF:CV_LF + 16], -2.0, 0.0, ALU.mult, ALU.max))
            step.wait()
            step(dve.tensor_tensor(two_sp, two_sp, e, ALU.add))
            dve.tensor_scalar(rgc[:, 16:48], cv[:, CV_RF:CV_RF + 32], 0.5, None, ALU.mult)\
               .then_inc(sem("rgc_ready"), 1)

            take("ev0", 1, qT[:, 2:4, :], 0.125)
            ada_cols()
            take("ev1", 1, kT[:, 2:4, :])
            ada_cols()
            take("ev2", 1, v_tok[:, 1, :])
            dve.wait_ge(sem("bias_a_loaded"), 16)
            score_max("dilated")
            score_probs("dilated")
            for h in range(8):
                if h < 7:
                    score_max("dilated")
                if h > TWO_A:
                    ada_cols()
                if h < 7:
                    score_probs("dilated")
                if h == 1:
                    dve.wait_ge(sem("gmlp_loaded"), 48)
                    taken(dve, "ev4")
                    mv = small[:, MV:MV + 4]
                    for t in range(TT):
                        step(dve.bn_stats(small[:, BN + 6 * t:BN + 6 * t + 6], gv[:, t, :]))
                    step.wait()
                    for t in range(TT):
                        step(dve.bn_aggr(mv[:, 2 * t:2 * t + 2], small[:, BN + 6 * t:BN + 6 * t + 6]))
                    step.wait()
                    rs = small[:, MV + 4:MV + 6]
                    dve.tensor_scalar(rs, mv.rearrange("p (t c) -> p t c", c=2)[:, :, 1], EPS, None, ALU.add)\
                       .then_inc(sem("gv_var_ready"), 1)
                    dve.wait_ge(sem("gv_root_ready"), 1)
                    step(dve.reciprocal(rs, rs))
                    step.wait()
                    for t in range(TT):
                        step(dve.tensor_scalar(gv[:, t, :], gv[:, t, :], mv[:, 2 * t:2 * t + 1], rs[:, t:t + 1],
                                               ALU.subtract, ALU.mult))
                    step.wait()
                    step(dve.tensor_tensor(gv[:, :, :], gv[:, :, :], bc(lng_bc.unsqueeze(1), [P, TT, HW]), ALU.mult))
                    step.wait()
                    dve.tensor_tensor(gv[:, :, :], gv[:, :, :], bc(lnb_bc.unsqueeze(1), [P, TT, HW]), ALU.add)\
                       .then_inc(sem("gv_ready"), 1)
                if h == 3:
                    taken(dve, "ev3")
                    for b in range(2):
                        src, free = full_at(dve, "mixA", b)
                        o = oT[:, 4 + 2 * b:6 + 2 * b, :]
                        for g in range(2):
                            ins = dve.tensor_tensor(o[:, g, :].rearrange("p (t c) -> p t c", c=P),
                                                    src[:, g * S:(g + 1) * S].rearrange("p (t c) -> p t c", c=P),
                                                    bc(bs_bc[:, 2 * b + g, :].unsqueeze(1), [P, TT, P]), ALU.add)
                            if g == 0:
                                step(ins)
                        ins.then_inc(free, 1)
                        step.wait()
                        n = dense["mixA"]
                        dve.wait_ge(bank_free[2 * (n % 2) + b], n // 2 + 1)
                        ins = dve.tensor_tensor(o, o, uT[:, 2 * b:2 * b + 2, :], ALU.mult)
                        if b == 0:
                            step(ins)
                    ins.then_inc(sem("o_b_ready"), 1)
                    diagonals("gateA")
                if h == 5:
                    gate_rows("gateA")
                ada_cols()
            ada_cols()
            taken(dve, "gateA")
            add_mixed(("evo0", "evo1"), (pr[:, 0, :], pr[:, 1, :]))
            gain(1)
            normalise(1)
            diagonals("gateB")
            turned(1)
            gate_rows("gateB")
            taken(dve, "gateB")
            overflow(0, experts(0))
            dve.wait_ge(sem("rpb_sent"), 16)

            normalise(2)
            gain(2)
            turned(2)
            dve.memset(hcT[:, :, 0:PAD], 0.0)
            step(dve.tensor_scalar(cv[:, CV_DW:CV_DW + 124], cv[:, CV_DW:CV_DW + 124], 0.5, None, ALU.mult))
            taken(dve, "od0")
            taken(dve, "od1")
            step(stt(hcT[:, :, PAD:PAD + S], glT[:, :, :], 1.0, aT[:, :, :], ALU.add, ALU.mult))
            step.wait()
            def taps(two, lo, hi):
                for j in range(lo, hi):
                    for ct in (two, two + 1):
                        w = cv[:, CV_DW + CONV * ct + j:CV_DW + CONV * ct + j + 1]
                        if j == 0:
                            ins = dve.tensor_scalar(cacc[:, ct, :], hcT[:, ct, 0:S], w,
                                                    cv[:, CV_BDW + ct:CV_BDW + ct + 1], ALU.mult, ALU.add)
                        else:
                            dve.wait_ge(step.sem, step.n - (1 if j > lo else 0))
                            ins = stt(cacc[:, ct, :], hcT[:, ct, j:j + S], w, cacc[:, ct, :], ALU.mult, ALU.add)
                        step(ins)
            taps(0, 0, CONV)
            softplus()
            for h in range(8):
                stick_arg(8 + h)
                if h > TWO_B:
                    ada_cols()
                if h < 7:
                    softplus()
                if h < 5:
                    taps(2, 7 * h, min(7 * h + 7, CONV))
                if h == 4:
                    step.wait()
                    dve.tensor_copy(small[:, 53:54], small[:, 52:53]).then_inc(sem("conv_ready"), 1)
                if h == 5:
                    dve.wait_ge(sem("mean_full"), 1)
                    stt(cacc[:, :, :], bc(ps[2][:, 0:S].unsqueeze(1), [P, 4, S]), -1.0 / HW, cacc[:, :, :],
                        ALU.mult, ALU.add).then_inc(sem("centred"), 1)
                if h == 6:
                    dve.wait_ge(sem("var_full"), 1)
                    dve.tensor_scalar(crs, ps[2][:, S:2 * S], 1.0 / HW, EPS, ALU.mult, ALU.add)\
                       .then_inc(sem("cvar_ready"), 1)
                    dve.wait_ge(sem("croot_ready"), 1)
                    dve.reciprocal(crs, crs).then_inc(sem("crs_ready"), 1)
                    dve.wait_ge(sem("crs_ready"), 1)
                    dve.tensor_tensor(cacc[:, :, :], cacc[:, :, :], bc(crs.unsqueeze(1), [P, 4, S]), ALU.mult)\
                       .then_inc(sem("conv_normed"), 1)
                if h == 5:
                    diagonals("gateC")
                if h == 7:
                    gate_rows("gateC")
                ada_cols()
            ada_cols()
            ada_cols()
            taken(dve, "gateC")
            add_mixed(("odo0", "odo1"), (pr[:, 0, :], pr[:, 1, :]))
            gain(3)
            normalise(3)
            diagonals("gateD")
            turned(3)
            gate_rows("gateD")
            taken(dve, "gateD")
            overflow(1, experts(1))

            rstd(4)
            dve.wait_ge(sem("fn_loaded"), 16)
            for t in range(TT):
                ins = stt(x[:, t, :], x[:, t, :], small[:, RSTD + t:RSTD + t + 1], fn_bc, ALU.mult, ALU.mult)
                if t == 0:
                    step(ins)
            ins.then_inc(sem("x_ready"), 1)
            normalise(5)
            gain(4)
            turned(4)
            dve.memset(xa_raw[:, :, 0:2], 0.0)
            step(dve.memset(xa_raw[:, :, 2 + S:3 + S], 0.0))
            taken(dve, "in0")
            taken(dve, "in1")
            step.wait()
            for j in range(4):
                for ct in range(KT):
                    w = cv[:, CV_CW2 + 8 * j + ct:CV_CW2 + 8 * j + ct + 1]
                    if j == 0:
                        ins = dve.tensor_scalar(xc[:, ct, :], xa_raw[:, ct, 0:S], w,
                                                cv[:, CV_CB2 + ct:CV_CB2 + ct + 1], ALU.mult, ALU.add)
                    else:
                        if ct == 0:
                            step.wait()
                        ins = stt(xc[:, ct, :], xa_raw[:, ct, j:j + S], w, xc[:, ct, :], ALU.mult, ALU.add)
                    if j < 3 or ct < KT - 1:
                        step(ins)
            ins.then_inc(sem("xc_ready"), 1)

            def silu(name, b, dst, n):
                src, free = full_at(dve, name, b)
                dve.wait_ge(sem("z_tanh"), n + 1)
                stt(dst, dst, 1.0, src[:, :].rearrange("p (a b) -> p a b", b=S), ALU.add, ALU.mult).then_inc(free, 1)

            def recurrence(ct, way):
                n = 2 * ct + way
                t, t_i, root, u, h_f, h_b, inv, dec = (rg_t[way], rg_ti[way], rg_root[way], rg_u, rg_hf, rg_hb,
                                                       rg_inv, rg_dec)
                dve.wait_ge(sem("rg_root_ready"), n + 1)
                step(dve.tensor_scalar(inv, t, 1.0, None, ALU.add))
                step.wait()
                step(dve.reciprocal(inv, inv))
                step(stt(t_i, t_i, 1.0, xc[:, ct, :], ALU.add, ALU.mult))
                step.wait()
                step(dve.tensor_scalar(dec, inv, 2.0, -1.0, ALU.mult, ALU.add))
                step(dve.tensor_tensor(root, root, inv, ALU.mult))
                step.wait()
                dve.tensor_tensor(u, root, t_i, ALU.mult).then_inc(sem("rg_u_ready"), 1)
                dve.wait_ge(sem("rg_u_ready"), n + 1)

                def way_of(v):
                    if way == 0:
                        return v
                    return bass.AP(v.tensor, v.offset + S - 1, [list(v.ap[0]), [-1, S]])

                step(dve.tensor_tensor_scan(way_of(h_b if way else h_f), way_of(dec), way_of(u), 0.0,
                                            ALU.mult, ALU.add))
                step.wait()
                if way:
                    taken(dve, "in2" if ct < 4 else "in3")
                    step(dve.tensor_tensor(h_f, h_f, h_b, ALU.add))
                    step.wait()
                    stt(yaT[:, ct, :], h_f, 0.5, yaT[:, ct, :], ALU.mult, ALU.mult).then_inc(sem("ya_ready"), 1)

            def next_bias(h):
                b = (h // 2) % 2
                dve.wait_ge(sem(f"bias_n_loaded{b}"), 64 * (h // 4 + 1))
                v = bias_n[:, b, :, :].rearrange("p h (i c) -> p (h i) c", c=GRID)
                step(dve.tensor_tensor(v, v, bc(kc[:, K_NAM:K_NAM + GRID].unsqueeze(1), [P, 12, GRID]), ALU.add))
                step.wait()

            def near(h):
                if h % 8 != 7:
                    if (h + 1) % 2 == 0:
                        next_bias(h + 1)
                    score_max("near")
                    score_probs("near")

            next_bias(0)
            score_max("near")
            score_probs("near")
            for h in range(8):
                if h >= 1:
                    recurrence(h - 1, 0)
                near(h)
                if h in (0, 1):
                    for b in range(2):
                        silu(f"in{2 + h}", b, yaT[:, 4 * h + 2 * b:4 * h + 2 * b + 2, :], 2 * h + b)
                if h in (2, 3):
                    i = h - 2
                    for b in range(2):
                        silu(f"in{10 + i}", b, zbT[:, 4 * i + 2 * b:4 * i + 2 * b + 2, :], 4 + 2 * i + b)
                if h >= 1:
                    recurrence(h - 1, 1)
            recurrence(7, 0)
            recurrence(7, 1)
            next_bias(8)
            score_max("near")
            score_probs("near")

            def gated(name, i, g, last):
                for b in range(2):
                    src, free = full_at(dve, name, b)
                    v = src[:, :].rearrange("p (a b) -> p a b", b=S)
                    gv_ = g[:, 4 * i + 2 * b:4 * i + 2 * b + 2, :]
                    stt(gv_, gv_, 1.0, v, ALU.add, ALU.mult).then_inc(free, 1)
                    if last:
                        n = dense[name]
                        dve.wait_ge(bank_free[2 * (n % 2) + b], n // 2 + 1)
                        m = gaT[:, 4 * i + 2 * b:4 * i + 2 * b + 2, :]
                        ins = dve.tensor_tensor(m, m, gv_, ALU.add)
                        if i == 1 and b == 1:
                            ins.then_inc(sem("merged_ready"), 1)
                        else:
                            step(ins)

            for h in range(8, 16):
                near(h)
                if h in (10, 12):
                    i = (h - 10) // 2
                    taken(dve, f"in{12 + i}")
                    gated(f"pa{i}", i, gaT, False)
            dve.wait_ge(sem("o_taken"), 32)
            for i in range(2):
                taken(dve, f"in{10 + i}")
            stt(oT[:, :, :], oT[:, :, :], 0.5, zbT[:, :, :], ALU.mult, ALU.mult).then_inc(sem("yb_ready"), 1)
            diagonals("gateE")
            taken(dve, "pa1")
            for i in range(2):
                taken(dve, f"in{14 + i}")
                gated(f"pb{i}", i, gbT, True)
            gate_rows("gateE", 0.5)
            taken(dve, "gateE")
            add_mixed(("wo0", "wo1"), (pr[:, 0, :], pr[:, 1, :]))
            rstd(6)
            dve.wait_ge(sem("gf_loaded"), 16)
            stt(x[:, 0, :], x[:, 0, :], small[:, RSTD:RSTD + 1], gf_bc, ALU.mult, ALU.mult)\
                .then_inc(sem("out_ready"), 1)
            dve.wait_ge(sem("x_scaled_act"), 1)
            dve.tensor_tensor(x[:, 1, :], x[:, 1, :], gf_bc, ALU.mult).then_inc(sem("out_ready"), 1)

        @block.gpsimd
        def _(pool):
            def load_router(layer):
                with nc.allow_non_contiguous_dma(reason="rows of four logits"):
                    srcs = [a["moe_w_group"][layer]] + [a["moe_w_router"][layer, g] for g in range(4)]
                    for n, src in enumerate(srcs):
                        pool.dma_start(rw[:, :, 4 * n:4 * n + 4], src.rearrange("(k p) g -> p k g", p=P))\
                           .then_inc(sem("rw_loaded"), 16)
                pool.dma_start(rb[:, 0:4], a["moe_b_group"][layer].partition_broadcast(P))\
                   .then_inc(sem("rw_loaded"), 16)
                pool.dma_start(rb[:, 4:20], a["moe_b_router"][layer].rearrange("g e -> (g e)").partition_broadcast(P))\
                   .then_inc(sem("rw_loaded"), 16)

            pool.wait_ge(sem("bias_rows_ready"), 1)
            pool.dma_start(bias_dram, bc(bias_rows[0:8, :].unsqueeze(1), [8, P, 384]))\
               .then_inc(sem("bias_rows_sent"), 16)
            pool.wait_ge(sem("bias_rows_sent"), 16)
            pool.dma_start(bias_a[:, :, :], bass.AP(bias_dram.tensor, P - 1, [[383, P], [384 * P, 8], [1, S]]))\
               .then_inc(sem("bias_a_loaded"), 16)
            pool.dma_start(k2[:, :], a["k_early"]).then_inc(sem("k2_loaded"), 16)
            for dst, src in ((lng_bc, a["ev_gmlp_ln_g"]), (lnb_bc, a["ev_gmlp_ln_b"])):
                pool.dma_start(dst, src.partition_broadcast(P).rearrange("p l c -> p (l c)"))\
                   .then_inc(sem("gmlp_loaded"), 16)
            pool.dma_start(bs_bc[:, :, :], a["ev_b_s"][0].partition_broadcast(P)).then_inc(sem("gmlp_loaded"), 16)

            load_router(0)

            def overflow(layer):
                pool.wait_ge(sem("x_summed"), layer + 1)
                some = pool.value_load(late[0:1, layer, 0, 0:1], min_val=0, max_val=1)
                with pool.If(some > 0):
                    late_experts(layer)

            def late_experts(layer):

                def load(j):
                    which = late[0:1, layer, 1, bass.ds(j, 1)] if not isinstance(j, int) else late[0:1, layer, 1, 0:1]
                    expert = pool.value_load(which, min_val=0, max_val=EXPERTS - 1)
                    for m, w in enumerate((a["moe_w_gate"], a["moe_w_up"], a["moe_w_down"])):
                        src = w[layer][bass.ds(expert, 1)].rearrange("e (k p) c -> p (e k) c", p=P)
                        pool.dma_start(o_w[m].rearrange("p (k c) -> p k c", c=src.shape[2]), src)\
                            .then_inc(sem(f"o_loaded{layer}{m}"), 16)

                there = pool.value_load(late[0:1, layer, 0, 0:1], min_val=0, max_val=1)
                with pool.If(there > 0):
                    load(0)
                with pool.Fori(1, LATE) as j:
                    there = pool.value_load(late[0:1, layer, 0, bass.ds(j, 1)], min_val=0, max_val=1)
                    with pool.If(there > 0):
                        pool.wait_ge(sem(f"o_y_taken{layer}"), j)
                        load(j)

            def load_bias(pair):
                with nc.allow_non_contiguous_dma(reason="one row per query"):
                    for half, h in ((0, 0), (0, 1), (1, 0), (1, 1)):
                        src = bass.AP(rpb_dram.tensor, (2 * pair + h) * GRID * 7 * P + (1 - half) * P + GRID - 1,
                                      [[7 * P - 1, GRID], [P, 6], [1, GRID]])
                        dst = bias_n[64 * half:64 * half + 64, pair % 2, h, :].rearrange("p (i c) -> p i c", c=GRID)
                        pool.dma_start(dst, src).then_inc(sem(f"bias_n_loaded{pair % 2}"), 16)

            def load_gates(ct):
                for s_, name in enumerate(("w_r_f_2", "w_i_f_2", "w_r_b_2", "w_i_b_2")):
                    for half in range(2):
                        cut = slice(64 * half, 64 * half + 64)
                        pool.dma_start(rg_w[cut, ct % 2, s_, cut], a[name][0, 2 * ct + half])\
                            .then_inc(sem(f"rg_w_loaded{ct % 2}"), 16)

            pool.wait_ge(sem("x_ready"), 1)
            pool.memset(rpb_pad[0:16, :, :], 0.0).then_inc(sem("rpb_zero"), 1)
            pool.wait_ge(sem("rpb_zero"), 1)
            with nc.allow_non_contiguous_dma(reason="short rows"):
                pool.dma_start(rpb_pad[0:16, :, 48:79], a["rpb_2"][0, :, 4:11, :]).then_inc(sem("rpb_loaded"), 16)
            pool.wait_ge(sem("rpb_loaded"), 16)
            rows = rpb_pad[0:16, :, :].rearrange("h i c -> h (i c)").unsqueeze(1)
            pool.dma_start(rpb_dram.rearrange("h q i c -> h q (i c)"), bc(rows, [16, GRID, 7 * P]))\
                .then_inc(sem("rpb_sent"), 16)
            pool.wait_ge(sem("rpb_sent"), 16)
            pool.wait_ge(sem("rb_used"), 1)
            load_router(1)
            overflow(0)
            pool.memset(rg_w[:, :, :, :], 0.0).then_inc(sem("rg_w_zero"), 1)
            pool.wait_ge(sem("rg_w_zero"), 1)
            for n in range(2):
                load_bias(n)
                load_gates(n)
            overflow(1)
            for h in range(12):
                if h % 2 == 0:
                    pool.wait_ge(sem("max_ready"), 8 + h + 2)
                    load_bias(h // 2 + 2)
                if h < KT - 2:
                    pool.wait_ge(sem("rg_gates_full"), 2 * h + 2)
                    load_gates(h + 2)


_INS = ["x", "c", "rel_bias", "norm1_g", "norm2_g", "w_ada", "b_ada", "ev_w_in", "ev_w_out", "ev_gmlp_ln_g",
        "ev_gmlp_ln_b", "ev_w_s", "ev_b_s", "od_w_in", "od_w_out", "od_w_dw", "od_b_dw", "od_conv_ln_g",
        "od_conv_ln_b", "moe_w_group", "moe_b_group", "moe_w_router", "moe_b_router", "moe_w_gate", "moe_w_up",
        "moe_w_down", "final_norm_g", "c_2", "g_pre_2", "w_c_2", "b_c_2", "w_in_2", "conv_w_2", "conv_b_2",
        "w_r_f_2", "b_r_f_2", "w_i_f_2", "b_i_f_2", "lam_f_2", "w_r_b_2", "b_r_b_2", "w_i_b_2", "b_i_b_2",
        "lam_b_2", "rpb_2", "w_pa_2", "w_pb_2", "w_o_2", "g_final_2"]


def kernel(**inputs):
    import concourse.bacc as bacc
    from concourse.bass_utils import run_bass_kernel_spmd

    nc = bacc.Bacc("TRN2", target_bir_lowering=False, num_devices=1)
    main, early, onehot = tables()
    arrays = {name: np.ascontiguousarray(inputs[name]) for name in _INS}
    arrays |= {"k_main": main, "k_early": early, "k_onehot": onehot}
    sent, aps = {}, {}
    for name, v in arrays.items():
        sent[f"in_{name}"] = v
        aps[name] = nc.dram_tensor(f"in_{name}", v.shape, mybir.dt.from_np(v.dtype), kind="ExternalInput").ap()
    out = nc.dram_tensor("out_0", (1, S, D), F32, kind="ExternalOutput").ap()
    program(nc, aps, out)
    r = run_bass_kernel_spmd(nc, [sent], core_ids=[0])
    return r.results[0]["out_0"]
```
